# Optimizing a Trainium2 kernel written in Bass

```python
import jax, jax.numpy as jnp
from jax import lax
import numpy as np

D_MODEL = 1024
BATCH = 1
SEQ = 512
DEPTH = 2

ATTN_HEAD_DIM = 64
ATTN_HEADS = D_MODEL // 128
ATTN_KV_HEADS = ATTN_HEADS // 4
ROPE_DIM = ATTN_HEAD_DIM // 4
ROPE_THETA = 500000.0
WINDOW = 128
ATTN_BLOCK = 128
MLSTM_HEAD_DIM = 128
MLSTM_HEADS = D_MODEL // 256
MLSTM_CHUNK = 64
CONV_WIDTH = 4
N_EXPERTS = 16
N_GROUPS = 4
EXPERTS_PER_GROUP = N_EXPERTS // N_GROUPS
TOP_K = 2
D_FF_EXPERT = D_MODEL // 2
MOE_BLOCK = 256
EPS = 1e-6

ATTN_Q_W = ATTN_HEADS * ATTN_HEAD_DIM
ATTN_KV_W = ATTN_KV_HEADS * ATTN_HEAD_DIM
MLSTM_W = MLSTM_HEADS * MLSTM_HEAD_DIM
IN_WIDTHS = (ATTN_Q_W, ATTN_KV_W, ATTN_KV_W, 2 * MLSTM_W, MLSTM_W, MLSTM_HEADS, MLSTM_HEADS, MLSTM_W, D_MODEL, D_MODEL)
D_IN = ATTN_Q_W + 2 * ATTN_KV_W + 4 * MLSTM_W + 2 * MLSTM_HEADS + 2 * D_MODEL

kernel_name = "hybrid_swa_mlstm_grouped_moe_trunk"

def rms_norm(x, w):
    xf = x.astype(jnp.float32)
    y = xf * lax.rsqrt(jnp.mean(xf * xf, axis=-1, keepdims=True) + EPS)
    return (y * w.astype(jnp.float32)).astype(x.dtype)

def split_cols(p):
    outs = []
    start = 0
    for w in IN_WIDTHS:
        outs.append(p[..., start:start + w])
        start += w
    return outs

def partial_rope(t, cos, sin):
    half = ROPE_DIM // 2
    tf = t.astype(jnp.float32)
    t1 = tf[..., :half]
    t2 = tf[..., half:ROPE_DIM]
    out = jnp.concatenate([t1 * cos - t2 * sin, t2 * cos + t1 * sin, tf[..., ROPE_DIM:]], axis=-1)
    return out.astype(t.dtype)

def sliding_window_attention(q, k, v, sinks):
    B, S, Hq, hd = q.shape
    Hkv = k.shape[2]
    G = Hq // Hkv
    nb = S // ATTN_BLOCK
    f32 = jnp.float32
    qb = q.astype(f32).reshape(B, nb, ATTN_BLOCK, Hkv, G, hd)

    def band(t):
        tb = t.astype(f32).reshape(B, nb, ATTN_BLOCK, Hkv, hd)
        prev = jnp.concatenate([jnp.zeros_like(tb[:, :1]), tb[:, :-1]], axis=1)
        return jnp.concatenate([prev, tb], axis=2)

    kb, vb = band(k), band(v)
    s = jnp.einsum('bnqhgd,bnkhd->bhgnqk', qb, kb) * (hd ** -0.5)
    qi = jnp.arange(ATTN_BLOCK)[:, None]
    kj = jnp.arange(2 * ATTN_BLOCK)[None, :]
    dist = qi + ATTN_BLOCK - kj
    in_window = (dist >= 0) & (dist < WINDOW)
    has_prev = (jnp.arange(nb)[:, None, None] > 0) | (kj >= ATTN_BLOCK)[None]
    mask = in_window[None] & has_prev
    s = jnp.where(mask, s, -jnp.inf)
    sink = sinks.astype(f32).reshape(1, Hkv, G, 1, 1)
    m = jnp.maximum(jnp.max(s, axis=-1), sink)
    p = jnp.exp(s - m[..., None])
    den = jnp.sum(p, axis=-1) + jnp.exp(sink - m)
    o = jnp.einsum('bhgnqk,bnkhd->bnqhgd', p / den[..., None], vb)
    return o.reshape(B, S, Hq * hd).astype(q.dtype)

def causal_depthwise_conv(u, w, b):
    S = u.shape[1]
    K = w.shape[0]
    up = jnp.pad(u, ((0, 0), (K - 1, 0), (0, 0)))
    out = b
    for j in range(K):
        out = out + up[:, j:j + S] * w[j]
    return out

def mlstm_chunkwise(q, k, v, i_pre, f_pre):
    B, S, H, Dh = q.shape
    Dv = v.shape[-1]
    L = MLSTM_CHUNK
    nc = S // L
    f32 = jnp.float32

    def to_chunks(t):
        return t.astype(f32).reshape(B, nc, L, H, -1).transpose(0, 3, 1, 2, 4)

    qc, kc, vc = to_chunks(q), to_chunks(k), to_chunks(v)
    log_i = i_pre.astype(f32).reshape(B, nc, L, H).transpose(0, 3, 1, 2)
    log_f = jax.nn.log_sigmoid(f_pre.astype(f32)).reshape(B, nc, L, H).transpose(0, 3, 1, 2)
    b = jnp.cumsum(log_f, axis=-1)
    b_last = b[..., -1]

    w_state = b_last[..., None] - b + log_i
    m_loc = jnp.max(w_state, axis=-1)
    e_state = jnp.exp(w_state - m_loc[..., None])
    kv_chunk = jnp.einsum('bhcld,bhcle->bhcde', kc * e_state[..., None], vc)
    n_chunk = jnp.einsum('bhcl,bhcld->bhcd', e_state, kc)

    def step(carry, inp):
        C, n, m = carry
        kv_c, n_c, m_c, bl = inp
        m_new = jnp.maximum(bl + m, m_c)
        a = jnp.exp(bl + m - m_new)
        s = jnp.exp(m_c - m_new)
        C_new = a[..., None, None] * C + s[..., None, None] * kv_c
        n_new = a[..., None] * n + s[..., None] * n_c
        return (C_new, n_new, m_new), (C, n, m)

    init = (jnp.zeros((B, H, Dh, Dv), f32), jnp.zeros((B, H, Dh), f32), jnp.zeros((B, H), f32))
    xs = (jnp.moveaxis(kv_chunk, 2, 0), jnp.moveaxis(n_chunk, 2, 0),
          jnp.moveaxis(m_loc, 2, 0), jnp.moveaxis(b_last, 2, 0))
    _, (C_prev, n_prev, m_prev) = lax.scan(step, init, xs)
    C_prev = jnp.moveaxis(C_prev, 0, 2)
    n_prev = jnp.moveaxis(n_prev, 0, 2)
    m_prev = jnp.moveaxis(m_prev, 0, 2)

    causal = jnp.tril(jnp.ones((L, L), dtype=bool))
    d_mat = b[..., :, None] - b[..., None, :] + log_i[..., None, :]
    d_mat = jnp.where(causal, d_mat, -jnp.inf)
    g = b + m_prev[..., None]
    m_t = jnp.maximum(jnp.max(d_mat, axis=-1), g)
    p = jnp.exp(d_mat - m_t[..., None])
    qk = jnp.einsum('bhctd,bhcsd->bhcts', qc, kc) * p
    inter = jnp.exp(g - m_t)
    num = jnp.einsum('bhcts,bhcse->bhcte', qk, vc) + inter[..., None] * jnp.einsum('bhctd,bhcde->bhcte', qc, C_prev)
    den = jnp.sum(qk, axis=-1) + inter * jnp.einsum('bhctd,bhcd->bhct', qc, n_prev)
    den = jnp.maximum(jnp.abs(den), jnp.exp(-m_t))
    h = num / den[..., None]
    return h.transpose(0, 2, 3, 1, 4).reshape(B, S, H, Dv).astype(q.dtype)

def grouped_moe(h, router_w, router_bias, w_gate, w_up, w_down):
    B, S, D = h.shape
    T = B * S
    E = N_EXPERTS
    f32 = jnp.float32
    xt = h.reshape(T, D)
    scores = jax.nn.sigmoid(xt.astype(f32) @ router_w.astype(f32))
    sel = scores + router_bias.astype(f32)
    grp = sel.reshape(T, N_GROUPS, EXPERTS_PER_GROUP)
    grp_score = jnp.sum(lax.top_k(grp, TOP_K)[0], axis=-1)
    g_idx = jnp.argmax(grp_score, axis=-1)
    in_grp = jnp.take_along_axis(grp, g_idx[:, None, None], axis=1)[:, 0]
    _, local = lax.top_k(in_grp, TOP_K)
    expert_idx = (g_idx[:, None] * EXPERTS_PER_GROUP + local).astype(jnp.int32)
    gate = jnp.take_along_axis(scores, expert_idx, axis=1)
    gate = gate / jnp.sum(gate, axis=-1, keepdims=True)

    n_assign = T * TOP_K
    flat_e = expert_idx.reshape(-1)
    flat_tok = jnp.arange(n_assign, dtype=jnp.int32) // TOP_K
    order = jnp.argsort(flat_e)
    e_sorted = flat_e[order]
    tok_sorted = flat_tok[order]
    gate_sorted = gate.reshape(-1)[order]
    counts = jnp.zeros((E,), jnp.int32).at[flat_e].add(1)
    starts = jnp.cumsum(counts) - counts
    padded = (counts + MOE_BLOCK - 1) // MOE_BLOCK * MOE_BLOCK
    pad_ends = jnp.cumsum(padded)
    pad_starts = pad_ends - padded
    dest = pad_starts[e_sorted] + jnp.arange(n_assign, dtype=jnp.int32) - starts[e_sorted]
    n_blocks = (n_assign + E * (MOE_BLOCK - 1) + MOE_BLOCK - 1) // MOE_BLOCK
    x_pad = jnp.zeros((n_blocks * MOE_BLOCK, D), xt.dtype).at[dest].set(xt[tok_sorted])
    blk_start = jnp.arange(n_blocks, dtype=jnp.int32) * MOE_BLOCK
    blk_e = jnp.minimum(jnp.searchsorted(pad_ends, blk_start, side='right'), E - 1)

    def expert_block(args):
        xb, e = args
        return (jax.nn.silu(xb @ w_gate[e]) * (xb @ w_up[e])) @ w_down[e]

    y_pad = lax.map(expert_block, (x_pad.reshape(n_blocks, MOE_BLOCK, D), blk_e)).reshape(-1, D)
    y = jax.ops.segment_sum(y_pad[dest] * gate_sorted[:, None].astype(y_pad.dtype), tok_sorted, num_segments=T)
    return y.reshape(B, S, D)

def setup_inputs(seed: int = 0) -> dict:
    key = jax.random.key(seed)
    ks = jax.random.split(key, 26)
    nrm = jax.random.normal
    D = D_MODEL
    E = N_EXPERTS
    F = D_FF_EXPERT
    x = nrm(ks[0], (BATCH, SEQ, D), jnp.float32)
    c = nrm(ks[1], (BATCH, D), jnp.float32)
    offs = jax.random.randint(ks[2], (BATCH, 1), 0, 4096, dtype=jnp.int32)
    positions = (jnp.arange(SEQ, dtype=jnp.int32)[None, :] + offs).astype(jnp.int32)
    ada_w = nrm(ks[3], (DEPTH, D, 6 * D)) * (0.5 * D ** -0.5)
    ada_b = 0.02 * nrm(ks[4], (DEPTH, 6 * D))
    norm_mix_w = 1.0 + 0.05 * nrm(ks[5], (DEPTH, D))
    norm_ffn_w = 1.0 + 0.05 * nrm(ks[6], (DEPTH, D))
    w_in = nrm(ks[7], (DEPTH, D, D_IN)) * D ** -0.5
    b_igate = 0.1 * nrm(ks[8], (DEPTH, MLSTM_HEADS))
    b_fgate = jnp.linspace(3.0, 6.0, MLSTM_HEADS)[None, :] + 0.1 * nrm(ks[9], (DEPTH, MLSTM_HEADS))
    q_norm_w = 1.0 + 0.05 * nrm(ks[10], (DEPTH, ATTN_HEAD_DIM))
    k_norm_w = 1.0 + 0.05 * nrm(ks[11], (DEPTH, ATTN_HEAD_DIM))
    sinks = 0.5 * nrm(ks[12], (DEPTH, ATTN_HEADS))
    conv_w = nrm(ks[13], (DEPTH, CONV_WIDTH, 2 * MLSTM_W)) * CONV_WIDTH ** -0.5
    conv_b = 0.02 * nrm(ks[14], (DEPTH, 2 * MLSTM_W))
    mlstm_norm_w = 1.0 + 0.05 * nrm(ks[15], (DEPTH, MLSTM_W))
    w_attn_up = nrm(ks[16], (DEPTH, ATTN_Q_W, D)) * ATTN_Q_W ** -0.5
    w_mlstm_up = nrm(ks[17], (DEPTH, MLSTM_W, D)) * MLSTM_W ** -0.5
    w_out = nrm(ks[18], (DEPTH, D, D)) * D ** -0.5
    router_w = nrm(ks[19], (D, E)) * D ** -0.5
    router_bias = 0.01 * nrm(ks[20], (E,))
    w_gate = nrm(ks[21], (DEPTH, E, D, F)) * D ** -0.5
    w_up = nrm(ks[22], (DEPTH, E, D, F)) * D ** -0.5
    w_down = nrm(ks[23], (DEPTH, E, F, D)) * F ** -0.5
    return {"x": x, "c": c, "positions": positions, "ada_w": ada_w, "ada_b": ada_b,
            "norm_mix_w": norm_mix_w, "norm_ffn_w": norm_ffn_w, "w_in": w_in,
            "b_igate": b_igate, "b_fgate": b_fgate, "q_norm_w": q_norm_w, "k_norm_w": k_norm_w,
            "sinks": sinks, "conv_w": conv_w, "conv_b": conv_b, "mlstm_norm_w": mlstm_norm_w,
            "w_attn_up": w_attn_up, "w_mlstm_up": w_mlstm_up, "w_out": w_out,
            "router_w": router_w, "router_bias": router_bias,
            "w_gate": w_gate, "w_up": w_up, "w_down": w_down}

def reference(x, c, positions, ada_w, ada_b, norm_mix_w, norm_ffn_w, w_in, b_igate, b_fgate,
              q_norm_w, k_norm_w, sinks, conv_w, conv_b, mlstm_norm_w, w_attn_up, w_mlstm_up,
              w_out, router_w, router_bias, w_gate, w_up, w_down):
    B, S, D = x.shape
    inv_freq = ROPE_THETA ** (-(jnp.arange(0, ROPE_DIM, 2, dtype=jnp.float32) / ROPE_DIM))
    ang = positions.astype(jnp.float32)[..., None] * inv_freq
    cos = jnp.cos(ang)[:, :, None, :]
    sin = jnp.sin(ang)[:, :, None, :]
    c_act = jax.nn.silu(c)

    for l in range(DEPTH):
        mod = c_act @ ada_w[l] + ada_b[l]
        sh1, sc1, g1, sh2, sc2, g2 = [t[:, None, :] for t in jnp.split(mod, 6, axis=-1)]

        h = rms_norm(x, norm_mix_w[l]) * (1.0 + sc1) + sh1
        proj = h @ w_in[l]
        aq, ak, av, mqk, mv, mi, mf, mo, ga, gb = split_cols(proj)

        aq = rms_norm(aq.reshape(B, S, ATTN_HEADS, ATTN_HEAD_DIM), q_norm_w[l])
        ak = rms_norm(ak.reshape(B, S, ATTN_KV_HEADS, ATTN_HEAD_DIM), k_norm_w[l])
        aq = partial_rope(aq, cos, sin)
        ak = partial_rope(ak, cos, sin)
        av = av.reshape(B, S, ATTN_KV_HEADS, ATTN_HEAD_DIM)
        ya = sliding_window_attention(aq, ak, av, sinks[l]) @ w_attn_up[l]

        mqk = jax.nn.silu(causal_depthwise_conv(mqk, conv_w[l], conv_b[l]))
        mq = mqk[..., :MLSTM_W].reshape(B, S, MLSTM_HEADS, MLSTM_HEAD_DIM)
        mk = mqk[..., MLSTM_W:].reshape(B, S, MLSTM_HEADS, MLSTM_HEAD_DIM) * (MLSTM_HEAD_DIM ** -0.5)
        mv = mv.reshape(B, S, MLSTM_HEADS, MLSTM_HEAD_DIM)
        hm = mlstm_chunkwise(mq, mk, mv, mi + b_igate[l], mf + b_fgate[l])
        hm = rms_norm(hm, mlstm_norm_w[l].reshape(MLSTM_HEADS, MLSTM_HEAD_DIM)).reshape(B, S, MLSTM_W)
        yb = (jax.nn.sigmoid(mo) * hm) @ w_mlstm_up[l]

        merged = jax.nn.sigmoid(ga) * ya + jax.nn.sigmoid(gb) * yb
        x = x + g1 * (merged @ w_out[l])

        h2 = rms_norm(x, norm_ffn_w[l]) * (1.0 + sc2) + sh2
        x = x + g2 * grouped_moe(h2, router_w, router_bias, w_gate[l], w_up[l], w_down[l])
    return x


_drawn_inputs = setup_inputs


def setup_inputs(seed=0):
    import zlib

    import numpy as np

    out = dict(_drawn_inputs(seed))
    spreads = {}
    factors = {'norm_mix_w': 3.114,
     'b_igate': 64.0,
     'q_norm_w': 6.957,
     'k_norm_w': 6.521,
     'sinks': 8.0,
     'conv_b': 17.882}
    for name, (base, spread) in spreads.items():
        noise = np.random.default_rng([zlib.crc32(name.encode()), seed]).standard_normal(out[name].shape)
        drawn = base * np.exp(spread * noise) if base else spread * noise
        out[name] = __import__('jax').numpy.asarray(drawn.astype(out[name].dtype))
    for name, factor in factors.items():
        out[name] = (out[name] * factor).astype(out[name].dtype)
    return out
```

```python
from contextlib import ExitStack

import numpy as np

import concourse.bass as bass
from concourse import mybir

ALU = mybir.AluOpType
ACT = mybir.ActivationFunctionType
F32 = mybir.dt.float32
BF16 = mybir.dt.bfloat16
I32 = mybir.dt.int32
U32 = mybir.dt.uint32
AX = mybir.AxisListType

P = 128
NEG = -1.0e30
THETA = 500000.0
EPS = 1e-6
MB = 64
RING = 6
MIX_SLOTS = 4


def group_order(NT, NH, HM):
    o = [("ada", j) for j in range(12)]
    o += [("h1T", k) for k in range(8)]
    for i in range(NT):
        o += [("q", i), ("kv", i)]
    o += [("gates", 0)]
    for m in range(8):
        o += [("mqk", m)]
        if 1 <= m <= NT:
            o += [("qT", m - 1), ("kT", m - 1)]
    o += [("mv", i) for i in range(NT)]
    o += [("mo", i) for i in range(NT)]
    o += [("rT", 0)] + [("mubc", h) for h in range(HM)] + [("dec", 0)]
    for j in range(8):
        o += [("ga", j), ("ya", j)]
    o += [("gb", 0), ("gb", 1)]
    o += [("hmT", i) for i in range(NT)]
    for j in range(8):
        if j >= 2:
            o += [("gb", j)]
        o += [("yb", j)]
    for i in range(NT):
        o += [("wo", 2 * i), ("wo", 2 * i + 1)]
    o += [("h2T", k) for k in range(8)]
    o += [("rl", 0), ("lg", 0), ("rank", 0)]
    return {name: n for n, name in enumerate(o)}


def trunk(nc, x, c, positions, ada_w, ada_b, norm_mix_w, norm_ffn_w, w_in, b_igate, b_fgate,
          q_norm_w, k_norm_w, sinks, conv_w, conv_b, mlstm_norm_w, w_attn_up, w_mlstm_up, w_out,
          router_w, router_bias, w_gate, w_up, w_down, out):
    _, S, D = x.shape
    DEPTH = ada_w.shape[0]
    NT = S // P
    KD = D // P
    HD = q_norm_w.shape[1]
    HQ = sinks.shape[1]
    HKV = HQ // 4
    G = HQ // HKV
    ROPE = HD // 4
    HALF = ROPE // 2
    HM = b_igate.shape[1]
    DM = 128
    E = router_w.shape[1]
    NG = 4
    EG = E // NG
    F = w_gate.shape[3]
    FC = F // P
    assert (S, D, HD, HQ, HM, E, F) == (512, 1024, 64, 8, 4, 16, 512)
    MAXB = (2 * S + E * (MB - 1)) // MB
    ROWS = ((MAXB + 1) * MB + P - 1) // P * P
    AQ, AK, MQK, MV, MI, MF, MO, GA, GB = 0, 512, 768, 1792, 2304, 2308, 2312, 2824, 3848
    assert GB + D == w_in.shape[2]
    GI = group_order(NT, HM, HM)
    KSCALE = DM ** -0.5 / 4.0

    xd = nc.dram_tensor("dispatched_rows", [ROWS, D], F32).ap()
    yd = nc.dram_tensor("expert_rows", [ROWS, D], F32).ap()

    with ExitStack() as ctx:
        def sb(name, shape, dt=F32):
            return ctx.enter_context(nc.sbuf_tensor(name, shape, dt))

        ring = sb("weight_ring", [P, RING, 4096])
        xs = sb("x_tokens", [P, NT, D])
        regA = sb("regA", [P, NT * D])
        hT = sb("h_features", [P, KD, S])
        regB = sb("regB", [P, 6 * S])
        regP = sb("regP", [P, 2 * 2 * 512])
        regU = sb("regU", [P, 2 * 516])
        vaug = sb("mlstm_v_and_one", [P, NT, HM, DM + 1])
        merged = sb("merged_features", [P, KD, S])

        xn = regA[:, :].rearrange("p (i d) -> p i d", i=NT)
        qk_rows = regA[:, 0:NT * 768].rearrange("p (i n) -> p i n", i=NT)
        attn_o = regA[:, 0:4 * S].rearrange("p (c t) -> p c t", c=4)
        rstack = regA[:, NT * 896:NT * 896 + S]
        v_rows = regA[:, NT * 768:NT * 768 + NT * P].rearrange("p (i n) -> p i n", i=NT)
        qkT = regB[:, :].rearrange("p (c t) -> p c t", c=6)
        hmT = regB[:, 0:4 * S].rearrange("p (c t) -> p c t", c=4)
        num = regB[:, 4 * S:4 * S + HM * (DM + 1)].rearrange("p (h n) -> p h n", h=HM)
        pT = regP[:, :].rearrange("p (b k n) -> p b k n", b=2, k=2)
        ke = regP[:, 0:256].rearrange("p (b n) -> p b n", b=2)
        ex = regP[:, 256:512].rearrange("p (b n) -> p b n", b=2)
        wS = regP[:, 512:768].rearrange("p (b n) -> p b n", b=2)
        icb = regP[:, 768:768 + 2 * (DM + 1)].rearrange("p (b n) -> p b n", b=2)
        cst = regP[:, 1028:1028 + HM * (DM + 1)].rearrange("p (h n) -> p h n", h=HM)
        sqs = regP[:, 1544:1544 + 128]
        prm = regP[:, 1024:1024 + P]
        rt = regP[:, 0:1024]
        mqkT = ring[:, 4, :].rearrange("p (m t) -> p m t", m=KD)
        prob = ring[:, 5, 0:2048].rearrange("p (b h n) -> p b h n", b=2, h=4)
        argm = ring[:, 5, 0:2048].rearrange("p (h t) -> p h t", h=HM)
        mo_t = ring[:, 5, 2048:4096].rearrange("p (i n) -> p i n", i=NT)
        conv_u = regU[:, :].rearrange("p (b n) -> p b n", b=2)
        tb = regU[:, 0:1024].rearrange("p (b n) -> p b n", b=2)
        mflat = merged[:, :, :].rearrange("p a b -> p (a b)")
        small = mflat[:, 0:D]
        squares = hT[:, 0:2, :].rearrange("p a b -> p (a b)")
        xg = mflat[0:MB, 0:D]
        xT = mflat[:, 1024:1024 + KD * MB].rearrange("p (k r) -> p k r", k=KD)
        hsil = mflat[:, 1536:2048]
        hx = mflat[0:MB, 2048:2560]
        hxT = mflat[:, 2560:2560 + FC * MB].rearrange("p (k r) -> p k r", k=FC)
        yb = mflat[:, 3072:3584]
        rows4 = mflat[0:HM, D:D + 6 * S].rearrange("p (r t) -> p r t", r=6)
        yg = ring[:, 4:6, :].rearrange("p a b -> p (a b)").rearrange("p (i s d) -> p i s d", i=NT, s=2)
        mrow = regU[:, 0:1024].rearrange("p (b n) -> p b n", b=2)

        ident = sb("ident", [P, P])
        ones = sb("ones", [P, P])
        onesb = sb("ones_bf16", [P, P], BF16)
        triu = sb("strictly_before_bf16", [P, P], BF16)
        mask = sb("window_mask", [P, 256])
        maskT = sb("causal_mask_T", [P, P])
        fold = sb("fold16", [P, E])
        cz = sb("c_padded", [P, KD, 32])
        rwz = sb("router_padded", [P, KD, 32])
        cosr = sb("cos", [P, NT, HALF])
        sinr = sb("sin", [P, NT, HALF])
        rbias = sb("router_bias", [P, E])
        thr = sb("block_thresholds", [P, 7])
        iog = sb("iota_minus", [P, 4])
        ioe = sb("block_iota", [1, 32])
        nhalf = sb("minus_half", [P, 16])
        pc = sb("param_cols", [P, P])
        modc = sb("mod_cols", [P, 48])
        A1 = sb("scale1", [P, KD])
        A2 = sb("scale2", [P, KD])
        wmc = sb("mlstm_norm_half", [P, HM])
        g1bc = sb("g1_rows", [P, D])
        g2bc = sb("g2_rows", [P, 512])
        wqk = sb("qk_norm_rows", [P, 2, HD])
        gbias = sb("gate_bias", [36, 1])
        sinkb = sb("sinks", [P, HQ])
        wg36 = sb("gate_columns", [P, KD, 36])
        ss = sb("sum_sq", [P, 16])
        rs = sb("rstd", [P, 16])
        ssq = sb("sum_sq_qk", [P, 16])
        rsq = sb("rstd_qk", [P, 16])
        att = sb("att_small", [P, 2, 32])
        g16 = sb("gate_small", [HM, 40])
        colR = sb("gate_cols", [P, NT, 4, HM])
        decb = sb("decay", [P, HM, 4])
        fin = sb("fin_small", [P, 32])
        Mb = sb("assigned_bf16", [P, NT, E], BF16)
        slot_u = sb("slot_index", [P, 2, NT], U32)
        wsel = sb("gate_weights", [P, 2, NT])
        tabs = sb("block_tables", [1, 64], I32)

        ps = [ctx.enter_context(nc.psum_tensor(f"bank{b}", [P, 512], F32)) for b in range(8)]
        pj = ps[0:2]
        att_s = [ps[2], ps[3]]
        att_t = [ps[4], ps[5]]

        cleared = []

        def lsem(name):
            s = ctx.enter_context(nc.semaphore(name))
            cleared.append(s)
            return s

        swdma = []

        def psem(name):
            s = ctx.enter_context(nc.semaphore(name))
            swdma.append(s)
            return s

        def gsem(name):
            return ctx.enter_context(nc.semaphore(name))

        const_in, const_ready, pool_const, dve_const, act_const = (gsem(n) for n in (
            "const_in", "const_ready", "pool_const", "dve_const", "act_const"))
        zeroed, rows_zeroed, c_cols, x_in, meet_a, meet_b = (gsem(n) for n in (
            "zeroed", "rows_zeroed", "c_cols", "x_in", "meet_a", "meet_b"))
        ring_in = [lsem(f"ring_in{s}") for s in range(MIX_SLOTS)]
        params_in, scattered, xg_in, y_out = (psem(n) for n in ("params_in", "scattered", "xg_in", "y_out"))
        yg_in = [psem(f"yg_in{i}") for i in range(NT)]
        pj_ready = lsem("pj_ready")
        pj_free = [lsem("pj_free0"), lsem("pj_free1")]
        param_cols, mrow_ready, bc_ready, bc_read = (lsem(n) for n in ("param_cols", "mrow_ready", "bc_ready", "bc_read"))
        mod_ready, act_step, dve_step, pool_step, pow_ask, pow_done = (lsem(n) for n in (
            "mod_ready", "act_step", "dve_step", "pool_step", "pow_ask", "pow_done"))
        xn_ready, qk_ready, qk_sq = lsem("xn_ready"), lsem("qk_ready"), lsem("qk_sq")
        s_ready, s_read, m_ready, e_ready, p_norm, pt_ready, pt_evac, o_ready, o_evac = (lsem(n) for n in (
            "s_ready", "s_read", "m_ready", "e_ready", "p_norm", "pt_ready", "pt_evac", "o_ready", "o_evac"))
        rows_ready = lsem("rows_ready")
        gates_f, stack_zero = lsem("gates_f"), lsem("stack_zero")
        ma_ready, ma_act, w_ready, mb_ready, ic_ready, c_upd, hm_ready = (lsem(n) for n in (
            "ma_ready", "ma_act", "w_ready", "mb_ready", "ic_ready", "c_upd", "hm_ready"))
        tb_sum, merged_ready, x_upd, ffn_sq = (lsem(n) for n in ("tb_sum", "merged_ready", "x_upd", "ffn_sq"))
        conv_in, conv_z, conv_t = lsem("conv_in"), lsem("conv_z"), lsem("conv_t")
        routed, tables = lsem("routed"), lsem("tables")
        xt_ready, xt_evac_a, xt_evac_d, gu_ready, sil_ready, hx_ready, ht_ready, ht_evac, y_ready, y_taken = (
            lsem(n) for n in ("xt_ready", "xt_evac_a", "xt_evac_d", "gu_ready", "sil_ready", "hx_ready",
                              "ht_ready", "ht_evac", "y_ready", "y_taken"))
        w_expert = [lsem("w_expert0"), lsem("w_expert1")]
        out_done, passed = gsem("out_done"), gsem("passed")

        def lay(ap, l):
            return ap[bass.ds(l, 1)]

        def cols8(w, l, c0, n):
            return lay(w, l)[:, :, c0:c0 + n].rearrange("a (k p) n -> p (a k) n", p=P)

        def mix_item(l, n):
            if n < 12:
                return cols8(ada_w, l, 512 * n, 512), 512, 8
            plan = [(AQ, 512), (AK, 256), (MQK, 512), (MQK + 512, 512), (MV, 512), (MO, 512), (GA, 512), (GA + 512, 512)]
            if n < 20:
                c0, w = plan[n - 12]
                return cols8(w_in, l, c0, w), w, 8
            if n == 20:
                return cols8(w_attn_up, l, 0, D), D, 4
            if n == 21:
                return cols8(w_mlstm_up, l, 0, D), D, 4
            if n < 24:
                return cols8(w_in, l, GB + 512 * (n - 22), 512), 512, 8
            return lay(w_out, l)[:, 512 * (n - 24):512 * (n - 23), :].rearrange("a (k p) n -> p (a k) n", p=P), D, 4

        IT_ADA, IT_Q, IT_KV, IT_MQK, IT_MV, IT_MO, IT_GA, IT_YA, IT_YB, IT_GB, IT_WO, N_ITEMS = 0, 12, 13, 14, 16, 17, 18, 20, 21, 22, 24, 26

        def slot(n, k, w):
            return ring[:, n % MIX_SLOTS, 0:k * w].rearrange("p (k n) -> p k n", k=k)

        LAST = [("ada", j) for j in range(12)] + [
            ("q", NT - 1), ("kv", NT - 1), ("mqk", 3), ("mqk", 7), ("mv", NT - 1), ("mo", NT - 1), ("ga", 3), ("ga", 7),
            ("ya", 7), ("yb", 7), ("gb", 3), ("gb", 7), ("wo", 2 * NT - 1), ("wo", 2 * NT - 1)]

        def through(eng, n):
            eng.wait_ge(pj_ready, GI[LAST[n]] + 1)

        def arrived(eng, n):
            eng.wait_ge(ring_in[n % MIX_SLOTS], 16 * (n // MIX_SLOTS + 1))

        def ready(eng, name, i=0):
            g = GI[(name, i)]
            eng.wait_ge(pj_ready, g + 1)
            return pj[g % 2], pj_free[g % 2]

        def wait_reg(eng, sem, value):
            eng.wait_ge(sem, value)
            eng.sem_inc(passed, 1)

        def layer_end(eng, l, mine, dma_sems=()):
            eng.sem_inc(meet_a, 1)
            wait_reg(eng, meet_a, l * 5 + 5)
            if dma_sems:
                eng.dma_reset(range(min(s.num for s in dma_sems), max(s.num for s in dma_sems) + 1))
            for s in list(mine) + list(dma_sems):
                eng.sem_clear(s)
            eng.sem_inc(meet_b, 1)
            wait_reg(eng, meet_b, l * 5 + 5)

        def share(n):
            return cleared[n::5]

        block = ctx.enter_context(nc.Block())

        @block.sync
        def _(sp):
            nc.sync.dma_start(xs[:, :, :], x.rearrange("a (i p) d -> p (a i) d", p=P)).then_inc(x_in, 16)
            with sp.Fori(0, DEPTH) as l:
                for n in range(N_ITEMS):
                    src, w, k = mix_item(l, n)
                    if n >= MIX_SLOTS:
                        through(sp, n - MIX_SLOTS)
                    sp.dma_start(slot(n, k, w), src).then_inc(ring_in[n % MIX_SLOTS], 16)

                wg_e = w_gate.rearrange("l e (k p) f -> (l e) p k f", p=P)
                wu_e = w_up.rearrange("l e (k p) f -> (l e) p k f", p=P)
                wd_e = w_down.rearrange("l e (k p) f -> (l e) p k f", p=P)

                def load(part, p, e):
                    src = (wg_e, wu_e, wd_e)[part][bass.ds(e, 1)].rearrange("a p k f -> p (a k) f")
                    dst = ring[:, 3 * p + part, :].rearrange("p (k n) -> p k n", k=(KD, KD, FC)[part])
                    sp.dma_start(dst, src).then_inc(w_expert[p], 16)

                through(sp, 22)
                load(2, 0, l * E)
                through(sp, 23)
                load(0, 1, l * E + 1)
                sp.wait_ge(pj_ready, GI[("hmT", NT - 1)] + 1)
                load(1, 1, l * E + 1)
                load(2, 1, l * E + 1)
                through(sp, 24)
                load(0, 0, l * E)
                load(1, 0, l * E)
                sp.wait_ge(tables, 1)
                with sp.Fori(1, E // 2) as i:
                    for p in range(2):
                        last = sp.value_load(tabs[0:1, bass.ds(i * 2 + (32 - 2 + p), 1)], min_val=1, max_val=MAXB)
                        wait_reg(sp, y_ready, last)
                        for part in range(3):
                            load(part, p, l * E + i * 2 + p)
                layer_end(sp, l, share(0))
            sp.dma_start(out.rearrange("a (i p) d -> p (a i) d", p=P), xs[:, :, :]).then_inc(out_done, 16)
            sp.wait_ge(out_done, 16)

        @block.gpsimd
        def _(pool):
            po = nc.gpsimd
            n_const = [0]

            def pc_link(ins):
                n_const[0] += 1
                ins.then_inc(pool_const, 1)
                pool.wait_ge(pool_const, n_const[0])

            with nc.allow_non_contiguous_dma(reason="small parameter loads"):
                po.dma_start(rt[:, 0:NT].bitcast(I32), positions.rearrange("a (i p) -> p (a i)", p=P)).then_inc(const_in, 16)
            po.dma_start(prm[0:KD, :], c.rearrange("a (k p) -> (a k) p", p=P)).then_inc(const_in, 16)
            po.dma_start(rbias[:, :], router_bias.rearrange("(a e) -> a e", a=1).to_broadcast([P, E])).then_inc(const_in, 16)
            po.memset(rwz[:, :, :], 0.0).then_inc(zeroed, 1)
            po.memset(cz[:, :, :], 0.0)
            po.memset(wg36[:, :, :], 0.0).then_inc(zeroed, 1)
            po.memset(mflat[:, 0:D], 0.0).then_inc(zeroed, 1)
            pool.wait_ge(zeroed, 3)
            po.memset(prm[32:64, :], 0.0).then_inc(zeroed, 1)
            pool.wait_ge(zeroed, 4)
            po.memset(prm[64:P, :], 0.0).then_inc(zeroed, 1)
            pool.wait_ge(zeroed, 5)
            po.dma_start(rwz[:, :, 0:E], router_w.rearrange("(k p) e -> p k e", p=P)).then_inc(const_in, 16)
            po.dma_start(xd.rearrange("(n p) d -> p n d", p=P),
                         mflat[:, 0:D].unsqueeze(1).to_broadcast([P, ROWS // P, D])).then_inc(rows_zeroed, 16)
            po.dma_start(yd[E * MB:ROWS, :].rearrange("(n p) d -> p n d", p=P),
                         mflat[:, 0:D].unsqueeze(1).to_broadcast([P, (ROWS - E * MB) // P, D])).then_inc(rows_zeroed, 16)
            po.memset(ones[:, :], 1.0)
            po.memset(onesb[:, :], 1.0)
            po.memset(ident[:, :], 0.0)
            po.memset(mask[:, :], 0.0)
            po.memset(maskT[:, :], 0.0)
            pc_link(po.memset(nhalf[:, :], -0.5))
            po.affine_select(out=ident[:, :], in_=ident[:, :], compare_op=ALU.not_equal, fill=1.0, base=0,
                             pattern=[[-1, P]], channel_multiplier=1)
            po.affine_select(out=mask[:, 0:P], in_=mask[:, 0:P], compare_op=ALU.is_gt, fill=NEG, base=0,
                             pattern=[[1, P]], channel_multiplier=-1)
            po.affine_select(out=mask[:, P:256], in_=mask[:, P:256], compare_op=ALU.is_ge, fill=NEG, base=0,
                             pattern=[[-1, P]], channel_multiplier=1)
            po.affine_select(out=maskT[:, :], in_=maskT[:, :], compare_op=ALU.is_ge, fill=NEG, base=0,
                             pattern=[[1, P]], channel_multiplier=-1)
            po.affine_select(out=triu[:, :], in_=onesb[:, :], compare_op=ALU.is_gt, fill=0.0, base=0,
                             pattern=[[1, P]], channel_multiplier=-1)
            for k in range(1, 8):
                po.memset(thr[:, k - 1:k], float(MB * k))
            for g in range(4):
                po.memset(iog[:, g:g + 1], float(g - 8))
            pc_link(po.iota(ioe[:, :], pattern=[[1, 32]], base=0, channel_multiplier=0, allow_small_or_imprecise_dtypes=True))

            def power(n, dst, src):
                pool.wait_ge(pow_ask, n)
                w = src.shape[1]
                po.tensor_tensor(dst, src, nhalf[:, 0:w], ALU.pow).then_inc(pow_done, 1)

            with pool.Fori(0, DEPTH) as l:
                def rows(dst, src):
                    po.dma_start(dst, src).then_inc(params_in, 16)

                pool.wait_ge(c_cols, 1)
                rows(prm[0:8, :], lay(norm_mix_w, l).rearrange("a (k p) -> (a k) p", p=P))
                rows(prm[8:16, :], lay(norm_ffn_w, l).rearrange("a (k p) -> (a k) p", p=P))
                rows(prm[16:48, :], lay(conv_w, l).rearrange("a j (m p) -> (a j m) p", p=P))
                rows(prm[48:56, :], lay(conv_b, l).rearrange("a (m p) -> (a m) p", p=P))
                rows(prm[56:60, :], lay(mlstm_norm_w, l).rearrange("a (m p) -> (a m) p", p=P))
                rows(prm[60:108, :], lay(ada_b, l).rearrange("a (m p) -> (a m) p", p=P))
                rows(g1bc[:, :], lay(ada_b, l)[:, 2 * D:3 * D].to_broadcast([P, D]))
                po.dma_start(g2bc[0:64, :], lay(ada_b, l)[:, 5 * D:5 * D + 512].to_broadcast([64, 512])).then_inc(y_out, 16)
                po.dma_start(g2bc[64:P, :], lay(ada_b, l)[:, 5 * D + 512:6 * D].to_broadcast([64, 512])).then_inc(y_out, 16)
                rows(wqk[:, 0, :], lay(q_norm_w, l).to_broadcast([P, HD]))
                rows(wqk[:, 1, :], lay(k_norm_w, l).to_broadcast([P, HD]))
                rows(sinkb[:, :], lay(sinks, l).to_broadcast([P, HQ]))
                with nc.allow_non_contiguous_dma(reason="gate columns and biases"):
                    rows(gbias[0:4, :], lay(b_igate, l).rearrange("a h -> h a"))
                    rows(gbias[32:36, :], lay(b_fgate, l).rearrange("a h -> h a"))
                    rows(wg36[:, :, 0:4], cols8(w_in, l, MI, 4))
                    rows(wg36[:, :, 32:36], cols8(w_in, l, MF, 4))

                power(1, rs[:, 0:NT], ss[:, 0:NT])
                pool.wait_ge(pj_ready, GI[("h1T", KD - 1)] + 1)
                po.memset(rstack[:, :], 0.0).then_inc(stack_zero, 1)
                for i in range(NT):
                    power(2 + i, rsq[:, 0:10], ssq[:, 0:10])
                for i in range(NT):
                    power(6 + i, fin[:, 8:12], fin[:, 4:8])
                for j in range(KD):
                    pool.wait_ge(tb_sum, j + 1)
                    po.tensor_tensor(merged[:, j, :], merged[:, j, :], tb[:, j % 2, :], ALU.add).then_inc(merged_ready, 1)
                for i in range(NT):
                    power(10 + i, rs[:, 4 + i:5 + i], ss[:, 4 + i:5 + i])

                pool.wait_ge(routed, 2)
                pool.wait_ge(xn_ready, 2 * NT)
                pool.wait_ge(rows_zeroed, 32)
                for k in range(2):
                    for i in range(NT):
                        po.indirect_dma_start(out=xd, out_offset=bass.IndirectOffsetOnAxis(ap=slot_u[:, k, i:i + 1], axis=0),
                                              in_=xn[:, i, :], in_offset=None).then_inc(scattered, 16)
                pool.wait_ge(scattered, 16 * 2 * NT)
                po.dma_start(xg, xd[0:MB, :]).then_inc(xg_in, 16)
                pool.wait_ge(tables, 1)
                nb = po.value_load(tabs[0:1, 47:48], min_val=E, max_val=MAXB)

                def load_rows(b):
                    po.dma_start(xg, xd[bass.ds(b * MB, MB), :]).then_inc(xg_in, 16)

                def store_rows(b):
                    for h in range(2):
                        po.dma_start(yd[bass.ds(b * MB, MB), 512 * h:512 * h + 512], yb[64 * h:64 * h + 64, :]).then_inc(y_out, 16)

                pool.wait_ge(xt_ready, 1)
                load_rows(1)
                with pool.Fori(1, nb) as b:
                    pool.wait_ge(xt_ready, b + 1)
                    load_rows(b + 1)
                    pool.wait_ge(y_taken, b + 1)
                    store_rows(b - 1)
                pool.wait_ge(y_taken, nb + 1)
                store_rows(nb - 1)
                pool.wait_ge(y_out, nb * 32 + 32)
                wait_reg(pool, xg_in, nb * 16 + 16)
                for i in range(NT):
                    for k in range(2):
                        po.indirect_dma_start(out=yg[:, i, k, :], out_offset=None, in_=yd,
                                              in_offset=bass.IndirectOffsetOnAxis(ap=slot_u[:, k, i:i + 1], axis=0)).then_inc(yg_in[i], 16)
                for i in range(NT):
                    pool.wait_ge(yg_in[i], 32)
                layer_end(pool, l, share(1), swdma)

        @block.scalar
        def _(act):
            ac = nc.scalar
            step = [0]

            def link(ins):
                step[0] += 1
                ins.then_inc(act_step, 1)
                act.wait_ge(act_step, step[0])

            act.wait_ge(dve_const, 1)
            ac.activation(sinr[:, :, :].rearrange("p i f -> p (i f)"), rt[:, 64:96], ACT.Sin).then_inc(act_const, 1)
            ac.activation(cosr[:, :, :].rearrange("p i f -> p (i f)"), rt[:, 96:128], ACT.Sin).then_inc(act_const, 1)
            act.wait_ge(c_cols, 1)
            ac.activation(cz[:, :, 0], ps[2][:, 0:KD], ACT.Silu).then_inc(act_const, 1)

            with act.Fori(0, DEPTH) as l:
                step[0] = 0
                for i in range(NT):
                    act.wait_ge(x_in, 16)
                    ac.activation(squares, xs[:, i, :], ACT.Square, accum_out=ss[:, i:i + 1]).then_inc(ffn_sq, 1)
                    act.wait_ge(ffn_sq, i + 1)
                for j in range(12):
                    bank, free = ready(act, "ada", j)
                    if j >= 2:
                        act.wait_ge(bc_ready, j - 1)
                    ac.activation(mrow[:, j % 2, :], bank[:, :], ACT.Copy).then_inc(mrow_ready, 1)
                    act.wait_ge(mrow_ready, j + 1)
                    act.sem_inc(free, 1)
                act.wait_ge(mod_ready, 1)
                for k in range(1, KD, 2):
                    bank, free = ready(act, "h1T", k)
                    ac.activation(hT[:, k, :], bank[:, :], ACT.Identity, scale=A1[:, k:k + 1],
                                  bias=modc[:, k:k + 1]).then_inc(free, 1)
                act.wait_ge(rows_zeroed, 32)
                for i in range(NT):
                    bank, free = ready(act, "q", i)
                    ac.activation(qk_rows[:, i, 0:512], bank[:, :], ACT.Copy)
                    if i >= 1:
                        act.wait_ge(qk_sq, i)
                    ac.activation(small[:, 0:512], bank[:, :], ACT.Square).then_inc(free, 1)
                    bank, free = ready(act, "kv", i)
                    ac.activation(qk_rows[:, i, 512:640], bank[:, 0:128], ACT.Copy)
                    ac.activation(v_rows[:, i, :], bank[:, 128:256], ACT.Copy)
                    ac.activation(small[:, 512:640], bank[:, 0:128], ACT.Square).then_inc(free, 1)
                bank, free = ready(act, "gates")
                ac.activation(rows4[:, 0, :], bank[0:4, :], ACT.Identity, bias=gbias[0:4, :]).then_inc(gates_f, 1)
                act.wait_ge(gates_f, 2)
                ac.activation(rows4[:, 2, :], rows4[:, 2, :], ACT.Exp, scale=-1.0).then_inc(gates_f, 1)
                act.wait_ge(gates_f, 3)
                ac.activation(rows4[:, 2, :], rows4[:, 2, :], ACT.Ln, bias=1.0).then_inc(gates_f, 1)

                def conv_act(m):
                    bank, free = ready(act, "mqk", m)
                    if m >= 2:
                        act.wait_ge(conv_z, m - 1)
                    ac.activation(conv_u[:, m % 2, 3:515], bank[:, :], ACT.Copy).then_inc(conv_in, 1)
                    act.wait_ge(conv_in, m + 1)
                    act.sem_inc(free, 1)

                def conv_tanh(m):
                    act.wait_ge(conv_z, m + 1)
                    if m == 0:
                        act.wait_ge(qk_sq, NT)
                    if m >= 1:
                        act.wait_ge(conv_t, 2 * m)
                    ac.activation(small[:, 0:512], mqkT[:, m, :], ACT.Tanh, scale=0.5).then_inc(conv_t, 1)

                def qkT_evac(i):
                    bank, free = ready(act, "qT", i)
                    ac.activation(qkT[:, 0:4, P * i:P * i + P], bank[:, :].rearrange("p (c t) -> p c t", c=4), ACT.Copy).then_inc(free, 1)
                    bank, free = ready(act, "kT", i)
                    ac.activation(qkT[:, 4:6, P * i:P * i + P], bank[:, 0:256].rearrange("p (c t) -> p c t", c=2), ACT.Copy).then_inc(free, 1)

                def att_exp(u):
                    n, g = u // HKV, u % HKV
                    lo = 0 if n else P
                    act.wait_ge(m_ready, u + 1)
                    a = att[:, u % 2, :]
                    for h in range(4):
                        ac.activation(prob[:, u % 2, h, lo:256], prob[:, u % 2, h, lo:256], ACT.Exp,
                                      bias=a[:, 4 + h:5 + h], accum_out=a[:, 8 + h:9 + h])
                    ac.activation(a[:, 12:16], a[:, 16:20], ACT.Exp).then_inc(e_ready, 1)

                def att_pt(u):
                    n = u // HKV
                    act.wait_ge(pt_ready, u + 1)
                    if u >= 2:
                        act.wait_ge(o_ready, u - 1)
                    ac.activation(pT[:, u % 2, 1, :], att_t[1][:, :], ACT.Copy).then_inc(pt_evac, 1)

                def att_o(u):
                    n, g = u // HKV, u % HKV
                    act.wait_ge(o_ready, u + 1)
                    o4 = ps[6][0:64, :].rearrange("p (a b t) -> p b a t", a=2, b=2)
                    for odd in range(2):
                        last = ac.activation(attn_o[64 * odd:64 * odd + 64, 2 * g:2 * g + 2, P * n:P * n + P], o4[:, odd], ACT.Copy)
                    last.then_inc(o_evac, 1)

                for s in range(16):
                    if s < 8:
                        conv_act(s)
                    elif s < 12:
                        i = s - 8
                        bank, free = ready(act, "mv", i)
                        ac.activation(vaug[:, i, :, 0:DM], bank[:, :].rearrange("p (h n) -> p h n", h=HM), ACT.Copy).then_inc(free, 1)
                    else:
                        i = s - 12
                        bank, free = ready(act, "mo", i)
                        ac.activation(mo_t[:, i, :], bank[:, :], ACT.Tanh, scale=0.5).then_inc(free, 1)
                    if 1 <= s <= NT:
                        qkT_evac(s - 1)
                    if 1 <= s <= 8:
                        conv_tanh(s - 1)
                    if 4 <= s < 12:
                        att_exp(s - 4)
                    if 5 <= s < 13:
                        att_pt(s - 5)
                    if 6 <= s < 14:
                        att_o(s - 6)
                    if s == 8:
                        act.wait_ge(rows_ready, 1)
                        for q in (32, 64, 96):
                            ac.activation(rstack[q:q + 4, :], rstack[q:q + 4, :], ACT.Exp)
                        ac.activation(g16[:, 24:28], g16[:, 20:24], ACT.Exp).then_inc(rows_ready, 1)
                bank, free = ready(act, "rT")
                for q in range(4):
                    ins = ac.activation(colR[:, :, q, :], bank[:, :].rearrange("p (i n) -> p i n", i=NT)[:, :, 32 * q:32 * q + HM], ACT.Copy)
                ins.then_inc(free, 1)
                act.wait_ge(free, GI[("rT", 0)] // 2 + 1)

                def m_act_a(u):
                    c_, h = u // HM, u % HM
                    act.wait_ge(ma_ready, u + 1)
                    if u >= 2:
                        act.wait_ge(mb_ready, u - 1)
                    b = 2 + u % 2
                    ac.activation(ke[:, u % 2, :], ps[b][:, 0:P], ACT.Copy, scale=colR[:, c_, 2, h:h + 1])
                    ac.activation(ex[:, u % 2, :], argm[:, h, P * c_:P * c_ + P], ACT.Exp, bias=colR[:, c_, 0, h:h + 1]).then_inc(ma_act, 1)

                def m_act_b(u):
                    c_, h = u // HM, u % HM
                    act.wait_ge(mb_ready, u + 1)
                    if c_ > 0:
                        if u >= HM + 2:
                            act.wait_ge(c_upd, u - 1)
                        ac.activation(icb[:, u % 2, :], ps[4 + u % 2][:, 256:256 + DM + 1], ACT.Copy,
                                      scale=colR[:, c_, 1, h:h + 1]).then_inc(ic_ready, 1)

                act.wait_ge(pj_free[GI[("mubc", HM - 1)] % 2], GI[("mubc", HM - 1)] // 2 + 1)
                act.wait_ge(pj_free[GI[("mubc", HM - 2)] % 2], GI[("mubc", HM - 2)] // 2 + 1)
                for j in range(8):
                    bank, free = ready(act, "ga", j)
                    ac.activation(merged[:, j, :], bank[:, :], ACT.Tanh, scale=0.5).then_inc(free, 1)
                    for u in (2 * j, 2 * j + 1):
                        m_act_a(u)
                        if u >= 1:
                            m_act_b(u - 1)
                m_act_b(15)
                for j in range(8):
                    bank, free = ready(act, "gb", j)
                    if j >= 2:
                        act.wait_ge(merged_ready, j - 1)
                    ac.activation(tb[:, j % 2, :], bank[:, :], ACT.Tanh, scale=0.5).then_inc(free, 1)

                for i in range(NT):
                    act.wait_ge(x_upd, i + 1)
                    act.wait_ge(ffn_sq, NT + i)
                    ac.activation(squares, xs[:, i, :], ACT.Square, accum_out=ss[:, 4 + i:5 + i]).then_inc(ffn_sq, 1)
                for k in range(1, KD, 2):
                    bank, free = ready(act, "h2T", k)
                    ac.activation(hT[:, k, :], bank[:, :], ACT.Identity, scale=A2[:, k:k + 1],
                                  bias=modc[:, 24 + k:25 + k]).then_inc(free, 1)
                bank, free = ready(act, "rl")
                act.wait_ge(ffn_sq, 2 * NT)
                ac.activation(small[:, 0:512], bank[:, :], ACT.Copy).then_inc(free, 1)
                bank, free = ready(act, "lg")
                ac.activation(rt[:, 0:64], bank[:, 0:64], ACT.Exp, scale=-1.0).then_inc(free, 1)

                act.wait_ge(tables, 1)
                nb = ac.value_load(tabs[0:1, 47:48], min_val=E, max_val=MAXB)

                def xt_act():
                    for k in range(0, KD, 2):
                        last = ac.activation(xT[:, k, :], ps[2][:, MB * k:MB * k + MB], ACT.Identity,
                                             scale=A2[:, k:k + 1], bias=modc[:, 24 + k:25 + k])
                    last.then_inc(xt_evac_a, 1)

                act.wait_ge(xt_ready, 1)
                xt_act()
                with act.Fori(0, nb) as b:
                    act.wait_ge(gu_ready, b + 1)
                    ac.activation(hsil[64:P, :], ps[3][0:64, :], ACT.Silu).then_inc(sil_ready, 1)
                    act.wait_ge(xt_ready, b + 2)
                    xt_act()
                    act.wait_ge(ht_ready, b + 1)
                    ac.activation(hxT[:, :, :].rearrange("p k r -> p (k r)"), ps[4][:, 0:FC * MB], ACT.Copy).then_inc(ht_evac, 1)
                layer_end(act, l, share(2))

        @block.tensor
        def _(pe):
            te = nc.tensor
            pe.wait_ge(const_in, 16 * 4)
            pe.wait_ge(pool_const, 2)
            te.transpose(ps[2][:, 0:KD], prm[0:KD, :], ident[0:KD, 0:KD]).then_inc(c_cols, 1)
            pe.wait_ge(act_const, 3)
            pe.wait_ge(dve_const, 3)

            with pe.Fori(0, DEPTH) as l:
                def take(name, i=0):
                    g = GI[(name, i)]
                    if g >= 2:
                        pe.wait_ge(pj_free[g % 2], g // 2)
                    return pj[g % 2]

                pe.wait_ge(params_in, 14 * 16)
                te.transpose(ps[4][:, 0:P], prm[:, :], ident[:, :]).then_inc(param_cols, 1)

                def bcast(j):
                    pe.wait_ge(mrow_ready, j + 1)
                    if j >= 2:
                        pe.wait_ge(bc_read, j - 1)
                    te.matmul(ps[2 + j % 2][:, :], ones[:, :], mrow[:, j % 2, :], start=True, stop=True).then_inc(bc_ready, 1)

                for j in range(12):
                    arrived(pe, IT_ADA + j)
                    bank = take("ada", j)
                    w = slot(j, 8, 512)
                    for k in range(KD):
                        g = k % 4
                        ins = te.matmul(bank[32 * g:32 * g + 32, :], cz[:, k, :], w[:, k, :], start=(k < 4), stop=(k >= 4))
                    ins.then_inc(pj_ready, 1)
                    if j >= 1:
                        bcast(j - 1)
                bcast(11)

                pe.wait_ge(xn_ready, NT)
                for k in range(KD):
                    bank = take("h1T", k)
                    for i in range(NT):
                        ins = te.transpose(bank[:, P * i:P * i + P], xn[:, i, P * k:P * k + P], ident[:, :])
                    ins.then_inc(pj_ready, 1)
                g = GI[("h1T", KD - 1)]
                pe.wait_ge(pj_free[g % 2], g // 2 + 1)
                pe.wait_ge(pj_free[1 - g % 2], (g - 1) // 2 + 1)

                def token_group(name, i, n, w):
                    arrived(pe, n)
                    bank = take(name, i)
                    wv = slot(n, 8, w)
                    for k in range(KD):
                        ins = te.matmul(bank[:, 0:w], hT[:, k, P * i:P * i + P], wv[:, k, :], start=(k == 0), stop=(k == KD - 1))
                    ins.then_inc(pj_ready, 1)

                def feature_group(name, m, n, rhs, kn, w):
                    arrived(pe, n)
                    bank = take(name, m)
                    wv = slot(n, kn, w)
                    c0 = P * (m % (w // P))
                    for k in range(kn):
                        ins = te.matmul(bank[:, :], wv[:, k, c0:c0 + P], rhs[:, k, :], start=(k == 0), stop=(k == kn - 1))
                    ins.then_inc(pj_ready, 1)

                for i in range(NT):
                    token_group("q", i, IT_Q, 512)
                    token_group("kv", i, IT_KV, 256)
                bank = take("gates")
                for k in range(KD):
                    ins = te.matmul(bank[0:36, :], wg36[:, k, :], hT[:, k, :], start=(k == 0), stop=(k == KD - 1))
                ins.then_inc(pj_ready, 1)

                def qk_transposes(i):
                    pe.wait_ge(qk_ready, i + 1)
                    for name, c0, n in (("qT", 0, 4), ("kT", 4, 2)):
                        bank = take(name, i)
                        for m in range(n):
                            ins = te.transpose(bank[:, P * m:P * m + P], qk_rows[:, i, P * (c0 + m):P * (c0 + m) + P], ident[:, :])
                        ins.then_inc(pj_ready, 1)

                def att_scores(u):
                    n, g = u // HKV, u % HKV
                    if u == 0:
                        pe.wait_ge(bc_read, 12)
                    gi = GI[("kT", n)]
                    pe.wait_ge(pj_free[gi % 2], gi // 2 + 1)
                    pe.wait_ge(pj_free[(gi - 1) % 2], (gi - 1) // 2 + 1)
                    if u >= 1:
                        pe.wait_ge(s_read, u)
                    for h in range(4):
                        hq = 4 * g + h
                        r = 64 * (hq % 2)
                        q = qkT[r:r + 64, hq // 2, P * n:P * n + P]
                        bank = att_s[h % 2]
                        o = 256 * (h // 2)
                        if n:
                            ins = te.matmul(bank[:, o:o + 256], q, qkT[r:r + 64, 4 + g, P * (n - 1):P * (n + 1)], start=True, stop=True)
                        else:
                            ins = te.matmul(bank[:, o + P:o + 256], q, qkT[r:r + 64, 4 + g, 0:P], start=True, stop=True)
                    ins.then_inc(s_ready, 1)

                def att_ptrans(u):
                    n = u // HKV
                    pe.wait_ge(p_norm, u + 1)
                    if u >= 1:
                        pe.wait_ge(pt_evac, 2 * u)
                    for kb in range(0 if n else 1, 2):
                        for h in range(4):
                            ins = te.transpose(att_t[kb][:, P * h:P * h + P], prob[:, u % 2, h, P * kb:P * kb + P], ident[:, :])
                    ins.then_inc(pt_ready, 1)

                def att_out(u):
                    n, g = u // HKV, u % HKV
                    pe.wait_ge(pt_evac, 2 * (u + 1))
                    if u >= 1:
                        pe.wait_ge(o_evac, u)
                    for kb in range(0 if n else 1, 2):
                        ins = te.matmul(ps[6][0:64, :], v_rows[:, n - 1 + kb, 64 * g:64 * g + 64], pT[:, u % 2, kb, :],
                                        start=(kb == 0 or n == 0), stop=(kb == 1))
                    ins.then_inc(o_ready, 1)

                for s in range(16):
                    if s < 8:
                        feature_group("mqk", s, IT_MQK + s // 4, hT, 8, 512)
                    elif s < 12:
                        token_group("mv", s - 8, IT_MV, 512)
                    else:
                        token_group("mo", s - 12, IT_MO, 512)
                    if 1 <= s <= NT:
                        qk_transposes(s - 1)
                    if 4 <= s < 12:
                        att_scores(s - 4)
                    if 5 <= s < 13:
                        att_ptrans(s - 5)
                    if 6 <= s < 14:
                        att_out(s - 6)
                pe.wait_ge(rows_ready, 2)
                bank = take("rT")
                for i in range(NT):
                    ins = te.transpose(bank[:, P * i:P * i + P], rstack[:, P * i:P * i + P], ident[:, :])
                ins.then_inc(pj_ready, 1)
                for h in range(HM):
                    bank = take("mubc", h)
                    te.matmul(bank[:, :], ident[0:HM, h:h + 1].to_broadcast([HM, P]), rows4[:, 5, :], start=True, stop=True).then_inc(pj_ready, 1)
                bank = take("dec")
                for h in range(HM):
                    ins = te.matmul(bank[:, 4 * h:4 * h + 4], ident[0:HM, h:h + 1].to_broadcast([HM, P]), g16[:, 24:28], start=True, stop=True)
                ins.then_inc(pj_ready, 1)
                pe.wait_ge(pj_free[GI[("mo", NT - 1)] % 2], GI[("mo", NT - 1)] // 2 + 1)
                pe.wait_ge(conv_t, 16)
                pe.wait_ge(pt_evac, 16)
                pe.wait_ge(o_evac, 8)

                def m_a(u):
                    c_, h = u // HM, u % HM
                    b = 2 + u % 2
                    if u >= 2:
                        pe.wait_ge(ma_act, u - 1)
                        pe.wait_ge(w_ready, u - 1)
                    kf = mqkT[:, HM + h, P * c_:P * c_ + P]
                    te.transpose(ps[b][:, 0:P], kf, ident[:, :])
                    te.matmul(ps[b][:, P:2 * P], kf, mqkT[:, h, P * c_:P * c_ + P], start=True, stop=True).then_inc(ma_ready, 1)

                def m_b(u):
                    c_, h = u // HM, u % HM
                    pe.wait_ge(w_ready, u + 1)
                    pe.wait_ge(ma_act, u + 1)
                    if u >= 2:
                        pe.wait_ge(c_upd, u - 1)
                    ins = te.matmul(ps[4 + u % 2][:, 0:DM + 1], wS[:, u % 2, :], vaug[:, c_, h, :], start=True, stop=True)
                    if c_ > 0:
                        pe.wait_ge(c_upd, u - HM + 1)
                        ins = te.matmul(ps[4 + u % 2][:, 256:256 + DM + 1], mqkT[:, h, P * c_:P * c_ + P], cst[:, h, :], start=True, stop=True)
                    if c_ < NT - 1:
                        ins = te.matmul(ps[6 + u % 2][:, 0:DM + 1], ke[:, u % 2, :], vaug[:, c_, h, :], start=True, stop=True)
                    ins.then_inc(mb_ready, 1)

                for j in range(8):
                    feature_group("ga", j, IT_GA + j // 4, hT, 8, 512)
                    for u in (2 * j, 2 * j + 1):
                        m_a(u)
                        if u >= 1:
                            m_b(u - 1)
                    feature_group("ya", j, IT_YA, attn_o, 4, D)
                m_b(15)
                feature_group("gb", 0, IT_GB, hT, 8, 512)
                feature_group("gb", 1, IT_GB, hT, 8, 512)
                for i in range(NT):
                    pe.wait_ge(hm_ready, i + 1)
                    bank = take("hmT", i)
                    for h in range(HM):
                        ins = te.transpose(bank[:, P * h:P * h + P], mo_t[:, i, P * h:P * h + P], ident[:, :])
                    ins.then_inc(pj_ready, 1)
                for j in range(8):
                    if j >= 2:
                        feature_group("gb", j, IT_GB + j // 4, hT, 8, 512)
                    if j == 0:
                        for g in (GI[("hmT", NT - 1)], GI[("hmT", NT - 2)]):
                            pe.wait_ge(pj_free[g % 2], g // 2 + 1)
                    feature_group("yb", j, IT_YB, hmT, 4, D)
                pe.wait_ge(merged_ready, 8)
                for i in range(NT):
                    for h in range(2):
                        arrived(pe, IT_WO)
                        arrived(pe, IT_WO + 1)
                        bank = take("wo", 2 * i + h)
                        for k in range(KD):
                            ins = te.matmul(bank[:, :], merged[:, k, P * i:P * i + P],
                                            slot(IT_WO + k // 4, 4, D)[:, k % 4, 512 * h:512 * h + 512], start=(k == 0), stop=(k == KD - 1))
                        ins.then_inc(pj_ready, 1)

                pe.wait_ge(xn_ready, 2 * NT)
                for k in range(KD):
                    bank = take("h2T", k)
                    for i in range(NT):
                        ins = te.transpose(bank[:, P * i:P * i + P], xn[:, i, P * k:P * k + P], ident[:, :])
                    ins.then_inc(pj_ready, 1)
                g = GI[("h2T", KD - 1)]
                pe.wait_ge(pj_free[g % 2], g // 2 + 1)
                pe.wait_ge(pj_free[1 - g % 2], (g - 1) // 2 + 1)
                bank = take("rl")
                for k in range(KD):
                    g = k % 4
                    ins = te.matmul(bank[32 * g:32 * g + 32, :], rwz[:, k, :], hT[:, k, :], start=(k < 4), stop=(k >= 4))
                ins.then_inc(pj_ready, 1)
                g = GI[("rl", 0)]
                pe.wait_ge(pj_free[g % 2], g // 2 + 1)
                bank = take("lg")
                for i in range(NT):
                    ins = te.matmul(bank[:, E * i:E * i + E], small[:, P * i:P * i + P], fold[:, :], start=True, stop=True)
                ins.then_inc(pj_ready, 1)
                pe.wait_ge(routed, 1)
                bank = take("rank")
                for i in range(NT):
                    for j in range(i):
                        te.matmul(bank[:, E * i:E * i + E], onesb[:, :], Mb[:, j, :], start=(j == 0), stop=False)
                    te.matmul(bank[:, E * i:E * i + E], triu[:, :], Mb[:, i, :], start=(i == 0), stop=True)
                for j in range(NT):
                    ins = te.matmul(bank[:, E * NT:E * NT + E], onesb[:, :], Mb[:, j, :], start=(j == 0), stop=(j == NT - 1))
                ins.then_inc(pj_ready, 1)

                pe.wait_ge(tables, 1)
                nb = te.value_load(tabs[0:1, 47:48], min_val=E, max_val=MAXB)
                nb1 = te.value_load(tabs[0:1, 48:49], min_val=E - 1, max_val=MAXB - 1)

                def x_transposes():
                    for k in range(KD):
                        ins = te.transpose(ps[(2, 6)[k % 2]][:, MB * k:MB * k + MB], xg[:, P * k:P * k + P], ident[0:MB, 0:MB])
                    ins.then_inc(xt_ready, 1)

                def gate_up(p):
                    for k in range(KD):
                        for part in range(2):
                            w = ring[:, 3 * p + part, :].rearrange("p (k n) -> p k n", k=KD)
                            ins = te.matmul(ps[3][64 * part:64 * part + 64, :], xT[:, k, :], w[:, k, :], start=(k == 0), stop=(k == KD - 1))
                    ins.then_inc(gu_ready, 1)

                def h_transposes(b):
                    wait_reg(pe, hx_ready, b + 1)
                    for k in range(FC):
                        ins = te.transpose(ps[4][:, MB * k:MB * k + MB], hx[:, P * k:P * k + P], ident[0:MB, 0:MB])
                    ins.then_inc(ht_ready, 1)

                def down(p):
                    w = ring[:, 3 * p + 2, :].rearrange("p (k n) -> p k n", k=FC)
                    for k in range(FC):
                        for half in range(2):
                            ins = te.matmul(ps[5][64 * half:64 * half + 64, :], hxT[:, k, :], w[:, k, 512 * half:512 * half + 512],
                                            start=(k == 0), stop=(k == FC - 1))
                    ins.then_inc(y_ready, 1)

                pe.wait_ge(xg_in, 16)
                x_transposes()
                pe.wait_ge(xt_evac_a, 1)
                pe.wait_ge(xt_evac_d, 1)
                pe.wait_ge(w_expert[0], 48)
                gate_up(0)
                pe.wait_ge(xg_in, 32)
                x_transposes()
                h_transposes(0)
                with pe.Fori(0, nb1) as b:
                    e1 = te.value_load(tabs[0:1, bass.ds(b + 1, 1)], min_val=0, max_val=E - 1)
                    e0 = te.value_load(tabs[0:1, bass.ds(b, 1)], min_val=0, max_val=E - 1)
                    pe.wait_ge(xt_evac_a, b + 2)
                    pe.wait_ge(xt_evac_d, b + 2)
                    with pe.If(e1 % 2 == 0):
                        pe.wait_ge(w_expert[0], (e1 // 2) * 48 + 48)
                        gate_up(0)
                    with pe.Else():
                        pe.wait_ge(w_expert[1], (e1 // 2) * 48 + 48)
                        gate_up(1)
                    wait_reg(pe, xg_in, (b + 3) * 16)
                    x_transposes()
                    pe.wait_ge(ht_evac, b + 1)
                    pe.wait_ge(y_taken, b + 1)
                    with pe.If(e0 % 2 == 0):
                        down(0)
                    with pe.Else():
                        down(1)
                    h_transposes(b + 1)
                pe.wait_ge(ht_evac, nb)
                pe.wait_ge(y_taken, nb)
                down(1)
                layer_end(pe, l, share(3))

        @block.vector
        def _(dve):
            ve = nc.vector
            cstep = [0]

            def clink(ins):
                cstep[0] += 1
                ins.then_inc(dve_step, 1)
                dve.wait_ge(dve_step, cstep[0])

            dve.wait_ge(const_in, 16 * 4)
            clink(ve.tensor_copy(rt[:, 4:8], rt[:, 0:4].bitcast(I32)))
            inv = np.power(np.float32(THETA), -(np.arange(0, ROPE, 2, dtype=np.float32) / np.float32(ROPE)), dtype=np.float32)
            for f in range(HALF):
                ins = ve.tensor_scalar(rt[:, 64:96].rearrange("p (i f) -> p i f", f=HALF)[:, :, f], rt[:, 4:8], float(inv[f]), None, ALU.mult)
            clink(ins)
            parts, rest = [], 2.0 * np.pi
            for bits in (8, 8, 8):
                e = np.floor(np.log2(rest)) - (bits - 1)
                parts.append(float(np.floor(rest / 2.0 ** e) * 2.0 ** e))
                rest -= parts[-1]
            parts.append(float(rest))
            BIG = 12582912.0
            clink(ve.tensor_copy(rt[:, 96:128], rt[:, 64:96]))
            for off, shift, last in ((64, 0.0, 0.0), (96, 0.25, float(np.pi / 2))):
                a, k = rt[:, off:off + 32], rt[:, 128:160]
                clink(ve.tensor_scalar(k, a, float(1.0 / (2.0 * np.pi)), shift, ALU.mult, ALU.add))
                clink(ve.tensor_scalar(k, k, BIG, None, ALU.add))
                clink(ve.tensor_scalar(k, k, -BIG, None, ALU.add))
                for part in parts:
                    clink(ve.scalar_tensor_tensor(a, k, -part, a, ALU.mult, ALU.add))
                clink(ve.tensor_scalar(a, a, last, None, ALU.add))
                clink(ve.tensor_scalar(a, a, 3.1415925, -3.1415925, ALU.min, ALU.max))
            ve.sem_inc(dve_const, 1)
            dve.wait_ge(pool_const, 2)
            clink(ve.tensor_tensor(fold[:, :], ident[:, 0:E], ident[:, 32:32 + E], ALU.add))
            clink(ve.tensor_tensor(fold[:, :], fold[:, :], ident[:, 64:64 + E], ALU.add))
            clink(ve.tensor_tensor(fold[:, :], fold[:, :], ident[:, 96:96 + E], ALU.add))
            ve.memset(g16[:, 0:1], 0.0)
            clink(ve.memset(vaug[:, :, :, DM:DM + 1], 1.0))
            ve.sem_inc(dve_const, 2)
            dve.wait_ge(act_const, 3)
            ve.sem_clear(dve_step)

            with dve.Fori(0, DEPTH) as l:
                n = [0]
                asks = [0]

                def link(ins):
                    n[0] += 1
                    ins.then_inc(dve_step, 1)
                    dve.wait_ge(dve_step, n[0])

                def ask_power():
                    asks[0] += 1
                    ve.sem_inc(pow_ask, 1)
                    dve.wait_ge(pow_done, asks[0])

                dve.wait_ge(param_cols, 1)
                link(ve.tensor_copy(pc[:, :], ps[4][:, 0:P]))
                dve.wait_ge(ffn_sq, NT)
                link(ve.tensor_scalar(ss[:, 0:NT], ss[:, 0:NT], 1.0 / D, EPS, ALU.mult, ALU.add))
                ask_power()
                for i in range(NT):
                    ve.tensor_scalar(xn[:, i, :], xs[:, i, :], rs[:, i:i + 1], None, ALU.mult).then_inc(xn_ready, 1)
                for j in range(12):
                    dve.wait_ge(bc_ready, j + 1)
                    bank = ps[2 + j % 2]
                    if j in (4, 5):
                        h = j - 4
                        link(ve.tensor_tensor(g1bc[:, 512 * h:512 * h + 512], bank[:, :], g1bc[:, 512 * h:512 * h + 512], ALU.add))
                        ve.sem_inc(bc_read, 1)
                    elif j in (10, 11):
                        dve.wait_ge(y_out, 32)
                        r = 64 * (j - 10)
                        link(ve.tensor_tensor(g2bc[r:r + 64, :], bank[r:r + 64, :], g2bc[r:r + 64, :], ALU.add))
                        ve.sem_inc(bc_read, 1)
                    else:
                        link(ve.tensor_tensor(regP[:, 0:512].rearrange("p (q m) -> p q m", q=4), bank[:, :].rearrange("p (q m) -> p q m", q=4),
                                              ident[:, :].unsqueeze(1).to_broadcast([P, 4, P]), ALU.mult))
                        ve.sem_inc(bc_read, 1)
                        link(ve.tensor_reduce(modc[:, 4 * j:4 * j + 4], regP[:, 0:512].rearrange("p (q m) -> p q m", q=4), AX.X, ALU.add))
                    if j == 3:
                        link(ve.tensor_tensor(modc[:, 0:16], modc[:, 0:16], pc[:, 60:76], ALU.add))
                        link(ve.scalar_tensor_tensor(A1[:, :], modc[:, 8:16], 1.0, pc[:, 0:8], ALU.add, ALU.mult))
                        ve.sem_inc(mod_ready, 1)
                ve.memset(conv_u[:, :, 0:3], 0.0)
                link(ve.tensor_tensor(modc[:, 24:40], modc[:, 24:40], pc[:, 84:100], ALU.add))
                link(ve.scalar_tensor_tensor(A2[:, :], modc[:, 32:40], 1.0, pc[:, 8:16], ALU.add, ALU.mult))
                ve.tensor_scalar(wmc[:, :], pc[:, 56:60], 0.5, None, ALU.mult)
                link(ve.tensor_scalar(wqk[:, 0, :], wqk[:, 0, :], HD ** -0.5, None, ALU.mult))
                for k in range(0, KD, 2):
                    bank, free = ready(dve, "h1T", k)
                    ve.tensor_scalar(hT[:, k, :], bank[:, :], A1[:, k:k + 1], modc[:, k:k + 1], ALU.mult, ALU.add).then_inc(free, 1)

                nh = HQ + HKV
                for i in range(NT):
                    g = GI[("kv", i)]
                    dve.wait_ge(pj_free[g % 2], g // 2 + 1)
                    dve.wait_ge(pj_free[1 - g % 2], (g - 1) // 2 + 1)
                    qk = qk_rows[:, i, 0:nh * HD].rearrange("p (h n) -> p h n", n=HD)
                    link(ve.tensor_reduce(ssq[:, 0:nh], small[:, 0:nh * HD].rearrange("p (h n) -> p h n", n=HD), AX.X, ALU.add))
                    ve.sem_inc(qk_sq, 1)
                    link(ve.tensor_scalar(ssq[:, 0:nh], ssq[:, 0:nh], 1.0 / HD, EPS, ALU.mult, ALU.add))
                    ask_power()
                    link(ve.tensor_tensor(qk, qk, rsq[:, 0:nh].unsqueeze(2).to_broadcast([P, nh, HD]), ALU.mult))
                    ve.tensor_tensor(qk[:, 0:HQ], qk[:, 0:HQ], wqk[:, 0:1, :].to_broadcast([P, HQ, HD]), ALU.mult)
                    link(ve.tensor_tensor(qk[:, HQ:nh], qk[:, HQ:nh], wqk[:, 1:2, :].to_broadcast([P, HKV, HD]), ALU.mult))
                    t1, t2 = qk[:, :, 0:HALF], qk[:, :, HALF:ROPE]
                    co = cosr[:, i, :].unsqueeze(1).to_broadcast([P, nh, HALF])
                    si = sinr[:, i, :].unsqueeze(1).to_broadcast([P, nh, HALF])
                    r4 = rt[:, 0:4 * nh * HALF].rearrange("p (a h f) -> p a h f", a=4, h=nh)
                    ve.tensor_tensor(r4[:, 0], t1, co, ALU.mult)
                    ve.tensor_tensor(r4[:, 1], t2, si, ALU.mult)
                    ve.tensor_tensor(r4[:, 2], t2, co, ALU.mult)
                    link(ve.tensor_tensor(r4[:, 3], t1, si, ALU.mult))
                    ve.tensor_tensor(t1, r4[:, 0], r4[:, 1], ALU.subtract)
                    link(ve.tensor_tensor(t2, r4[:, 2], r4[:, 3], ALU.add))
                    link(ve.tensor_copy(qk_rows[:, i, 640:768].rearrange("p (a n) -> p a n", a=2), qk_rows[:, i, 576:640].unsqueeze(1).to_broadcast([P, 2, HD])))
                    ve.tensor_copy(qk_rows[:, i, 576:640], qk_rows[:, i, 512:576]).then_inc(qk_ready, 1)

                bank, free = ready(dve, "gates")
                dve.wait_ge(gates_f, 1)
                link(ve.tensor_scalar(rows4[:, 1, :], bank[32:36, :], gbias[32:36, :], None, ALU.add))
                ve.sem_inc(free, 1)
                link(ve.scalar_tensor_tensor(rows4[:, 2, :], rows4[:, 1, :], -1.0, rows4[:, 1, :], ALU.mult, ALU.max))
                ve.sem_inc(gates_f, 1)

                def conv(m):
                    dve.wait_ge(conv_in, m + 1)
                    u = conv_u[:, m % 2, :]
                    z = mqkT[:, m, :]
                    link(ve.tensor_scalar(z, u[:, 0:S], pc[:, 16 + m:17 + m], pc[:, 48 + m:49 + m], ALU.mult, ALU.add))
                    for t in range(1, 4):
                        link(ve.scalar_tensor_tensor(z, u[:, t:t + S], pc[:, 16 + 8 * t + m:17 + 8 * t + m], z, ALU.mult, ALU.add))
                    ve.sem_inc(conv_z, 1)

                def conv_silu(m):
                    dve.wait_ge(conv_t, 2 * m + 1)
                    ve.scalar_tensor_tensor(mqkT[:, m, :], small[:, 0:S], 1.0, mqkT[:, m, :], ALU.add, ALU.mult).then_inc(conv_t, 1)

                def att_max(u):
                    nb_, g = u // HKV, u % HKV
                    lo = 0 if nb_ else P
                    dve.wait_ge(s_ready, u + 1)
                    if u >= 2:
                        dve.wait_ge(pt_ready, u - 1)
                    a = att[:, u % 2, :]
                    for h in range(4):
                        ins = ve.tensor_tensor_reduce(prob[:, u % 2, h, lo:256], att_s[h % 2][:, 256 * (h // 2) + lo:256 * (h // 2) + 256],
                                                      mask[:, lo:256], 1.0, sinkb[:, 4 * g + h:4 * g + h + 1], ALU.add, ALU.max, a[:, h:h + 1])
                    link(ins)
                    ve.sem_inc(s_read, 1)
                    ve.tensor_scalar(a[:, 4:8], a[:, 0:4], -1.0, None, ALU.mult)
                    link(ve.tensor_tensor(a[:, 16:20], sinkb[:, 4 * g:4 * g + 4], a[:, 0:4], ALU.subtract))
                    ve.sem_inc(m_ready, 1)

                def att_norm(u):
                    nb_ = u // HKV
                    lo = 0 if nb_ else P
                    dve.wait_ge(e_ready, u + 1)
                    a = att[:, u % 2, :]
                    link(ve.tensor_tensor(a[:, 8:12], a[:, 8:12], a[:, 12:16], ALU.add))
                    link(ve.reciprocal(a[:, 8:12], a[:, 8:12]))
                    for h in range(4):
                        ins = ve.tensor_scalar(prob[:, u % 2, h, lo:256], prob[:, u % 2, h, lo:256], a[:, 8 + h:9 + h], None, ALU.mult)
                    ins.then_inc(p_norm, 1)

                def att_pt(u):
                    nb_ = u // HKV
                    if nb_:
                        dve.wait_ge(pt_ready, u + 1)
                        if u >= 2:
                            dve.wait_ge(o_ready, u - 1)
                        ve.tensor_copy(pT[:, u % 2, 0, :], att_t[0][:, :]).then_inc(pt_evac, 1)
                    else:
                        ve.sem_inc(pt_evac, 1)

                def gate_rows():
                    lf, b_, mu, nmu = rows4[:, 1, :], rows4[:, 3, :], rows4[:, 4, :], rows4[:, 5, :]
                    dve.wait_ge(gates_f, 4)
                    dve.wait_ge(stack_zero, 1)
                    link(ve.scalar_tensor_tensor(lf, rows4[:, 1, :], 0.0, rows4[:, 2, :], ALU.min, ALU.subtract))
                    ch = [slice(P * i, P * i + P) for i in range(NT)]
                    for t in ch:
                        ins = ve.tensor_tensor_scan(b_[:, t], ones[0:HM, :], lf[:, t], 0.0, ALU.mult, ALU.add)
                    link(ins)
                    a_ = rstack[0:4, :]
                    link(ve.tensor_tensor(a_, rows4[:, 0, :], b_, ALU.subtract))
                    for t in ch:
                        ins = ve.tensor_tensor_scan(mu[:, t], a_[:, t], a_[:, t], NEG, ALU.max, ALU.max)
                    link(ins)
                    last = lambda r: r.rearrange("p (i t) -> p i t", t=P)[:, :, P - 1]
                    bl = g16[:, 8:12]
                    ve.tensor_copy(bl, last(b_))
                    link(ve.tensor_copy(g16[:, 12:16], last(mu)))
                    link(ve.tensor_tensor_scan(g16[:, 1:5], g16[:, 12:16], bl, 0.0, ALU.max, ALU.add))
                    mprev, mnew = g16[:, 0:4], g16[:, 1:5]
                    mp = mprev.unsqueeze(2).to_broadcast([HM, 4, P])
                    v3 = lambda r: r.rearrange("p (i t) -> p i t", t=P)
                    link(ve.tensor_tensor(v3(mu), v3(mu), mp, ALU.max))
                    ve.tensor_scalar(nmu, mu, -1.0, None, ALU.mult)
                    link(ve.tensor_tensor(v3(rstack[32:36, :]), v3(mu), mp, ALU.subtract))
                    link(ve.tensor_scalar(rstack[32:36, :], rstack[32:36, :], -1.0, None, ALU.mult))
                    link(ve.tensor_tensor(g16[:, 16:20], bl, mnew, ALU.subtract))
                    link(ve.tensor_tensor(v3(rstack[64:68, :]), v3(a_), g16[:, 16:20].unsqueeze(2).to_broadcast([HM, 4, P]), ALU.add))
                    link(ve.tensor_tensor(rstack[96:100, :], b_, mu, ALU.add))
                    link(ve.tensor_scalar(rstack[96:100, :], rstack[96:100, :], -1.0, None, ALU.mult))
                    link(ve.tensor_tensor(g16[:, 20:24], g16[:, 16:20], mprev, ALU.add))
                    ve.sem_inc(rows_ready, 1)

                for s in range(16):
                    if s < 8:
                        conv(s)
                    if 1 <= s <= 8:
                        conv_silu(s - 1)
                    if 4 <= s < 12:
                        att_max(s - 4)
                        att_norm(s - 4)
                    if 5 <= s < 13:
                        att_pt(s - 5)
                    if s == 6:
                        gate_rows()
                for h in range(HM):
                    bank, free = ready(dve, "mubc", h)
                    link(ve.tensor_tensor(argm[:, h, :].rearrange("p (i t) -> p i t", t=P), bank[:, :].rearrange("p (i t) -> p i t", t=P),
                                          maskT[:, :].unsqueeze(1).to_broadcast([P, NT, P]), ALU.add))
                    ve.sem_inc(free, 1)
                bank, free = ready(dve, "dec")
                link(ve.tensor_copy(decb[:, :, :].rearrange("p h c -> p (h c)"), bank[:, 0:16]))
                ve.sem_inc(free, 1)

                def m_w(u):
                    dve.wait_ge(ma_ready, u + 1)
                    dve.wait_ge(ma_act, u + 1)
                    if u >= 2:
                        dve.wait_ge(mb_ready, u - 1)
                    ve.scalar_tensor_tensor(wS[:, u % 2, :], ps[2 + u % 2][:, P:2 * P], KSCALE, ex[:, u % 2, :], ALU.mult, ALU.mult).then_inc(w_ready, 1)

                def m_state(u):
                    c_, h = u // HM, u % HM
                    dve.wait_ge(mb_ready, u + 1)
                    if c_ == 0:
                        ins = ve.tensor_copy(num[:, h, :], ps[4 + u % 2][:, 0:DM + 1])
                    else:
                        dve.wait_ge(ic_ready, u - HM + 1)
                        ins = ve.tensor_tensor(num[:, h, :], ps[4 + u % 2][:, 0:DM + 1], icb[:, u % 2, :], ALU.add)
                    link(ins)
                    kv = ps[6 + u % 2][:, 0:DM + 1]
                    if c_ == 0:
                        link(ve.tensor_scalar(cst[:, h, :], kv, KSCALE, None, ALU.mult))
                    elif c_ < NT - 1:
                        link(ve.tensor_scalar(cst[:, h, :], cst[:, h, :], decb[:, h, c_:c_ + 1], None, ALU.mult))
                        link(ve.scalar_tensor_tensor(cst[:, h, :], kv, KSCALE, cst[:, h, :], ALU.mult, ALU.add))
                    ve.sem_inc(c_upd, 1)

                def m_finish(c_):
                    den = num[:, :, DM]
                    link(ve.scalar_tensor_tensor(fin[:, 0:4], den, -1.0, den, ALU.mult, ALU.max))
                    link(ve.tensor_tensor(fin[:, 0:4], fin[:, 0:4], colR[:, c_, 3, :], ALU.max))
                    link(ve.reciprocal(fin[:, 0:4], fin[:, 0:4]))
                    hv = num[:, :, 0:DM]
                    link(ve.tensor_tensor(hv, hv, fin[:, 0:4].unsqueeze(2).to_broadcast([P, HM, DM]), ALU.mult))
                    for h in range(HM):
                        ins = ve.tensor_tensor_reduce(sqs, num[:, h, 0:DM], num[:, h, 0:DM], 1.0, 0.0, ALU.mult, ALU.add, fin[:, 4 + h:5 + h])
                        link(ins)
                    link(ve.tensor_scalar(fin[:, 4:8], fin[:, 4:8], 1.0 / DM, EPS, ALU.mult, ALU.add))
                    ask_power()
                    mo = mo_t[:, c_, :].rearrange("p (h n) -> p h n", h=HM)
                    link(ve.tensor_scalar(mo, mo, 1.0, None, ALU.add))
                    link(ve.tensor_tensor(mo, mo, hv, ALU.mult))
                    ve.tensor_tensor(mo, mo, fin[:, 8:12].unsqueeze(2).to_broadcast([P, HM, DM]), ALU.mult).then_inc(hm_ready, 1)

                ve.memset(fin[:, :], 0.0)
                for j in range(8):
                    for u in (2 * j, 2 * j + 1):
                        m_w(u)
                        if u >= 1:
                            m_state(u - 1)
                            if u % HM == 0:
                                m_finish(u // HM - 1)
                    bank, free = ready(dve, "ya", j)
                    g = GI[("ga", j)]
                    dve.wait_ge(pj_free[g % 2], g // 2 + 1)
                    ve.scalar_tensor_tensor(merged[:, j, :], merged[:, j, :], 1.0, bank[:, :], ALU.add, ALU.mult).then_inc(free, 1)
                m_state(15)
                m_finish(NT - 1)
                for i in range(NT):
                    bank, free = ready(dve, "hmT", i)
                    ve.tensor_tensor(hmT[:, :, P * i:P * i + P], bank[:, :].rearrange("p (h t) -> p h t", h=HM),
                                     wmc[:, :].unsqueeze(2).to_broadcast([P, HM, P]), ALU.mult).then_inc(free, 1)
                for j in range(8):
                    bank, free = ready(dve, "yb", j)
                    g = GI[("gb", j)]
                    dve.wait_ge(pj_free[g % 2], g // 2 + 1)
                    link(ve.scalar_tensor_tensor(tb[:, j % 2, :], tb[:, j % 2, :], 1.0, bank[:, :], ALU.add, ALU.mult))
                    ve.sem_inc(free, 1)
                    ve.sem_inc(tb_sum, 1)
                for i in range(NT):
                    for h in range(2):
                        bank, free = ready(dve, "wo", 2 * i + h)
                        link(ve.scalar_tensor_tensor(regP[:, 0:512], bank[:, :], 0.5, g1bc[:, 512 * h:512 * h + 512], ALU.mult, ALU.mult))
                        ve.sem_inc(free, 1)
                        link(ve.tensor_tensor(xs[:, i, 512 * h:512 * h + 512], xs[:, i, 512 * h:512 * h + 512], regP[:, 0:512], ALU.add))
                    ve.sem_inc(x_upd, 1)
                    dve.wait_ge(ffn_sq, NT + i + 1)
                    link(ve.tensor_scalar(ss[:, 4 + i:5 + i], ss[:, 4 + i:5 + i], 1.0 / D, EPS, ALU.mult, ALU.add))
                    ask_power()
                    ve.tensor_scalar(xn[:, i, :], xs[:, i, :], rs[:, 4 + i:5 + i], None, ALU.mult).then_inc(xn_ready, 1)
                for k in range(0, KD, 2):
                    bank, free = ready(dve, "h2T", k)
                    ve.tensor_scalar(hT[:, k, :], bank[:, :], A2[:, k:k + 1], modc[:, 24 + k:25 + k], ALU.mult, ALU.add).then_inc(free, 1)

                g = GI[("lg", 0)]
                dve.wait_ge(pj_free[g % 2], g // 2 + 1)
                NS = NT * E
                r = lambda a, w: rt[:, a:a + w]
                s_, sel = r(0, 64), r(64, 64)
                link(ve.tensor_scalar(s_, s_, 1.0, None, ALU.add))
                link(ve.reciprocal(s_, s_))
                link(ve.tensor_tensor(sel.rearrange("p (i e) -> p i e", e=E), s_.rearrange("p (i e) -> p i e", e=E),
                                      rbias[:, :].unsqueeze(1).to_broadcast([P, NT, E]), ALU.add))
                v4 = sel.rearrange("p (g j) -> p g j", j=EG)
                hi1, hi2, lo1, lo2 = (r(128 + 16 * q, 16) for q in range(4))
                ve.tensor_tensor(hi1, v4[:, :, 0], v4[:, :, 1], ALU.max)
                ve.tensor_tensor(lo1, v4[:, :, 0], v4[:, :, 1], ALU.min)
                ve.tensor_tensor(hi2, v4[:, :, 2], v4[:, :, 3], ALU.max)
                link(ve.tensor_tensor(lo2, v4[:, :, 2], v4[:, :, 3], ALU.min))
                m1, mn, ml = r(192, 16), r(208, 16), r(224, 16)
                ve.tensor_tensor(m1, hi1, hi2, ALU.max)
                ve.tensor_tensor(mn, hi1, hi2, ALU.min)
                link(ve.tensor_tensor(ml, lo1, lo2, ALU.max))
                link(ve.tensor_tensor(mn, mn, ml, ALU.max))
                gs = r(240, 16)
                link(ve.tensor_tensor(gs, m1, mn, ALU.add))

                def first_max(one, val, tmp, red):
                    v = val.rearrange("p (i g) -> p i g", g=4)
                    o = one.rearrange("p (i g) -> p i g", g=4)
                    t = tmp.rearrange("p (i g) -> p i g", g=4)
                    io = iog[:, :].unsqueeze(1).to_broadcast([P, NT, 4])
                    link(ve.tensor_reduce(red, v, AX.X, ALU.max))
                    link(ve.tensor_tensor(t, v, red.unsqueeze(2).to_broadcast([P, NT, 4]), ALU.is_equal))
                    link(ve.tensor_tensor(t, t, io, ALU.mult))
                    link(ve.tensor_reduce(red, t, AX.X, ALU.min))
                    link(ve.tensor_tensor(o, io, red.unsqueeze(2).to_broadcast([P, NT, 4]), ALU.is_equal))

                og, tmp, red, ing, o1, o2 = r(256, 16), r(272, 16), r(288, 4), r(292, 16), r(308, 16), r(324, 16)
                first_max(og, gs, tmp, red)
                big = r(340, 64)
                link(ve.tensor_tensor(big.rearrange("p (g j) -> p g j", j=EG), v4, og.unsqueeze(2).to_broadcast([P, NT * NG, EG]), ALU.mult))
                link(ve.tensor_reduce(ing.rearrange("p (i j) -> p i j", j=EG), big.rearrange("p (i g j) -> p i j g", g=NG, j=EG), AX.X, ALU.add))
                first_max(o1, ing, tmp, red)
                link(ve.scalar_tensor_tensor(ing, o1, NEG, ing, ALU.mult, ALU.add))
                first_max(o2, ing, tmp, red)
                E1, E2 = r(404, 64), r(468, 64)
                for Ek, ok in ((E1, o1), (E2, o2)):
                    for i in range(NT):
                        ins = ve.tensor_tensor(Ek[:, E * i:E * i + E].rearrange("p (g j) -> p g j", j=EG),
                                               og[:, 4 * i:4 * i + 4].unsqueeze(2).to_broadcast([P, NG, EG]),
                                               ok[:, 4 * i:4 * i + 4].unsqueeze(1).to_broadcast([P, NG, EG]), ALU.mult)
                link(ins)
                link(ve.tensor_tensor(Mb[:, :, :].rearrange("p i e -> p (i e)"), E1, E2, ALU.add))
                for k, Ek in enumerate((E1, E2)):
                    link(ve.tensor_tensor(big, s_, Ek, ALU.mult))
                    link(ve.tensor_reduce(wsel[:, k, :], big.rearrange("p (i e) -> p i e", e=E), AX.X, ALU.add))
                link(ve.tensor_tensor(red, wsel[:, 0, :], wsel[:, 1, :], ALU.add))
                link(ve.reciprocal(red, red))
                link(ve.tensor_tensor(wsel[:, :, :], wsel[:, :, :], red.unsqueeze(1).to_broadcast([P, 2, NT]), ALU.mult))
                ve.sem_inc(routed, 1)
                bank, free = ready(dve, "rank")
                cmp, nbk, cum, base = r(532, 112), r(644, 16), r(660, 16), r(676, 16)
                cnt = r(692, 80)
                link(ve.tensor_copy(cnt, bank[:, 0:80]))
                link(ve.tensor_tensor(cmp.rearrange("p (e k) -> p e k", k=7), cnt[:, 64:80].unsqueeze(2).to_broadcast([P, E, 7]),
                                      thr[:, :].unsqueeze(1).to_broadcast([P, E, 7]), ALU.is_gt))
                link(ve.tensor_reduce(nbk, cmp.rearrange("p (e k) -> p e k", k=7), AX.X, ALU.add))
                link(ve.tensor_scalar(nbk, nbk, 1.0, None, ALU.add))
                link(ve.tensor_tensor_scan(cum, ones[:, 0:E], nbk, 0.0, ALU.mult, ALU.add))
                link(ve.tensor_tensor(base, cum, nbk, ALU.subtract))
                link(ve.tensor_scalar(base, base, float(MB), None, ALU.mult))
                link(ve.tensor_tensor(cnt[:, 0:64].rearrange("p (i e) -> p i e", e=E), cnt[:, 0:64].rearrange("p (i e) -> p i e", e=E),
                                      base.unsqueeze(1).to_broadcast([P, NT, E]), ALU.add))
                for k, Ek in enumerate((E1, E2)):
                    link(ve.tensor_tensor(big, cnt[:, 0:64], Ek, ALU.mult))
                    link(ve.tensor_reduce(red, big.rearrange("p (i e) -> p i e", e=E), AX.X, ALU.add))
                    link(ve.tensor_copy(slot_u[:, k, :], red))
                ve.sem_inc(routed, 1)
                tb32 = rt[0:1, 0:512]
                link(ve.tensor_tensor(tb32.rearrange("p (b e) -> p b e", e=E), cum[0:1, :].unsqueeze(1).to_broadcast([1, 32, E]),
                                      ioe[:, :].unsqueeze(2).to_broadcast([1, 32, E]), ALU.is_le))
                link(ve.tensor_reduce(rt[0:1, 512:544], tb32.rearrange("p (b e) -> p b e", e=E), AX.X, ALU.add))
                ve.tensor_copy(tabs[0:1, 0:32], rt[0:1, 512:544])
                ve.tensor_copy(tabs[0:1, 32:48], cum[0:1, :])
                link(ve.tensor_scalar(tabs[0:1, 48:49], cum[0:1, E - 1:E], 1.0, None, ALU.subtract))
                ve.sem_inc(tables, 1)

                nb = ve.value_load(tabs[0:1, 47:48], min_val=E, max_val=MAXB)
                nb1 = ve.value_load(tabs[0:1, 48:49], min_val=E - 1, max_val=MAXB - 1)

                def xt_dve():
                    for k in range(1, KD, 2):
                        last = ve.tensor_scalar(xT[:, k, :], ps[6][:, MB * k:MB * k + MB], A2[:, k:k + 1], modc[:, 24 + k:25 + k], ALU.mult, ALU.add)
                    last.then_inc(xt_evac_d, 1)

                def y_row():
                    ve.tensor_tensor(yb, ps[5][:, :], g2bc[:, :], ALU.mult).then_inc(y_taken, 1)

                ve.sem_inc(y_taken, 1)
                dve.wait_ge(xt_ready, 1)
                xt_dve()
                dve.wait_ge(sil_ready, 1)
                ve.tensor_tensor(hx, ps[3][64:P, :], hsil[64:P, :], ALU.mult).then_inc(hx_ready, 1)
                dve.wait_ge(xt_ready, 2)
                xt_dve()
                with dve.Fori(0, nb1) as b:
                    dve.wait_ge(sil_ready, b + 2)
                    dve.wait_ge(ht_ready, b + 1)
                    ve.tensor_tensor(hx, ps[3][64:P, :], hsil[64:P, :], ALU.mult).then_inc(hx_ready, 1)
                    dve.wait_ge(xt_ready, b + 3)
                    xt_dve()
                    dve.wait_ge(y_ready, b + 1)
                    dve.wait_ge(y_out, b * 32 + 32)
                    y_row()
                dve.wait_ge(y_ready, nb)
                dve.wait_ge(y_out, nb * 32)
                y_row()
                for i in range(NT):
                    dve.wait_ge(yg_in[i], 32)
                    for k in range(2):
                        link(ve.scalar_tensor_tensor(xs[:, i, :], yg[:, i, k, :], wsel[:, k, i:i + 1], xs[:, i, :], ALU.mult, ALU.add))
                layer_end(dve, l, share(4))


def program(nc, args):
    trunk(nc, *args)


_INS = ["x", "c", "positions", "ada_w", "ada_b", "norm_mix_w", "norm_ffn_w", "w_in", "b_igate", "b_fgate",
        "q_norm_w", "k_norm_w", "sinks", "conv_w", "conv_b", "mlstm_norm_w", "w_attn_up", "w_mlstm_up",
        "w_out", "router_w", "router_bias", "w_gate", "w_up", "w_down"]


def kernel(**inputs):
    import concourse.bacc as _bacc
    from concourse.bass_utils import run_bass_kernel_spmd as _run

    nc = _bacc.Bacc("TRN2", target_bir_lowering=False, num_devices=1)
    arrays, args = {}, []
    for name in _INS:
        a = np.ascontiguousarray(inputs[name])
        arrays[f"in_{name}_dram"] = a
        args.append(nc.dram_tensor(f"in_{name}_dram", a.shape, mybir.dt.from_np(a.dtype), kind="ExternalInput").ap())
    args.append(nc.dram_tensor("out_0_dram", inputs["x"].shape, F32, kind="ExternalOutput").ap())
    program(nc, args)
    r = _run(nc, [arrays], core_ids=[0])
    return r.results[0]["out_0_dram"]
```

```python
from contextlib import ExitStack

import numpy as np

import concourse.bass as bass
from concourse import mybir

ALU = mybir.AluOpType
ACT = mybir.ActivationFunctionType
F32 = mybir.dt.float32
BF16 = mybir.dt.bfloat16
I32 = mybir.dt.int32
U32 = mybir.dt.uint32
AX = mybir.AxisListType

P = 128
NEG = -1.0e30
THETA = 500000.0
EPS = 1e-6
MB = 64
RING = 6
MIX_SLOTS = 4
HEAD_ADA = 4


def group_order(NT, NH, HM):
    o = [("ada", j) for j in range(HEAD_ADA)]
    o += [("h1T", k) for k in range(8)]
    for i in range(NT):
        o += [("q", i), ("kv", i)]
    o += [("gates", 0)]
    for m in range(8):
        o += [("mqk", m), ("ada", HEAD_ADA + m)]
        if 1 <= m <= NT:
            o += [("qT", m - 1), ("kT", m - 1)]
    o += [("mv", i) for i in range(NT)]
    o += [("mo", i) for i in range(NT)]
    o += [("rT", 0)] + [("mubc", h) for h in range(HM)] + [("dec", 0)]
    for j in range(8):
        o += [("ga", j), ("ya", j)]
    o += [("gb", 0), ("gb", 1)]
    o += [("hmT", i) for i in range(NT)]
    for j in range(8):
        if j >= 2:
            o += [("gb", j)]
        o += [("yb", j)]
    for i in range(NT):
        o += [("wo", 2 * i), ("wo", 2 * i + 1)]
    o += [("h2T", k) for k in range(8)]
    o += [("rl", 0), ("lg", 0), ("rank", 0)]
    return {name: n for n, name in enumerate(o)}


def trunk(nc, x, c, positions, ada_w, ada_b, norm_mix_w, norm_ffn_w, w_in, b_igate, b_fgate,
          q_norm_w, k_norm_w, sinks, conv_w, conv_b, mlstm_norm_w, w_attn_up, w_mlstm_up, w_out,
          router_w, router_bias, w_gate, w_up, w_down, out):
    _, S, D = x.shape
    DEPTH = ada_w.shape[0]
    NT = S // P
    KD = D // P
    HD = q_norm_w.shape[1]
    HQ = sinks.shape[1]
    HKV = HQ // 4
    G = HQ // HKV
    ROPE = HD // 4
    HALF = ROPE // 2
    HM = b_igate.shape[1]
    DM = 128
    E = router_w.shape[1]
    NG = 4
    EG = E // NG
    F = w_gate.shape[3]
    FC = F // P
    assert (S, D, HD, HQ, HM, E, F) == (512, 1024, 64, 8, 4, 16, 512)
    MAXB = (2 * S + E * (MB - 1)) // MB
    ROWS = ((MAXB + 2) * MB + P - 1) // P * P
    AQ, AK, MQK, MV, MI, MF, MO, GA, GB = 0, 512, 768, 1792, 2304, 2308, 2312, 2824, 3848
    assert GB + D == w_in.shape[2]
    GI = group_order(NT, HM, HM)
    KSCALE = DM ** -0.5 / 4.0

    xd = nc.dram_tensor("expert_rows", [ROWS, D], F32).ap()

    with ExitStack() as ctx:
        def sb(name, shape, dt=F32):
            return ctx.enter_context(nc.sbuf_tensor(name, shape, dt))

        ring = sb("weight_ring", [P, RING, 4096])
        xs = sb("x_tokens", [P, NT, D])
        regA = sb("regA", [P, NT * D])
        hT = sb("h_features", [P, KD, S])
        regB = sb("regB", [P, 6 * S])
        regP = sb("regP", [P, 2 * 2 * 512])
        regU = sb("regU", [P, 2 * 516])
        vaug = sb("mlstm_v_and_one", [P, NT, HM, DM + 1])
        merged = sb("merged_features", [P, KD, S])

        xn = regA[:, :].rearrange("p (i d) -> p i d", i=NT)
        qk_rows = regA[:, 0:NT * 768].rearrange("p (i n) -> p i n", i=NT)
        attn_o = regA[:, 0:4 * S].rearrange("p (c t) -> p c t", c=4)
        rstack = regA[:, NT * 896:NT * 896 + S]
        v_rows = regA[:, NT * 768:NT * 768 + NT * P].rearrange("p (i n) -> p i n", i=NT)
        qkT = regB[:, :].rearrange("p (c t) -> p c t", c=6)
        hmT = regB[:, 0:4 * S].rearrange("p (c t) -> p c t", c=4)
        num = regB[:, 4 * S:4 * S + HM * (DM + 1)].rearrange("p (h n) -> p h n", h=HM)
        pT = regP[:, :].rearrange("p (b k n) -> p b k n", b=2, k=2)
        ke = regP[:, 0:256].rearrange("p (b n) -> p b n", b=2)
        ex = regP[:, 256:512].rearrange("p (b n) -> p b n", b=2)
        wS = regP[:, 512:768].rearrange("p (b n) -> p b n", b=2)
        icb = regP[:, 768:768 + 2 * (DM + 1)].rearrange("p (b n) -> p b n", b=2)
        cst = regP[:, 1028:1028 + HM * (DM + 1)].rearrange("p (h n) -> p h n", h=HM)
        sqs = regP[:, 1544:1544 + 128]
        prm = regP[:, 1024:1024 + P]
        crow = regP[0:KD, 1024 + P:1024 + 2 * P]
        rt = regP[:, 0:1024]
        mqkT = ring[:, 4, :].rearrange("p (m t) -> p m t", m=KD)
        prob = ring[:, 5, 0:2048].rearrange("p (b h n) -> p b h n", b=2, h=4)
        argm = ring[:, 5, 0:2048].rearrange("p (h t) -> p h t", h=HM)
        mo_t = ring[:, 5, 2048:4096].rearrange("p (i n) -> p i n", i=NT)
        conv_u = regU[:, :].rearrange("p (b n) -> p b n", b=2)
        tb = regU[:, 0:1024].rearrange("p (b n) -> p b n", b=2)
        mflat = merged[:, :, :].rearrange("p a b -> p (a b)")
        small = mflat[:, 0:D]
        squares = hT[:, 0:2, :].rearrange("p a b -> p (a b)")
        xg = mflat[0:MB, 0:D]
        xT = mflat[:, 1024:1024 + KD * MB].rearrange("p (k r) -> p k r", k=KD)
        hsil = mflat[:, 1536:2048]
        hx = mflat[0:MB, 2048:2560]
        hxT = mflat[:, 2560:2560 + FC * MB].rearrange("p (k r) -> p k r", k=FC)
        yb = mflat[:, 3072:3584]
        zeros = vaug[:, :, :, :].rearrange("p a b c -> p (a b c)")[:, 0:D]
        rows4 = mflat[0:HM, D:D + 6 * S].rearrange("p (r t) -> p r t", r=6)
        yg = ring[:, 4:6, :].rearrange("p a b -> p (a b)").rearrange("p (i s d) -> p i s d", i=NT, s=2)
        mrow = [regU[:, 0:1024].rearrange("p (b n) -> p b n", b=2), ring[:, 5, 2048:3072].rearrange("p (b n) -> p b n", b=2)]
        diag = [regP[:, 0:512], ring[:, 5, 3072:3584]]

        ident = sb("ident", [P, P])
        ones = sb("ones", [P, P])
        onesb = sb("ones_bf16", [P, P], BF16)
        triu = sb("strictly_before_bf16", [P, P], BF16)
        mask = sb("window_mask", [P, 256])
        maskT = sb("causal_mask_T", [P, P])
        fold = sb("fold16", [P, E])
        cz = sb("c_padded", [P, KD, 32])
        rwz = sb("router_padded", [P, KD, 32])
        cosr = sb("cos", [P, NT, HALF])
        sinr = sb("sin", [P, NT, HALF])
        rbias = sb("router_bias", [P, E])
        thr = sb("block_thresholds", [P, 7])
        iog = sb("iota_minus", [P, 4])
        ioe = sb("block_iota", [1, 32])
        nhalf = sb("minus_half", [P, 16])
        pc = sb("param_cols", [P, P])
        modc = sb("mod_cols", [P, 48])
        A1 = sb("scale1", [P, KD])
        A2 = sb("scale2", [P, KD])
        wmc = sb("mlstm_norm_half", [P, HM])
        g1bc = sb("g1_rows", [P, D])
        g2bc = sb("g2_rows", [P, 512])
        wqk = sb("qk_norm_rows", [P, 2, HD])
        gbias = sb("gate_bias", [36, 1])
        sinkb = sb("sinks", [P, HQ])
        wg36 = sb("gate_columns", [P, KD, 36])
        ss = sb("sum_sq", [P, 16])
        rs = sb("rstd", [P, 16])
        ssq = sb("sum_sq_qk", [P, 16])
        rsq = sb("rstd_qk", [P, 16])
        att = sb("att_small", [P, 2, 32])
        g16 = sb("gate_small", [HM, 40])
        colR = sb("gate_cols", [P, NT, 4, HM])
        decb = sb("decay", [P, HM, 4])
        fin = sb("fin_small", [P, 32])
        Mb = sb("assigned_bf16", [P, NT, E], BF16)
        slot_u = sb("slot_index", [P, 2, NT], U32)
        wsel = sb("gate_weights", [P, 2, NT])
        tabs = sb("block_tables", [1, 64], I32)

        ps = [ctx.enter_context(nc.psum_tensor(f"bank{b}", [P, 512], F32)) for b in range(8)]
        pj = ps[0:2]
        att_s = [ps[2], ps[3]]
        att_t = [ps[4], ps[5]]

        cleared = []

        def lsem(name):
            s = ctx.enter_context(nc.semaphore(name))
            cleared.append(s)
            return s

        def gsem(name):
            return ctx.enter_context(nc.semaphore(name))

        const_in, const_ready, pool_const, dve_const, act_const = (gsem(n) for n in (
            "const_in", "const_ready", "pool_const", "dve_const", "act_const"))
        zeroed, rows_zeroed, c_cols, x_in, meet_a, meet_b = (gsem(n) for n in (
            "zeroed", "rows_zeroed", "c_cols", "x_in", "meet_a", "meet_b"))
        params_in, scattered, head_in = gsem("params_in"), gsem("scattered"), gsem("head_in")
        yg_in = [gsem(f"yg_in{i}") for i in range(NT)]
        ring_in = [lsem(f"ring_in{s}") for s in range(MIX_SLOTS)]
        xg_in, y_out = lsem("xg_in"), lsem("y_out")
        pj_ready = lsem("pj_ready")
        pj_free = [lsem("pj_free0"), lsem("pj_free1")]
        param_cols, mrow_ready, bc_ready, bc_read = (lsem(n) for n in ("param_cols", "mrow_ready", "bc_ready", "bc_read"))
        mod_ready, act_step, dve_step, pool_step, pow_ask, pow_done = (lsem(n) for n in (
            "mod_ready", "act_step", "dve_step", "pool_step", "pow_ask", "pow_done"))
        xn_ready, qk_ready, qk_sq = lsem("xn_ready"), lsem("qk_ready"), lsem("qk_sq")
        s_ready, s_read, m_ready, e_ready, p_norm, pt_ready, pt_evac, o_ready, o_evac = (lsem(n) for n in (
            "s_ready", "s_read", "m_ready", "e_ready", "p_norm", "pt_ready", "pt_evac", "o_ready", "o_evac"))
        rows_ready = lsem("rows_ready")
        gates_f, stack_zero = lsem("gates_f"), lsem("stack_zero")
        ma_ready, ma_act, w_ready, mb_ready, ic_ready, c_upd, hm_ready = (lsem(n) for n in (
            "ma_ready", "ma_act", "w_ready", "mb_ready", "ic_ready", "c_upd", "hm_ready"))
        tb_sum, merged_ready, x_upd, ffn_sq = (lsem(n) for n in ("tb_sum", "merged_ready", "x_upd", "ffn_sq"))
        conv_in, conv_z, conv_t = lsem("conv_in"), lsem("conv_z"), lsem("conv_t")
        routed, tables = lsem("routed"), lsem("tables")
        xt_ready, xt_evac_a, xt_evac_d, gu_ready, sil_ready, hx_ready, ht_ready, ht_evac, y_ready, y_taken = (
            lsem(n) for n in ("xt_ready", "xt_evac_a", "xt_evac_d", "gu_ready", "sil_ready", "hx_ready",
                              "ht_ready", "ht_evac", "y_ready", "y_taken"))
        w_gu = [lsem("w_gate_up0"), lsem("w_gate_up1")]
        w_dn = [lsem("w_down0"), lsem("w_down1")]
        out_done, passed = gsem("out_done"), gsem("passed")

        def lay(ap, l):
            return ap[bass.ds(l, 1)]

        def cols8(w, l, c0, n):
            return lay(w, l)[:, :, c0:c0 + n].rearrange("a (k p) n -> p (a k) n", p=P)

        ITEMS = [("ada", j, j, ("ada", j)) for j in range(HEAD_ADA)]
        ITEMS += [("q", 0, 0, ("q", NT - 1)), ("kv", 0, 1, ("kv", NT - 1)), ("mqk", 0, 2, ("mqk", 3)),
                  ("ada", 4, 3, ("ada", 4)), ("ada", 5, 0, ("ada", 5)), ("mqk", 1, 1, ("mqk", 7)),
                  ("ada", 6, 3, ("ada", 6)), ("ada", 7, 0, ("ada", 7)), ("ada", 8, 3, ("ada", 8)),
                  ("mv", 0, 2, ("mv", NT - 1)),
                  ("ada", 9, 0, ("ada", 9)), ("ada", 10, 3, ("ada", 10)), ("ada", 11, 0, ("ada", 11)),
                  ("mo", 0, 1, ("mo", NT - 1)), ("ga", 0, 3, ("ga", 3)), ("ga", 1, 0, ("ga", 7)), ("ya", 0, 2, ("ya", 7)),
                  ("yb", 0, 1, ("yb", 7)), ("gb", 0, 3, ("gb", 3)), ("gb", 1, 0, ("gb", 7)),
                  ("wo", 0, 2, ("wo", 2 * NT - 1)), ("wo", 1, 3, ("wo", 2 * NT - 1))]
        ITEM = {(name, part): n for n, (name, part, _, _) in enumerate(ITEMS)}
        COLS = {"q": (AQ, 512), "kv": (AK, 256), "mqk": (MQK, 512), "mv": (MV, 512), "mo": (MO, 512), "ga": (GA, 512), "gb": (GB, 512)}
        HEAD = 3

        def mix_item(l, n):
            name, part = ITEMS[n][:2]
            if name == "ada":
                return cols8(ada_w, l, 512 * part, 512), 512, 8
            if name in COLS:
                c0, w = COLS[name]
                return cols8(w_in, l, c0 + 512 * part, w), w, 8
            if name == "wo":
                return lay(w_out, l)[:, 512 * part:512 * part + 512, :].rearrange("a (k p) n -> p (a k) n", p=P), D, 4
            return cols8({"ya": w_attn_up, "yb": w_mlstm_up}[name], l, 0, D), D, 4

        def slot(name, part, k, w):
            return ring[:, ITEMS[ITEM[(name, part)]][2], 0:k * w].rearrange("p (k n) -> p k n", k=k)

        def before(n):
            return [it[2] for it in ITEMS[:n]].count(ITEMS[n][2])

        def load_item(sp, l, n, sem):
            src, w, k = mix_item(l, n)
            sp.dma_start(slot(ITEMS[n][0], ITEMS[n][1], k, w), src).then_inc(sem, 16)

        def through(eng, name, part):
            eng.wait_ge(pj_ready, GI[ITEMS[ITEM[(name, part)]][3]] + 1)

        def arrived(eng, name, part):
            n = ITEM[(name, part)]
            if n >= HEAD:
                eng.wait_ge(ring_in[ITEMS[n][2]], 16 * (before(n) + (ITEMS[n][2] >= HEAD)))

        def bc_bank(j):
            return ps[7] if j >= HEAD_ADA else ps[2 + j % 2]

        def ready(eng, name, i=0):
            g = GI[(name, i)]
            eng.wait_ge(pj_ready, g + 1)
            return pj[g % 2], pj_free[g % 2]

        def wait_reg(eng, sem, value):
            eng.wait_ge(sem, value)
            eng.sem_inc(passed, 1)

        def layer_end(eng, l, mine):
            eng.sem_inc(meet_a, 1)
            wait_reg(eng, meet_a, l * 5 + 5)
            for s in mine:
                eng.sem_clear(s)
            eng.sem_inc(meet_b, 1)
            wait_reg(eng, meet_b, l * 5 + 5)

        def share(n):
            return cleared[n::5]

        block = ctx.enter_context(nc.Block())

        @block.sync
        def _(sp):
            def params(l):
                def rows(dst, src):
                    sp.dma_start(dst, src).then_inc(params_in, 16)

                rows(prm[0:8, :], lay(norm_mix_w, l).rearrange("a (k p) -> (a k) p", p=P))
                rows(prm[8:16, :], lay(norm_ffn_w, l).rearrange("a (k p) -> (a k) p", p=P))
                rows(prm[16:48, :], lay(conv_w, l).rearrange("a j (m p) -> (a j m) p", p=P))
                rows(prm[48:56, :], lay(conv_b, l).rearrange("a (m p) -> (a m) p", p=P))
                rows(prm[56:60, :], lay(mlstm_norm_w, l).rearrange("a (m p) -> (a m) p", p=P))
                rows(prm[60:108, :], lay(ada_b, l).rearrange("a (m p) -> (a m) p", p=P))
                rows(g1bc[:, :], lay(ada_b, l)[:, 2 * D:3 * D].to_broadcast([P, D]))
                rows(wqk[:, 0, :], lay(q_norm_w, l).to_broadcast([P, HD]))
                rows(wqk[:, 1, :], lay(k_norm_w, l).to_broadcast([P, HD]))
                rows(sinkb[:, :], lay(sinks, l).to_broadcast([P, HQ]))
                with nc.allow_non_contiguous_dma(reason="gate columns and biases"):
                    rows(gbias[0:4, :], lay(b_igate, l).rearrange("a h -> h a"))
                    rows(gbias[32:36, :], lay(b_fgate, l).rearrange("a h -> h a"))
                    rows(wg36[:, :, 0:4], cols8(w_in, l, MI, 4))
                    rows(wg36[:, :, 32:36], cols8(w_in, l, MF, 4))

            sp.dma_start(crow, c.rearrange("a (k p) -> (a k) p", p=P)).then_inc(const_in, 16)
            with nc.allow_non_contiguous_dma(reason="positions by token"):
                sp.dma_start(rt[:, 0:NT].bitcast(I32), positions.rearrange("a (i p) -> p (a i)", p=P)).then_inc(const_in, 16)
            sp.dma_start(rbias[:, :], router_bias.rearrange("(a e) -> a e", a=1).to_broadcast([P, E])).then_inc(const_in, 16)
            sp.dma_start(xs[:, :, :], x.rearrange("a (i p) d -> p (a i) d", p=P)).then_inc(x_in, 16)
            sp.wait_ge(zeroed, 2)
            sp.dma_start(rwz[:, :, 0:E], router_w.rearrange("(k p) e -> p k e", p=P)).then_inc(const_in, 16)
            params(0)
            for n in range(HEAD):
                load_item(sp, 0, n, head_in)

            with sp.Fori(0, DEPTH) as l:
                nxt = nc.s_assert_within(l + 1, 1, DEPTH - 1, skip_runtime_bounds_check_because="used where l < DEPTH - 1 only")
                sp.dma_start(g2bc[0:64, :], lay(ada_b, l)[:, 5 * D:5 * D + 512].to_broadcast([64, 512])).then_inc(y_out, 16)
                sp.dma_start(g2bc[64:P, :], lay(ada_b, l)[:, 5 * D + 512:6 * D].to_broadcast([64, 512])).then_inc(y_out, 16)
                for n in range(HEAD, len(ITEMS)):
                    if before(n):
                        prev = [m for m in range(n) if ITEMS[m][2] == ITEMS[n][2]][-1]
                        through(sp, *ITEMS[prev][:2])
                    load_item(sp, l, n, ring_in[ITEMS[n][2]])
                    if ITEMS[n][:2] == ("mqk", 0):
                        with sp.If(l == 0):
                            sp.wait_ge(zeroed, 3)
                            sp.dma_start(xd.rearrange("(n p) d -> p n d", p=P),
                                         zeros.unsqueeze(1).to_broadcast([P, ROWS // P, D])).then_inc(rows_zeroed, 16)

                wg_e = w_gate.rearrange("l e (k p) f -> (l e) p k f", p=P)
                wu_e = w_up.rearrange("l e (k p) f -> (l e) p k f", p=P)
                wd_e = w_down.rearrange("l e (k p) f -> (l e) p k f", p=P)

                def load(part, p, e):
                    src = (wg_e, wu_e, wd_e)[part][bass.ds(l * E + e, 1)].rearrange("a p k f -> p (a k) f")
                    dst = ring[:, 3 * p + part, :].rearrange("p (k n) -> p k n", k=(KD, KD, FC)[part])
                    sp.dma_start(dst, src).then_inc(w_dn[p] if part == 2 else w_gu[p], 16)

                def blocks_through(e):
                    return sp.value_load(tabs[0:1, bass.ds(e + 32, 1)], min_val=1, max_val=MAXB)

                def load_gu(p, e):
                    wait_reg(sp, gu_ready, blocks_through(e - 2))
                    load(0, p, e)
                    load(1, p, e)

                def load_dn(p, e):
                    wait_reg(sp, y_ready, blocks_through(e - 2))
                    load(2, p, e)

                sp.wait_ge(pj_ready, GI[("hmT", NT - 1)] + 1)
                load(1, 1, 1)
                load(2, 1, 1)
                through(sp, "yb", 0)
                load(1, 0, 0)
                through(sp, "gb", 1)
                load(0, 0, 0)
                through(sp, "wo", 1)
                load(0, 1, 1)
                load(2, 0, 0)
                sp.wait_ge(tables, 1)
                with sp.If(l < DEPTH - 1):
                    params(nxt)
                load_gu(0, 2)
                load_gu(1, 3)
                load_dn(0, 2)
                with sp.Fori(2, E // 2) as i:
                    load_gu(0, i * 2)
                    load_dn(1, i * 2 - 1)
                    load_gu(1, i * 2 + 1)
                    load_dn(0, i * 2)
                load_dn(1, E - 1)
                with sp.If(l < DEPTH - 1):
                    for n in range(HEAD):
                        if n == 0:
                            wait_reg(sp, gu_ready, blocks_through(E - 2))
                        if n == 2:
                            wait_reg(sp, y_ready, blocks_through(E - 2))
                        load_item(sp, nxt, n, head_in)
                layer_end(sp, l, share(0))
            sp.dma_start(out.rearrange("a (i p) d -> p (a i) d", p=P), xs[:, :, :]).then_inc(out_done, 16)
            sp.wait_ge(out_done, 16)

        @block.gpsimd
        def _(pool):
            po = nc.gpsimd
            n_const = [0]

            def pc_link(ins):
                n_const[0] += 1
                ins.then_inc(pool_const, 1)
                pool.wait_ge(pool_const, n_const[0])

            po.memset(rwz[:, :, :], 0.0)
            po.memset(wg36[:, :, :], 0.0).then_inc(zeroed, 1)
            pool.wait_ge(zeroed, 1)
            po.memset(prm[96:P, :], 0.0).then_inc(zeroed, 1)
            pool.wait_ge(zeroed, 2)
            po.memset(cz[:, :, :], 0.0)
            po.memset(zeros, 0.0).then_inc(zeroed, 1)
            po.memset(ones[:, :], 1.0)
            po.memset(onesb[:, :], 1.0)
            po.memset(ident[:, :], 0.0)
            po.memset(mask[:, :], 0.0)
            po.memset(maskT[:, :], 0.0)
            pc_link(po.memset(nhalf[:, :], -0.5))
            po.affine_select(out=ident[:, :], in_=ident[:, :], compare_op=ALU.not_equal, fill=1.0, base=0,
                             pattern=[[-1, P]], channel_multiplier=1)
            po.affine_select(out=mask[:, 0:P], in_=mask[:, 0:P], compare_op=ALU.is_gt, fill=NEG, base=0,
                             pattern=[[1, P]], channel_multiplier=-1)
            po.affine_select(out=mask[:, P:256], in_=mask[:, P:256], compare_op=ALU.is_ge, fill=NEG, base=0,
                             pattern=[[-1, P]], channel_multiplier=1)
            po.affine_select(out=maskT[:, :], in_=maskT[:, :], compare_op=ALU.is_ge, fill=NEG, base=0,
                             pattern=[[1, P]], channel_multiplier=-1)
            po.affine_select(out=triu[:, :], in_=onesb[:, :], compare_op=ALU.is_gt, fill=0.0, base=0,
                             pattern=[[1, P]], channel_multiplier=-1)
            for k in range(1, 8):
                po.memset(thr[:, k - 1:k], float(MB * k))
            for g in range(4):
                po.memset(iog[:, g:g + 1], float(g - 8))
            pc_link(po.iota(ioe[:, :], pattern=[[1, 32]], base=0, channel_multiplier=0, allow_small_or_imprecise_dtypes=True))

            def power(n, dst, src):
                pool.wait_ge(pow_ask, n)
                w = src.shape[1]
                po.tensor_tensor(dst, src, nhalf[:, 0:w], ALU.pow).then_inc(pow_done, 1)

            with pool.Fori(0, DEPTH) as l:
                power(1, rs[:, 0:NT], ss[:, 0:NT])
                pool.wait_ge(pj_ready, GI[("h1T", KD - 1)] + 1)
                po.memset(rstack[:, :], 0.0).then_inc(stack_zero, 1)
                for i in range(NT):
                    power(2 + i, rsq[:, 0:10], ssq[:, 0:10])
                for i in range(NT):
                    power(6 + i, fin[:, 8:12], fin[:, 4:8])
                for j in range(KD):
                    pool.wait_ge(tb_sum, j + 1)
                    po.tensor_tensor(merged[:, j, :], merged[:, j, :], tb[:, j % 2, :], ALU.add).then_inc(merged_ready, 1)
                for i in range(NT):
                    power(10 + i, rs[:, 4 + i:5 + i], ss[:, 4 + i:5 + i])

                pool.wait_ge(routed, 2)
                pool.wait_ge(xn_ready, 2 * NT)
                pool.wait_ge(rows_zeroed, 16)
                for k in range(2):
                    for i in range(NT):
                        po.indirect_dma_start(out=xd, out_offset=bass.IndirectOffsetOnAxis(ap=slot_u[:, k, i:i + 1], axis=0),
                                              in_=xn[:, i, :], in_offset=None).then_inc(scattered, 16)
                pool.wait_ge(tables, 1)
                nb = po.value_load(tabs[0:1, 47:48], min_val=E, max_val=MAXB)
                wait_reg(pool, y_out, nb * 32 + 32)
                for i in range(NT):
                    for k in range(2):
                        po.indirect_dma_start(out=yg[:, i, k, :], out_offset=None, in_=xd,
                                              in_offset=bass.IndirectOffsetOnAxis(ap=slot_u[:, k, i:i + 1], axis=0)).then_inc(yg_in[i], 16)
                layer_end(pool, l, share(1))

        @block.scalar
        def _(act):
            ac = nc.scalar
            step = [0]

            def link(ins):
                step[0] += 1
                ins.then_inc(act_step, 1)
                act.wait_ge(act_step, step[0])

            act.wait_ge(dve_const, 1)
            ac.activation(sinr[:, :, :].rearrange("p i f -> p (i f)"), rt[:, 64:96], ACT.Sin).then_inc(act_const, 1)
            ac.activation(cosr[:, :, :].rearrange("p i f -> p (i f)"), rt[:, 96:128], ACT.Sin).then_inc(act_const, 1)
            act.wait_ge(c_cols, 1)
            ac.activation(cz[:, :, 0], ps[2][:, 0:KD], ACT.Silu).then_inc(act_const, 1)

            with act.Fori(0, DEPTH) as l:
                step[0] = 0
                for i in range(NT):
                    act.wait_ge(x_in, 16)
                    ac.activation(squares, xs[:, i, :], ACT.Square, accum_out=ss[:, i:i + 1]).then_inc(ffn_sq, 1)
                    act.wait_ge(ffn_sq, i + 1)
                def ada_row(j):
                    bank, free = ready(act, "ada", j)
                    if j >= 2:
                        act.wait_ge(bc_ready, j - 1)
                    ac.activation(mrow[j >= HEAD_ADA][:, j % 2, :], bank[:, :], ACT.Copy).then_inc(mrow_ready, 1)
                    act.wait_ge(mrow_ready, j + 1)
                    act.sem_inc(free, 1)

                for j in range(HEAD_ADA):
                    ada_row(j)
                act.wait_ge(mod_ready, 1)
                for k in range(1, KD, 2):
                    bank, free = ready(act, "h1T", k)
                    ac.activation(hT[:, k, :], bank[:, :], ACT.Identity, scale=A1[:, k:k + 1],
                                  bias=modc[:, k:k + 1]).then_inc(free, 1)
                for i in range(NT):
                    bank, free = ready(act, "q", i)
                    ac.activation(qk_rows[:, i, 0:512], bank[:, :], ACT.Copy)
                    if i >= 1:
                        act.wait_ge(qk_sq, i)
                    ac.activation(small[:, 0:512], bank[:, :], ACT.Square).then_inc(free, 1)
                    bank, free = ready(act, "kv", i)
                    ac.activation(qk_rows[:, i, 512:640], bank[:, 0:128], ACT.Copy)
                    ac.activation(v_rows[:, i, :], bank[:, 128:256], ACT.Copy)
                    ac.activation(small[:, 512:640], bank[:, 0:128], ACT.Square).then_inc(free, 1)
                bank, free = ready(act, "gates")
                ac.activation(rows4[:, 0, :], bank[0:4, :], ACT.Identity, bias=gbias[0:4, :]).then_inc(gates_f, 1)
                act.wait_ge(gates_f, 2)
                ac.activation(rows4[:, 2, :], rows4[:, 2, :], ACT.Exp, scale=-1.0).then_inc(gates_f, 1)
                act.wait_ge(gates_f, 3)
                ac.activation(rows4[:, 2, :], rows4[:, 2, :], ACT.Ln, bias=1.0).then_inc(gates_f, 1)

                def conv_act(m):
                    bank, free = ready(act, "mqk", m)
                    if m >= 2:
                        act.wait_ge(conv_z, m - 1)
                    ac.activation(conv_u[:, m % 2, 3:515], bank[:, :], ACT.Copy).then_inc(conv_in, 1)
                    act.wait_ge(conv_in, m + 1)
                    act.sem_inc(free, 1)

                def conv_tanh(m):
                    act.wait_ge(conv_z, m + 1)
                    if m == 0:
                        act.wait_ge(qk_sq, NT)
                    if m >= 1:
                        act.wait_ge(conv_t, 2 * m)
                    ac.activation(small[:, 0:512], mqkT[:, m, :], ACT.Tanh, scale=0.5).then_inc(conv_t, 1)

                def qkT_evac(i):
                    bank, free = ready(act, "qT", i)
                    ac.activation(qkT[:, 0:4, P * i:P * i + P], bank[:, :].rearrange("p (c t) -> p c t", c=4), ACT.Copy).then_inc(free, 1)
                    bank, free = ready(act, "kT", i)
                    ac.activation(qkT[:, 4:6, P * i:P * i + P], bank[:, 0:256].rearrange("p (c t) -> p c t", c=2), ACT.Copy).then_inc(free, 1)

                def att_exp(u):
                    n, g = u // HKV, u % HKV
                    lo = 0 if n else P
                    act.wait_ge(m_ready, u + 1)
                    a = att[:, u % 2, :]
                    for h in range(4):
                        ac.activation(prob[:, u % 2, h, lo:256], prob[:, u % 2, h, lo:256], ACT.Exp,
                                      bias=a[:, 4 + h:5 + h], accum_out=a[:, 8 + h:9 + h])
                    ac.activation(a[:, 12:16], a[:, 16:20], ACT.Exp).then_inc(e_ready, 1)

                def att_pt(u):
                    n = u // HKV
                    act.wait_ge(pt_ready, u + 1)
                    if u >= 2:
                        act.wait_ge(o_ready, u - 1)
                    ac.activation(pT[:, u % 2, 1, :], att_t[1][:, :], ACT.Copy).then_inc(pt_evac, 1)

                def att_o(u):
                    n, g = u // HKV, u % HKV
                    act.wait_ge(o_ready, u + 1)
                    o4 = ps[6][0:64, :].rearrange("p (a b t) -> p b a t", a=2, b=2)
                    for odd in range(2):
                        last = ac.activation(attn_o[64 * odd:64 * odd + 64, 2 * g:2 * g + 2, P * n:P * n + P], o4[:, odd], ACT.Copy)
                    last.then_inc(o_evac, 1)

                for s in range(16):
                    if s < 8:
                        if s == 0:
                            act.wait_ge(bc_ready, HEAD_ADA)
                        conv_act(s)
                        ada_row(HEAD_ADA + s)
                    elif s < 12:
                        i = s - 8
                        if i == 0:
                            act.wait_ge(rows_zeroed, 16)
                        bank, free = ready(act, "mv", i)
                        ac.activation(vaug[:, i, :, 0:DM], bank[:, :].rearrange("p (h n) -> p h n", h=HM), ACT.Copy).then_inc(free, 1)
                    else:
                        i = s - 12
                        if i == 0:
                            act.wait_ge(bc_read, 12)
                        bank, free = ready(act, "mo", i)
                        ac.activation(mo_t[:, i, :], bank[:, :], ACT.Tanh, scale=0.5).then_inc(free, 1)
                    if 1 <= s <= NT:
                        qkT_evac(s - 1)
                    if 1 <= s <= 8:
                        conv_tanh(s - 1)
                    if 4 <= s < 12:
                        att_exp(s - 4)
                    if 5 <= s < 13:
                        att_pt(s - 5)
                    if 6 <= s < 14:
                        att_o(s - 6)
                    if s == 8:
                        act.wait_ge(rows_ready, 1)
                        for q in (32, 64, 96):
                            ac.activation(rstack[q:q + 4, :], rstack[q:q + 4, :], ACT.Exp)
                        ac.activation(g16[:, 24:28], g16[:, 20:24], ACT.Exp).then_inc(rows_ready, 1)
                bank, free = ready(act, "rT")
                for q in range(4):
                    ins = ac.activation(colR[:, :, q, :], bank[:, :].rearrange("p (i n) -> p i n", i=NT)[:, :, 32 * q:32 * q + HM], ACT.Copy)
                ins.then_inc(free, 1)
                act.wait_ge(free, GI[("rT", 0)] // 2 + 1)

                def m_act_a(u):
                    c_, h = u // HM, u % HM
                    act.wait_ge(ma_ready, u + 1)
                    if u >= 2:
                        act.wait_ge(mb_ready, u - 1)
                    b = 2 + u % 2
                    ac.activation(ke[:, u % 2, :], ps[b][:, 0:P], ACT.Copy, scale=colR[:, c_, 2, h:h + 1])
                    ac.activation(ex[:, u % 2, :], argm[:, h, P * c_:P * c_ + P], ACT.Exp, bias=colR[:, c_, 0, h:h + 1]).then_inc(ma_act, 1)

                def m_act_b(u):
                    c_, h = u // HM, u % HM
                    act.wait_ge(mb_ready, u + 1)
                    if c_ > 0:
                        if u >= HM + 2:
                            act.wait_ge(c_upd, u - 1)
                        ac.activation(icb[:, u % 2, :], ps[4 + u % 2][:, 256:256 + DM + 1], ACT.Copy,
                                      scale=colR[:, c_, 1, h:h + 1]).then_inc(ic_ready, 1)

                act.wait_ge(pj_free[GI[("mubc", HM - 1)] % 2], GI[("mubc", HM - 1)] // 2 + 1)
                act.wait_ge(pj_free[GI[("mubc", HM - 2)] % 2], GI[("mubc", HM - 2)] // 2 + 1)
                for j in range(8):
                    bank, free = ready(act, "ga", j)
                    ac.activation(merged[:, j, :], bank[:, :], ACT.Tanh, scale=0.5).then_inc(free, 1)
                    for u in (2 * j, 2 * j + 1):
                        m_act_a(u)
                        if u >= 1:
                            m_act_b(u - 1)
                m_act_b(15)
                for j in range(8):
                    bank, free = ready(act, "gb", j)
                    if j >= 2:
                        act.wait_ge(merged_ready, j - 1)
                    ac.activation(tb[:, j % 2, :], bank[:, :], ACT.Tanh, scale=0.5).then_inc(free, 1)

                for i in range(NT):
                    act.wait_ge(x_upd, i + 1)
                    act.wait_ge(ffn_sq, NT + i)
                    ac.activation(squares, xs[:, i, :], ACT.Square, accum_out=ss[:, 4 + i:5 + i]).then_inc(ffn_sq, 1)
                for k in range(1, KD, 2):
                    bank, free = ready(act, "h2T", k)
                    ac.activation(hT[:, k, :], bank[:, :], ACT.Identity, scale=A2[:, k:k + 1],
                                  bias=modc[:, 24 + k:25 + k]).then_inc(free, 1)
                bank, free = ready(act, "rl")
                act.wait_ge(ffn_sq, 2 * NT)
                ac.activation(small[:, 0:512], bank[:, :], ACT.Copy).then_inc(free, 1)
                bank, free = ready(act, "lg")
                ac.activation(rt[:, 0:64], bank[:, 0:64], ACT.Exp, scale=-1.0).then_inc(free, 1)

                act.wait_ge(tables, 1)
                nb = ac.value_load(tabs[0:1, 47:48], min_val=E, max_val=MAXB)
                nb1 = ac.value_load(tabs[0:1, 48:49], min_val=E - 1, max_val=MAXB - 1)

                def xt_act():
                    for k in range(0, KD, 2):
                        last = ac.activation(xT[:, k, :], ps[2][:, MB * k:MB * k + MB], ACT.Identity,
                                             scale=A2[:, k:k + 1], bias=modc[:, 24 + k:25 + k])
                    last.then_inc(xt_evac_a, 1)

                def load_rows(b):
                    act.dma_start(xg, xd[bass.ds(b * MB, MB), :]).then_inc(xg_in, 16)

                def silu_():
                    ac.activation(hsil[64:P, :], ps[3][0:64, :], ACT.Silu).then_inc(sil_ready, 1)

                def h_evac():
                    ac.activation(hxT[:, :, :].rearrange("p k r -> p (k r)"), ps[4][:, 0:FC * MB], ACT.Copy).then_inc(ht_evac, 1)

                def store_rows(b):
                    wait_reg(act, y_taken, b + 2)
                    for h in range(2):
                        act.dma_start(xd[bass.ds(b * MB, MB), 512 * h:512 * h + 512], yb[64 * h:64 * h + 64, :]).then_inc(y_out, 16)

                wait_reg(act, scattered, l * (32 * NT) + 32 * NT)
                act.dma_start(xg, xd[0:MB, :]).then_inc(xg_in, 16)
                act.wait_ge(xt_ready, 1)
                xt_act()
                act.dma_start(xg, xd[MB:2 * MB, :]).then_inc(xg_in, 16)
                act.wait_ge(gu_ready, 1)
                silu_()
                act.wait_ge(xt_ready, 2)
                xt_act()
                act.dma_start(xg, xd[2 * MB:3 * MB, :]).then_inc(xg_in, 16)
                act.wait_ge(ht_ready, 1)
                h_evac()
                with act.Fori(0, nb1) as b:
                    act.wait_ge(gu_ready, b + 2)
                    silu_()
                    act.wait_ge(xt_ready, b + 3)
                    xt_act()
                    load_rows(b + 3)
                    act.wait_ge(ht_ready, b + 2)
                    h_evac()
                    store_rows(b)
                store_rows(nb1)
                wait_reg(act, xg_in, nb * 16 + 32)
                layer_end(act, l, share(2))

        @block.tensor
        def _(pe):
            te = nc.tensor
            pe.wait_ge(const_in, 16 * 4)
            pe.wait_ge(pool_const, 2)
            te.transpose(ps[2][:, 0:KD], crow, ident[0:KD, 0:KD]).then_inc(c_cols, 1)
            pe.wait_ge(act_const, 3)
            pe.wait_ge(dve_const, 3)

            with pe.Fori(0, DEPTH) as l:
                def take(name, i=0):
                    g = GI[(name, i)]
                    if g >= 2:
                        pe.wait_ge(pj_free[g % 2], g // 2)
                    return pj[g % 2]

                wait_reg(pe, params_in, l * 224 + 224)
                te.transpose(ps[4][:, 0:P], prm[:, :], ident[:, :]).then_inc(param_cols, 1)

                def bcast(j):
                    pe.wait_ge(mrow_ready, j + 1)
                    if j >= 1:
                        pe.wait_ge(bc_read, j if j >= HEAD_ADA else max(j - 1, 1))
                    te.matmul(bc_bank(j)[:, :], ones[:, :], mrow[j >= HEAD_ADA][:, j % 2, :], start=True, stop=True).then_inc(bc_ready, 1)

                def ada_group(j):
                    arrived(pe, "ada", j)
                    bank = take("ada", j)
                    w = slot("ada", j, 8, 512)
                    for k in range(KD):
                        g = k % 4
                        ins = te.matmul(bank[32 * g:32 * g + 32, :], cz[:, k, :], w[:, k, :], start=(k < 4), stop=(k >= 4))
                    ins.then_inc(pj_ready, 1)

                wait_reg(pe, head_in, l * (16 * HEAD) + 16 * HEAD)
                for j in range(HEAD_ADA):
                    ada_group(j)
                    if j >= 1:
                        bcast(j - 1)
                bcast(HEAD_ADA - 1)

                pe.wait_ge(xn_ready, NT)
                for k in range(KD):
                    bank = take("h1T", k)
                    for i in range(NT):
                        ins = te.transpose(bank[:, P * i:P * i + P], xn[:, i, P * k:P * k + P], ident[:, :])
                    ins.then_inc(pj_ready, 1)
                g = GI[("h1T", KD - 1)]
                pe.wait_ge(pj_free[g % 2], g // 2 + 1)
                pe.wait_ge(pj_free[1 - g % 2], (g - 1) // 2 + 1)

                def token_group(name, i, w):
                    arrived(pe, name, 0)
                    bank = take(name, i)
                    wv = slot(name, 0, 8, w)
                    for k in range(KD):
                        ins = te.matmul(bank[:, 0:w], hT[:, k, P * i:P * i + P], wv[:, k, :], start=(k == 0), stop=(k == KD - 1))
                    ins.then_inc(pj_ready, 1)

                def feature_group(name, m, rhs, kn, w):
                    arrived(pe, name, m // (w // P))
                    bank = take(name, m)
                    wv = slot(name, m // (w // P), kn, w)
                    c0 = P * (m % (w // P))
                    for k in range(kn):
                        ins = te.matmul(bank[:, :], wv[:, k, c0:c0 + P], rhs[:, k, :], start=(k == 0), stop=(k == kn - 1))
                    ins.then_inc(pj_ready, 1)

                for i in range(NT):
                    token_group("q", i, 512)
                    token_group("kv", i, 256)
                bank = take("gates")
                for k in range(KD):
                    ins = te.matmul(bank[0:36, :], wg36[:, k, :], hT[:, k, :], start=(k == 0), stop=(k == KD - 1))
                ins.then_inc(pj_ready, 1)

                def qk_transposes(i):
                    pe.wait_ge(qk_ready, i + 1)
                    for name, c0, n in (("qT", 0, 4), ("kT", 4, 2)):
                        bank = take(name, i)
                        for m in range(n):
                            ins = te.transpose(bank[:, P * m:P * m + P], qk_rows[:, i, P * (c0 + m):P * (c0 + m) + P], ident[:, :])
                        ins.then_inc(pj_ready, 1)

                def att_scores(u):
                    n, g = u // HKV, u % HKV
                    if u == 0:
                        pe.wait_ge(bc_read, HEAD_ADA)
                    gi = GI[("kT", n)]
                    pe.wait_ge(pj_free[gi % 2], gi // 2 + 1)
                    pe.wait_ge(pj_free[(gi - 1) % 2], (gi - 1) // 2 + 1)
                    if u >= 1:
                        pe.wait_ge(s_read, u)
                    for h in range(4):
                        hq = 4 * g + h
                        r = 64 * (hq % 2)
                        q = qkT[r:r + 64, hq // 2, P * n:P * n + P]
                        bank = att_s[h % 2]
                        o = 256 * (h // 2)
                        if n:
                            ins = te.matmul(bank[:, o:o + 256], q, qkT[r:r + 64, 4 + g, P * (n - 1):P * (n + 1)], start=True, stop=True)
                        else:
                            ins = te.matmul(bank[:, o + P:o + 256], q, qkT[r:r + 64, 4 + g, 0:P], start=True, stop=True)
                    ins.then_inc(s_ready, 1)

                def att_ptrans(u):
                    n = u // HKV
                    pe.wait_ge(p_norm, u + 1)
                    if u >= 1:
                        pe.wait_ge(pt_evac, 2 * u)
                    for kb in range(0 if n else 1, 2):
                        for h in range(4):
                            ins = te.transpose(att_t[kb][:, P * h:P * h + P], prob[:, u % 2, h, P * kb:P * kb + P], ident[:, :])
                    ins.then_inc(pt_ready, 1)

                def att_out(u):
                    n, g = u // HKV, u % HKV
                    pe.wait_ge(pt_evac, 2 * (u + 1))
                    if u >= 1:
                        pe.wait_ge(o_evac, u)
                    for kb in range(0 if n else 1, 2):
                        ins = te.matmul(ps[6][0:64, :], v_rows[:, n - 1 + kb, 64 * g:64 * g + 64], pT[:, u % 2, kb, :],
                                        start=(kb == 0 or n == 0), stop=(kb == 1))
                    ins.then_inc(o_ready, 1)

                for s in range(16):
                    if s < 8:
                        feature_group("mqk", s, hT, 8, 512)
                        ada_group(HEAD_ADA + s)
                    elif s < 12:
                        token_group("mv", s - 8, 512)
                    else:
                        token_group("mo", s - 12, 512)
                    if 1 <= s <= 8:
                        bcast(HEAD_ADA + s - 1)
                    if 1 <= s <= NT:
                        qk_transposes(s - 1)
                    if 4 <= s < 12:
                        att_scores(s - 4)
                    if 5 <= s < 13:
                        att_ptrans(s - 5)
                    if 6 <= s < 14:
                        att_out(s - 6)
                pe.wait_ge(rows_ready, 2)
                bank = take("rT")
                for i in range(NT):
                    ins = te.transpose(bank[:, P * i:P * i + P], rstack[:, P * i:P * i + P], ident[:, :])
                ins.then_inc(pj_ready, 1)
                for h in range(HM):
                    bank = take("mubc", h)
                    te.matmul(bank[:, :], ident[0:HM, h:h + 1].to_broadcast([HM, P]), rows4[:, 5, :], start=True, stop=True).then_inc(pj_ready, 1)
                bank = take("dec")
                for h in range(HM):
                    ins = te.matmul(bank[:, 4 * h:4 * h + 4], ident[0:HM, h:h + 1].to_broadcast([HM, P]), g16[:, 24:28], start=True, stop=True)
                ins.then_inc(pj_ready, 1)
                pe.wait_ge(pj_free[GI[("mo", NT - 1)] % 2], GI[("mo", NT - 1)] // 2 + 1)
                pe.wait_ge(conv_t, 16)
                pe.wait_ge(pt_evac, 16)
                pe.wait_ge(o_evac, 8)
                pe.wait_ge(bc_read, 12)

                def m_a(u):
                    c_, h = u // HM, u % HM
                    b = 2 + u % 2
                    if u >= 2:
                        pe.wait_ge(ma_act, u - 1)
                        pe.wait_ge(w_ready, u - 1)
                    kf = mqkT[:, HM + h, P * c_:P * c_ + P]
                    te.transpose(ps[b][:, 0:P], kf, ident[:, :])
                    te.matmul(ps[b][:, P:2 * P], kf, mqkT[:, h, P * c_:P * c_ + P], start=True, stop=True).then_inc(ma_ready, 1)

                def m_b(u):
                    c_, h = u // HM, u % HM
                    pe.wait_ge(w_ready, u + 1)
                    pe.wait_ge(ma_act, u + 1)
                    if u >= 2:
                        pe.wait_ge(c_upd, u - 1)
                    ins = te.matmul(ps[4 + u % 2][:, 0:DM + 1], wS[:, u % 2, :], vaug[:, c_, h, :], start=True, stop=True)
                    if c_ > 0:
                        pe.wait_ge(c_upd, u - HM + 1)
                        ins = te.matmul(ps[4 + u % 2][:, 256:256 + DM + 1], mqkT[:, h, P * c_:P * c_ + P], cst[:, h, :], start=True, stop=True)
                    if c_ < NT - 1:
                        ins = te.matmul(ps[6 + u % 2][:, 0:DM + 1], ke[:, u % 2, :], vaug[:, c_, h, :], start=True, stop=True)
                    ins.then_inc(mb_ready, 1)

                for j in range(8):
                    feature_group("ga", j, hT, 8, 512)
                    for u in (2 * j, 2 * j + 1):
                        m_a(u)
                        if u >= 1:
                            m_b(u - 1)
                    feature_group("ya", j, attn_o, 4, D)
                m_b(15)
                feature_group("gb", 0, hT, 8, 512)
                feature_group("gb", 1, hT, 8, 512)
                for i in range(NT):
                    pe.wait_ge(hm_ready, i + 1)
                    bank = take("hmT", i)
                    for h in range(HM):
                        ins = te.transpose(bank[:, P * h:P * h + P], mo_t[:, i, P * h:P * h + P], ident[:, :])
                    ins.then_inc(pj_ready, 1)
                for j in range(8):
                    if j >= 2:
                        feature_group("gb", j, hT, 8, 512)
                    if j == 0:
                        for g in (GI[("hmT", NT - 1)], GI[("hmT", NT - 2)]):
                            pe.wait_ge(pj_free[g % 2], g // 2 + 1)
                    feature_group("yb", j, hmT, 4, D)
                pe.wait_ge(merged_ready, 8)
                for i in range(NT):
                    for h in range(2):
                        if h == 0 and i == 0:
                            arrived(pe, "wo", 0)
                            arrived(pe, "wo", 1)
                        bank = take("wo", 2 * i + h)
                        for k in range(KD):
                            ins = te.matmul(bank[:, :], merged[:, k, P * i:P * i + P],
                                            slot("wo", k // 4, 4, D)[:, k % 4, 512 * h:512 * h + 512], start=(k == 0), stop=(k == KD - 1))
                        ins.then_inc(pj_ready, 1)

                pe.wait_ge(xn_ready, 2 * NT)
                for k in range(KD):
                    bank = take("h2T", k)
                    for i in range(NT):
                        ins = te.transpose(bank[:, P * i:P * i + P], xn[:, i, P * k:P * k + P], ident[:, :])
                    ins.then_inc(pj_ready, 1)
                g = GI[("h2T", KD - 1)]
                pe.wait_ge(pj_free[g % 2], g // 2 + 1)
                pe.wait_ge(pj_free[1 - g % 2], (g - 1) // 2 + 1)
                bank = take("rl")
                for k in range(KD):
                    g = k % 4
                    ins = te.matmul(bank[32 * g:32 * g + 32, :], rwz[:, k, :], hT[:, k, :], start=(k < 4), stop=(k >= 4))
                ins.then_inc(pj_ready, 1)
                g = GI[("rl", 0)]
                pe.wait_ge(pj_free[g % 2], g // 2 + 1)
                bank = take("lg")
                for i in range(NT):
                    ins = te.matmul(bank[:, E * i:E * i + E], small[:, P * i:P * i + P], fold[:, :], start=True, stop=True)
                ins.then_inc(pj_ready, 1)
                pe.wait_ge(routed, 1)
                bank = take("rank")
                for i in range(NT):
                    for j in range(i):
                        te.matmul(bank[:, E * i:E * i + E], onesb[:, :], Mb[:, j, :], start=(j == 0), stop=False)
                    te.matmul(bank[:, E * i:E * i + E], triu[:, :], Mb[:, i, :], start=(i == 0), stop=True)
                for j in range(NT):
                    ins = te.matmul(bank[:, E * NT:E * NT + E], onesb[:, :], Mb[:, j, :], start=(j == 0), stop=(j == NT - 1))
                ins.then_inc(pj_ready, 1)

                pe.wait_ge(tables, 1)
                nb = te.value_load(tabs[0:1, 47:48], min_val=E, max_val=MAXB)
                nb1 = te.value_load(tabs[0:1, 48:49], min_val=E - 1, max_val=MAXB - 1)

                def x_transposes():
                    for k in range(KD):
                        ins = te.transpose(ps[(2, 6)[k % 2]][:, MB * k:MB * k + MB], xg[:, P * k:P * k + P], ident[0:MB, 0:MB])
                    ins.then_inc(xt_ready, 1)

                def gate_up(p):
                    for k in range(KD):
                        for part in range(2):
                            w = ring[:, 3 * p + part, :].rearrange("p (k n) -> p k n", k=KD)
                            ins = te.matmul(ps[3][64 * part:64 * part + 64, :], xT[:, k, :], w[:, k, :], start=(k == 0), stop=(k == KD - 1))
                    ins.then_inc(gu_ready, 1)

                def h_transposes(b):
                    wait_reg(pe, hx_ready, b + 1)
                    for k in range(FC):
                        ins = te.transpose(ps[4][:, MB * k:MB * k + MB], hx[:, P * k:P * k + P], ident[0:MB, 0:MB])
                    ins.then_inc(ht_ready, 1)

                def down(p):
                    w = ring[:, 3 * p + 2, :].rearrange("p (k n) -> p k n", k=FC)
                    for k in range(FC):
                        for half in range(2):
                            ins = te.matmul(ps[5][64 * half:64 * half + 64, :], hxT[:, k, :], w[:, k, 512 * half:512 * half + 512],
                                            start=(k == 0), stop=(k == FC - 1))
                    ins.then_inc(y_ready, 1)

                pe.wait_ge(xg_in, 16)
                x_transposes()
                pe.wait_ge(xt_evac_a, 1)
                pe.wait_ge(xt_evac_d, 1)
                pe.wait_ge(w_gu[0], 32)
                gate_up(0)
                pe.wait_ge(xg_in, 32)
                x_transposes()
                h_transposes(0)
                with pe.Fori(0, nb1) as b:
                    e1 = te.value_load(tabs[0:1, bass.ds(b + 1, 1)], min_val=0, max_val=E - 1)
                    e0 = te.value_load(tabs[0:1, bass.ds(b, 1)], min_val=0, max_val=E - 1)
                    pe.wait_ge(xt_evac_a, b + 2)
                    pe.wait_ge(xt_evac_d, b + 2)
                    with pe.If(e1 % 2 == 0):
                        pe.wait_ge(w_gu[0], (e1 // 2) * 32 + 32)
                        gate_up(0)
                    with pe.Else():
                        pe.wait_ge(w_gu[1], (e1 // 2) * 32 + 32)
                        gate_up(1)
                    wait_reg(pe, xg_in, (b + 3) * 16)
                    x_transposes()
                    pe.wait_ge(ht_evac, b + 1)
                    pe.wait_ge(y_taken, b + 1)
                    with pe.If(e0 % 2 == 0):
                        pe.wait_ge(w_dn[0], (e0 // 2) * 16 + 16)
                        down(0)
                    with pe.Else():
                        pe.wait_ge(w_dn[1], (e0 // 2) * 16 + 16)
                        down(1)
                    h_transposes(b + 1)
                pe.wait_ge(ht_evac, nb)
                pe.wait_ge(y_taken, nb)
                pe.wait_ge(w_dn[1], E // 2 * 16)
                down(1)
                layer_end(pe, l, share(3))

        @block.vector
        def _(dve):
            ve = nc.vector
            cstep = [0]

            def clink(ins):
                cstep[0] += 1
                ins.then_inc(dve_step, 1)
                dve.wait_ge(dve_step, cstep[0])

            dve.wait_ge(const_in, 16 * 4)
            clink(ve.tensor_copy(rt[:, 4:8], rt[:, 0:4].bitcast(I32)))
            inv = np.power(np.float32(THETA), -(np.arange(0, ROPE, 2, dtype=np.float32) / np.float32(ROPE)), dtype=np.float32)
            for f in range(HALF):
                ins = ve.tensor_scalar(rt[:, 64:96].rearrange("p (i f) -> p i f", f=HALF)[:, :, f], rt[:, 4:8], float(inv[f]), None, ALU.mult)
            clink(ins)
            parts, rest = [], 2.0 * np.pi
            for bits in (8, 8, 8):
                e = np.floor(np.log2(rest)) - (bits - 1)
                parts.append(float(np.floor(rest / 2.0 ** e) * 2.0 ** e))
                rest -= parts[-1]
            parts.append(float(rest))
            BIG = 12582912.0
            clink(ve.tensor_copy(rt[:, 96:128], rt[:, 64:96]))
            for off, shift, last in ((64, 0.0, 0.0), (96, 0.25, float(np.pi / 2))):
                a, k = rt[:, off:off + 32], rt[:, 128:160]
                clink(ve.tensor_scalar(k, a, float(1.0 / (2.0 * np.pi)), shift, ALU.mult, ALU.add))
                clink(ve.tensor_scalar(k, k, BIG, None, ALU.add))
                clink(ve.tensor_scalar(k, k, -BIG, None, ALU.add))
                for part in parts:
                    clink(ve.scalar_tensor_tensor(a, k, -part, a, ALU.mult, ALU.add))
                clink(ve.tensor_scalar(a, a, last, None, ALU.add))
                clink(ve.tensor_scalar(a, a, 3.1415925, -3.1415925, ALU.min, ALU.max))
            ve.sem_inc(dve_const, 1)
            dve.wait_ge(pool_const, 2)
            clink(ve.tensor_tensor(fold[:, :], ident[:, 0:E], ident[:, 32:32 + E], ALU.add))
            clink(ve.tensor_tensor(fold[:, :], fold[:, :], ident[:, 64:64 + E], ALU.add))
            clink(ve.tensor_tensor(fold[:, :], fold[:, :], ident[:, 96:96 + E], ALU.add))
            ve.memset(g16[:, 0:1], 0.0)
            ve.sem_inc(dve_const, 2)
            dve.wait_ge(act_const, 3)
            ve.sem_clear(dve_step)

            with dve.Fori(0, DEPTH) as l:
                n = [0]
                asks = [0]

                def link(ins):
                    n[0] += 1
                    ins.then_inc(dve_step, 1)
                    dve.wait_ge(dve_step, n[0])

                def ask_power():
                    asks[0] += 1
                    ve.sem_inc(pow_ask, 1)
                    dve.wait_ge(pow_done, asks[0])

                dve.wait_ge(param_cols, 1)
                link(ve.tensor_copy(pc[:, :], ps[4][:, 0:P]))
                dve.wait_ge(ffn_sq, NT)
                link(ve.tensor_scalar(ss[:, 0:NT], ss[:, 0:NT], 1.0 / D, EPS, ALU.mult, ALU.add))
                ask_power()
                for i in range(NT):
                    ve.tensor_scalar(xn[:, i, :], xs[:, i, :], rs[:, i:i + 1], None, ALU.mult).then_inc(xn_ready, 1)
                def mod_chunk(j):
                    dve.wait_ge(bc_ready, j + 1)
                    bank = bc_bank(j)
                    if j in (4, 5):
                        h = j - 4
                        link(ve.tensor_tensor(g1bc[:, 512 * h:512 * h + 512], bank[:, :], g1bc[:, 512 * h:512 * h + 512], ALU.add))
                        ve.sem_inc(bc_read, 1)
                    elif j in (10, 11):
                        r = 64 * (j - 10)
                        dve.wait_ge(y_out, 32)
                        link(ve.tensor_tensor(g2bc[r:r + 64, :], bank[r:r + 64, :], g2bc[r:r + 64, :], ALU.add))
                        ve.sem_inc(bc_read, 1)
                    else:
                        dg = diag[j >= HEAD_ADA].rearrange("p (q m) -> p q m", q=4)
                        link(ve.tensor_tensor(dg, bank[:, :].rearrange("p (q m) -> p q m", q=4),
                                              ident[:, :].unsqueeze(1).to_broadcast([P, 4, P]), ALU.mult))
                        ve.sem_inc(bc_read, 1)
                        link(ve.tensor_reduce(modc[:, 4 * j:4 * j + 4], dg, AX.X, ALU.add))
                    if j == 3:
                        link(ve.tensor_tensor(modc[:, 0:16], modc[:, 0:16], pc[:, 60:76], ALU.add))
                        link(ve.scalar_tensor_tensor(A1[:, :], modc[:, 8:16], 1.0, pc[:, 0:8], ALU.add, ALU.mult))
                        ve.sem_inc(mod_ready, 1)
                    if j == 9:
                        link(ve.tensor_tensor(modc[:, 24:40], modc[:, 24:40], pc[:, 84:100], ALU.add))
                        link(ve.scalar_tensor_tensor(A2[:, :], modc[:, 32:40], 1.0, pc[:, 8:16], ALU.add, ALU.mult))

                for j in range(HEAD_ADA):
                    mod_chunk(j)
                ve.memset(conv_u[:, :, 0:3], 0.0)
                ve.tensor_scalar(wmc[:, :], pc[:, 56:60], 0.5, None, ALU.mult)
                link(ve.tensor_scalar(wqk[:, 0, :], wqk[:, 0, :], HD ** -0.5, None, ALU.mult))
                for k in range(0, KD, 2):
                    bank, free = ready(dve, "h1T", k)
                    ve.tensor_scalar(hT[:, k, :], bank[:, :], A1[:, k:k + 1], modc[:, k:k + 1], ALU.mult, ALU.add).then_inc(free, 1)

                nh = HQ + HKV
                for i in range(NT):
                    g = GI[("kv", i)]
                    dve.wait_ge(pj_free[g % 2], g // 2 + 1)
                    dve.wait_ge(pj_free[1 - g % 2], (g - 1) // 2 + 1)
                    qk = qk_rows[:, i, 0:nh * HD].rearrange("p (h n) -> p h n", n=HD)
                    link(ve.tensor_reduce(ssq[:, 0:nh], small[:, 0:nh * HD].rearrange("p (h n) -> p h n", n=HD), AX.X, ALU.add))
                    ve.sem_inc(qk_sq, 1)
                    link(ve.tensor_scalar(ssq[:, 0:nh], ssq[:, 0:nh], 1.0 / HD, EPS, ALU.mult, ALU.add))
                    ask_power()
                    link(ve.tensor_tensor(qk, qk, rsq[:, 0:nh].unsqueeze(2).to_broadcast([P, nh, HD]), ALU.mult))
                    ve.tensor_tensor(qk[:, 0:HQ], qk[:, 0:HQ], wqk[:, 0:1, :].to_broadcast([P, HQ, HD]), ALU.mult)
                    link(ve.tensor_tensor(qk[:, HQ:nh], qk[:, HQ:nh], wqk[:, 1:2, :].to_broadcast([P, HKV, HD]), ALU.mult))
                    t1, t2 = qk[:, :, 0:HALF], qk[:, :, HALF:ROPE]
                    co = cosr[:, i, :].unsqueeze(1).to_broadcast([P, nh, HALF])
                    si = sinr[:, i, :].unsqueeze(1).to_broadcast([P, nh, HALF])
                    r4 = rt[:, 0:4 * nh * HALF].rearrange("p (a h f) -> p a h f", a=4, h=nh)
                    ve.tensor_tensor(r4[:, 0], t1, co, ALU.mult)
                    ve.tensor_tensor(r4[:, 1], t2, si, ALU.mult)
                    ve.tensor_tensor(r4[:, 2], t2, co, ALU.mult)
                    link(ve.tensor_tensor(r4[:, 3], t1, si, ALU.mult))
                    ve.tensor_tensor(t1, r4[:, 0], r4[:, 1], ALU.subtract)
                    link(ve.tensor_tensor(t2, r4[:, 2], r4[:, 3], ALU.add))
                    link(ve.tensor_copy(qk_rows[:, i, 640:768].rearrange("p (a n) -> p a n", a=2), qk_rows[:, i, 576:640].unsqueeze(1).to_broadcast([P, 2, HD])))
                    ve.tensor_copy(qk_rows[:, i, 576:640], qk_rows[:, i, 512:576]).then_inc(qk_ready, 1)

                bank, free = ready(dve, "gates")
                dve.wait_ge(gates_f, 1)
                link(ve.tensor_scalar(rows4[:, 1, :], bank[32:36, :], gbias[32:36, :], None, ALU.add))
                ve.sem_inc(free, 1)
                link(ve.scalar_tensor_tensor(rows4[:, 2, :], rows4[:, 1, :], -1.0, rows4[:, 1, :], ALU.mult, ALU.max))
                ve.sem_inc(gates_f, 1)

                def conv(m):
                    dve.wait_ge(conv_in, m + 1)
                    u = conv_u[:, m % 2, :]
                    z = mqkT[:, m, :]
                    link(ve.tensor_scalar(z, u[:, 0:S], pc[:, 16 + m:17 + m], pc[:, 48 + m:49 + m], ALU.mult, ALU.add))
                    for t in range(1, 4):
                        link(ve.scalar_tensor_tensor(z, u[:, t:t + S], pc[:, 16 + 8 * t + m:17 + 8 * t + m], z, ALU.mult, ALU.add))
                    ve.sem_inc(conv_z, 1)

                def conv_silu(m):
                    dve.wait_ge(conv_t, 2 * m + 1)
                    ve.scalar_tensor_tensor(mqkT[:, m, :], small[:, 0:S], 1.0, mqkT[:, m, :], ALU.add, ALU.mult).then_inc(conv_t, 1)

                def att_max(u):
                    nb_, g = u // HKV, u % HKV
                    lo = 0 if nb_ else P
                    dve.wait_ge(s_ready, u + 1)
                    if u >= 2:
                        dve.wait_ge(pt_ready, u - 1)
                    a = att[:, u % 2, :]
                    for h in range(4):
                        ins = ve.tensor_tensor_reduce(prob[:, u % 2, h, lo:256], att_s[h % 2][:, 256 * (h // 2) + lo:256 * (h // 2) + 256],
                                                      mask[:, lo:256], 1.0, sinkb[:, 4 * g + h:4 * g + h + 1], ALU.add, ALU.max, a[:, h:h + 1])
                    link(ins)
                    ve.sem_inc(s_read, 1)
                    ve.tensor_scalar(a[:, 4:8], a[:, 0:4], -1.0, None, ALU.mult)
                    link(ve.tensor_tensor(a[:, 16:20], sinkb[:, 4 * g:4 * g + 4], a[:, 0:4], ALU.subtract))
                    ve.sem_inc(m_ready, 1)

                def att_norm(u):
                    nb_ = u // HKV
                    lo = 0 if nb_ else P
                    dve.wait_ge(e_ready, u + 1)
                    a = att[:, u % 2, :]
                    link(ve.tensor_tensor(a[:, 8:12], a[:, 8:12], a[:, 12:16], ALU.add))
                    link(ve.reciprocal(a[:, 8:12], a[:, 8:12]))
                    for h in range(4):
                        ins = ve.tensor_scalar(prob[:, u % 2, h, lo:256], prob[:, u % 2, h, lo:256], a[:, 8 + h:9 + h], None, ALU.mult)
                    ins.then_inc(p_norm, 1)

                def att_pt(u):
                    nb_ = u // HKV
                    if nb_:
                        dve.wait_ge(pt_ready, u + 1)
                        if u >= 2:
                            dve.wait_ge(o_ready, u - 1)
                        ve.tensor_copy(pT[:, u % 2, 0, :], att_t[0][:, :]).then_inc(pt_evac, 1)
                    else:
                        ve.sem_inc(pt_evac, 1)

                def gate_rows():
                    lf, b_, mu, nmu = rows4[:, 1, :], rows4[:, 3, :], rows4[:, 4, :], rows4[:, 5, :]
                    dve.wait_ge(gates_f, 4)
                    dve.wait_ge(stack_zero, 1)
                    link(ve.scalar_tensor_tensor(lf, rows4[:, 1, :], 0.0, rows4[:, 2, :], ALU.min, ALU.subtract))
                    ch = [slice(P * i, P * i + P) for i in range(NT)]
                    for t in ch:
                        ins = ve.tensor_tensor_scan(b_[:, t], ones[0:HM, :], lf[:, t], 0.0, ALU.mult, ALU.add)
                    link(ins)
                    a_ = rstack[0:4, :]
                    link(ve.tensor_tensor(a_, rows4[:, 0, :], b_, ALU.subtract))
                    for t in ch:
                        ins = ve.tensor_tensor_scan(mu[:, t], a_[:, t], a_[:, t], NEG, ALU.max, ALU.max)
                    link(ins)
                    last = lambda r: r.rearrange("p (i t) -> p i t", t=P)[:, :, P - 1]
                    bl = g16[:, 8:12]
                    ve.tensor_copy(bl, last(b_))
                    link(ve.tensor_copy(g16[:, 12:16], last(mu)))
                    link(ve.tensor_tensor_scan(g16[:, 1:5], g16[:, 12:16], bl, 0.0, ALU.max, ALU.add))
                    mprev, mnew = g16[:, 0:4], g16[:, 1:5]
                    mp = mprev.unsqueeze(2).to_broadcast([HM, 4, P])
                    v3 = lambda r: r.rearrange("p (i t) -> p i t", t=P)
                    link(ve.tensor_tensor(v3(mu), v3(mu), mp, ALU.max))
                    ve.tensor_scalar(nmu, mu, -1.0, None, ALU.mult)
                    link(ve.tensor_tensor(v3(rstack[32:36, :]), v3(mu), mp, ALU.subtract))
                    link(ve.tensor_scalar(rstack[32:36, :], rstack[32:36, :], -1.0, None, ALU.mult))
                    link(ve.tensor_tensor(g16[:, 16:20], bl, mnew, ALU.subtract))
                    link(ve.tensor_tensor(v3(rstack[64:68, :]), v3(a_), g16[:, 16:20].unsqueeze(2).to_broadcast([HM, 4, P]), ALU.add))
                    link(ve.tensor_tensor(rstack[96:100, :], b_, mu, ALU.add))
                    link(ve.tensor_scalar(rstack[96:100, :], rstack[96:100, :], -1.0, None, ALU.mult))
                    link(ve.tensor_tensor(g16[:, 20:24], g16[:, 16:20], mprev, ALU.add))
                    ve.sem_inc(rows_ready, 1)

                for s in range(16):
                    if s < 8:
                        conv(s)
                    if 1 <= s <= 8:
                        conv_silu(s - 1)
                        mod_chunk(HEAD_ADA + s - 1)
                    if 4 <= s < 12:
                        att_max(s - 4)
                        att_norm(s - 4)
                    if 5 <= s < 13:
                        att_pt(s - 5)
                    if s == 6:
                        gate_rows()
                    if s == 7:
                        dve.wait_ge(rows_zeroed, 16)
                        ve.memset(vaug[:, :, :, DM:DM + 1], 1.0)
                for h in range(HM):
                    bank, free = ready(dve, "mubc", h)
                    link(ve.tensor_tensor(argm[:, h, :].rearrange("p (i t) -> p i t", t=P), bank[:, :].rearrange("p (i t) -> p i t", t=P),
                                          maskT[:, :].unsqueeze(1).to_broadcast([P, NT, P]), ALU.add))
                    ve.sem_inc(free, 1)
                bank, free = ready(dve, "dec")
                link(ve.tensor_copy(decb[:, :, :].rearrange("p h c -> p (h c)"), bank[:, 0:16]))
                ve.sem_inc(free, 1)

                def m_w(u):
                    dve.wait_ge(ma_ready, u + 1)
                    dve.wait_ge(ma_act, u + 1)
                    if u >= 2:
                        dve.wait_ge(mb_ready, u - 1)
                    ve.scalar_tensor_tensor(wS[:, u % 2, :], ps[2 + u % 2][:, P:2 * P], KSCALE, ex[:, u % 2, :], ALU.mult, ALU.mult).then_inc(w_ready, 1)

                def m_state(u):
                    c_, h = u // HM, u % HM
                    dve.wait_ge(mb_ready, u + 1)
                    if c_ == 0:
                        ins = ve.tensor_copy(num[:, h, :], ps[4 + u % 2][:, 0:DM + 1])
                    else:
                        dve.wait_ge(ic_ready, u - HM + 1)
                        ins = ve.tensor_tensor(num[:, h, :], ps[4 + u % 2][:, 0:DM + 1], icb[:, u % 2, :], ALU.add)
                    link(ins)
                    kv = ps[6 + u % 2][:, 0:DM + 1]
                    if c_ == 0:
                        link(ve.tensor_scalar(cst[:, h, :], kv, KSCALE, None, ALU.mult))
                    elif c_ < NT - 1:
                        link(ve.tensor_scalar(cst[:, h, :], cst[:, h, :], decb[:, h, c_:c_ + 1], None, ALU.mult))
                        link(ve.scalar_tensor_tensor(cst[:, h, :], kv, KSCALE, cst[:, h, :], ALU.mult, ALU.add))
                    ve.sem_inc(c_upd, 1)

                def m_finish(c_):
                    den = num[:, :, DM]
                    link(ve.scalar_tensor_tensor(fin[:, 0:4], den, -1.0, den, ALU.mult, ALU.max))
                    link(ve.tensor_tensor(fin[:, 0:4], fin[:, 0:4], colR[:, c_, 3, :], ALU.max))
                    link(ve.reciprocal(fin[:, 0:4], fin[:, 0:4]))
                    hv = num[:, :, 0:DM]
                    link(ve.tensor_tensor(hv, hv, fin[:, 0:4].unsqueeze(2).to_broadcast([P, HM, DM]), ALU.mult))
                    for h in range(HM):
                        ins = ve.tensor_tensor_reduce(sqs, num[:, h, 0:DM], num[:, h, 0:DM], 1.0, 0.0, ALU.mult, ALU.add, fin[:, 4 + h:5 + h])
                        link(ins)
                    link(ve.tensor_scalar(fin[:, 4:8], fin[:, 4:8], 1.0 / DM, EPS, ALU.mult, ALU.add))
                    ask_power()
                    mo = mo_t[:, c_, :].rearrange("p (h n) -> p h n", h=HM)
                    link(ve.tensor_scalar(mo, mo, 1.0, None, ALU.add))
                    link(ve.tensor_tensor(mo, mo, hv, ALU.mult))
                    ve.tensor_tensor(mo, mo, fin[:, 8:12].unsqueeze(2).to_broadcast([P, HM, DM]), ALU.mult).then_inc(hm_ready, 1)

                ve.memset(fin[:, :], 0.0)
                for j in range(8):
                    for u in (2 * j, 2 * j + 1):
                        m_w(u)
                        if u >= 1:
                            m_state(u - 1)
                            if u % HM == 0:
                                m_finish(u // HM - 1)
                    bank, free = ready(dve, "ya", j)
                    g = GI[("ga", j)]
                    dve.wait_ge(pj_free[g % 2], g // 2 + 1)
                    ve.scalar_tensor_tensor(merged[:, j, :], merged[:, j, :], 1.0, bank[:, :], ALU.add, ALU.mult).then_inc(free, 1)
                m_state(15)
                m_finish(NT - 1)
                for i in range(NT):
                    bank, free = ready(dve, "hmT", i)
                    ve.tensor_tensor(hmT[:, :, P * i:P * i + P], bank[:, :].rearrange("p (h t) -> p h t", h=HM),
                                     wmc[:, :].unsqueeze(2).to_broadcast([P, HM, P]), ALU.mult).then_inc(free, 1)
                for j in range(8):
                    bank, free = ready(dve, "yb", j)
                    g = GI[("gb", j)]
                    dve.wait_ge(pj_free[g % 2], g // 2 + 1)
                    link(ve.scalar_tensor_tensor(tb[:, j % 2, :], tb[:, j % 2, :], 1.0, bank[:, :], ALU.add, ALU.mult))
                    ve.sem_inc(free, 1)
                    ve.sem_inc(tb_sum, 1)
                for i in range(NT):
                    for h in range(2):
                        bank, free = ready(dve, "wo", 2 * i + h)
                        link(ve.scalar_tensor_tensor(regP[:, 0:512], bank[:, :], 0.5, g1bc[:, 512 * h:512 * h + 512], ALU.mult, ALU.mult))
                        ve.sem_inc(free, 1)
                        link(ve.tensor_tensor(xs[:, i, 512 * h:512 * h + 512], xs[:, i, 512 * h:512 * h + 512], regP[:, 0:512], ALU.add))
                    ve.sem_inc(x_upd, 1)
                    dve.wait_ge(ffn_sq, NT + i + 1)
                    link(ve.tensor_scalar(ss[:, 4 + i:5 + i], ss[:, 4 + i:5 + i], 1.0 / D, EPS, ALU.mult, ALU.add))
                    ask_power()
                    ve.tensor_scalar(xn[:, i, :], xs[:, i, :], rs[:, 4 + i:5 + i], None, ALU.mult).then_inc(xn_ready, 1)
                for k in range(0, KD, 2):
                    bank, free = ready(dve, "h2T", k)
                    ve.tensor_scalar(hT[:, k, :], bank[:, :], A2[:, k:k + 1], modc[:, 24 + k:25 + k], ALU.mult, ALU.add).then_inc(free, 1)

                g = GI[("lg", 0)]
                dve.wait_ge(pj_free[g % 2], g // 2 + 1)
                NS = NT * E
                r = lambda a, w: rt[:, a:a + w]
                s_, sel = r(0, 64), r(64, 64)
                link(ve.tensor_scalar(s_, s_, 1.0, None, ALU.add))
                link(ve.reciprocal(s_, s_))
                link(ve.tensor_tensor(sel.rearrange("p (i e) -> p i e", e=E), s_.rearrange("p (i e) -> p i e", e=E),
                                      rbias[:, :].unsqueeze(1).to_broadcast([P, NT, E]), ALU.add))
                v4 = sel.rearrange("p (g j) -> p g j", j=EG)
                hi1, hi2, lo1, lo2 = (r(128 + 16 * q, 16) for q in range(4))
                ve.tensor_tensor(hi1, v4[:, :, 0], v4[:, :, 1], ALU.max)
                ve.tensor_tensor(lo1, v4[:, :, 0], v4[:, :, 1], ALU.min)
                ve.tensor_tensor(hi2, v4[:, :, 2], v4[:, :, 3], ALU.max)
                link(ve.tensor_tensor(lo2, v4[:, :, 2], v4[:, :, 3], ALU.min))
                m1, mn, ml = r(192, 16), r(208, 16), r(224, 16)
                ve.tensor_tensor(m1, hi1, hi2, ALU.max)
                ve.tensor_tensor(mn, hi1, hi2, ALU.min)
                link(ve.tensor_tensor(ml, lo1, lo2, ALU.max))
                link(ve.tensor_tensor(mn, mn, ml, ALU.max))
                gs = r(240, 16)
                link(ve.tensor_tensor(gs, m1, mn, ALU.add))

                def first_max(one, val, tmp, red):
                    v = val.rearrange("p (i g) -> p i g", g=4)
                    o = one.rearrange("p (i g) -> p i g", g=4)
                    t = tmp.rearrange("p (i g) -> p i g", g=4)
                    io = iog[:, :].unsqueeze(1).to_broadcast([P, NT, 4])
                    link(ve.tensor_reduce(red, v, AX.X, ALU.max))
                    link(ve.tensor_tensor(t, v, red.unsqueeze(2).to_broadcast([P, NT, 4]), ALU.is_equal))
                    link(ve.tensor_tensor(t, t, io, ALU.mult))
                    link(ve.tensor_reduce(red, t, AX.X, ALU.min))
                    link(ve.tensor_tensor(o, io, red.unsqueeze(2).to_broadcast([P, NT, 4]), ALU.is_equal))

                og, tmp, red, ing, o1, o2 = r(256, 16), r(272, 16), r(288, 4), r(292, 16), r(308, 16), r(324, 16)
                first_max(og, gs, tmp, red)
                big = r(340, 64)
                link(ve.tensor_tensor(big.rearrange("p (g j) -> p g j", j=EG), v4, og.unsqueeze(2).to_broadcast([P, NT * NG, EG]), ALU.mult))
                link(ve.tensor_reduce(ing.rearrange("p (i j) -> p i j", j=EG), big.rearrange("p (i g j) -> p i j g", g=NG, j=EG), AX.X, ALU.add))
                first_max(o1, ing, tmp, red)
                link(ve.scalar_tensor_tensor(ing, o1, NEG, ing, ALU.mult, ALU.add))
                first_max(o2, ing, tmp, red)
                E1, E2 = r(404, 64), r(468, 64)
                for Ek, ok in ((E1, o1), (E2, o2)):
                    for i in range(NT):
                        ins = ve.tensor_tensor(Ek[:, E * i:E * i + E].rearrange("p (g j) -> p g j", j=EG),
                                               og[:, 4 * i:4 * i + 4].unsqueeze(2).to_broadcast([P, NG, EG]),
                                               ok[:, 4 * i:4 * i + 4].unsqueeze(1).to_broadcast([P, NG, EG]), ALU.mult)
                link(ins)
                link(ve.tensor_tensor(Mb[:, :, :].rearrange("p i e -> p (i e)"), E1, E2, ALU.add))
                for k, Ek in enumerate((E1, E2)):
                    link(ve.tensor_tensor(big, s_, Ek, ALU.mult))
                    link(ve.tensor_reduce(wsel[:, k, :], big.rearrange("p (i e) -> p i e", e=E), AX.X, ALU.add))
                link(ve.tensor_tensor(red, wsel[:, 0, :], wsel[:, 1, :], ALU.add))
                link(ve.reciprocal(red, red))
                link(ve.tensor_tensor(wsel[:, :, :], wsel[:, :, :], red.unsqueeze(1).to_broadcast([P, 2, NT]), ALU.mult))
                ve.sem_inc(routed, 1)
                bank, free = ready(dve, "rank")
                cmp, nbk, cum, base = r(532, 112), r(644, 16), r(660, 16), r(676, 16)
                cnt = r(692, 80)
                link(ve.tensor_copy(cnt, bank[:, 0:80]))
                link(ve.tensor_tensor(cmp.rearrange("p (e k) -> p e k", k=7), cnt[:, 64:80].unsqueeze(2).to_broadcast([P, E, 7]),
                                      thr[:, :].unsqueeze(1).to_broadcast([P, E, 7]), ALU.is_gt))
                link(ve.tensor_reduce(nbk, cmp.rearrange("p (e k) -> p e k", k=7), AX.X, ALU.add))
                link(ve.tensor_scalar(nbk, nbk, 1.0, None, ALU.add))
                link(ve.tensor_tensor_scan(cum, ones[:, 0:E], nbk, 0.0, ALU.mult, ALU.add))
                link(ve.tensor_tensor(base, cum, nbk, ALU.subtract))
                link(ve.tensor_scalar(base, base, float(MB), None, ALU.mult))
                link(ve.tensor_tensor(cnt[:, 0:64].rearrange("p (i e) -> p i e", e=E), cnt[:, 0:64].rearrange("p (i e) -> p i e", e=E),
                                      base.unsqueeze(1).to_broadcast([P, NT, E]), ALU.add))
                for k, Ek in enumerate((E1, E2)):
                    link(ve.tensor_tensor(big, cnt[:, 0:64], Ek, ALU.mult))
                    link(ve.tensor_reduce(red, big.rearrange("p (i e) -> p i e", e=E), AX.X, ALU.add))
                    link(ve.tensor_copy(slot_u[:, k, :], red))
                ve.sem_inc(routed, 1)
                tb32 = rt[0:1, 0:512]
                link(ve.tensor_tensor(tb32.rearrange("p (b e) -> p b e", e=E), cum[0:1, :].unsqueeze(1).to_broadcast([1, 32, E]),
                                      ioe[:, :].unsqueeze(2).to_broadcast([1, 32, E]), ALU.is_le))
                link(ve.tensor_reduce(rt[0:1, 512:544], tb32.rearrange("p (b e) -> p b e", e=E), AX.X, ALU.add))
                ve.tensor_copy(tabs[0:1, 0:32], rt[0:1, 512:544])
                ve.tensor_copy(tabs[0:1, 32:48], cum[0:1, :])
                link(ve.tensor_scalar(tabs[0:1, 48:49], cum[0:1, E - 1:E], 1.0, None, ALU.subtract))
                ve.sem_inc(tables, 1)

                nb = ve.value_load(tabs[0:1, 47:48], min_val=E, max_val=MAXB)
                nb1 = ve.value_load(tabs[0:1, 48:49], min_val=E - 1, max_val=MAXB - 1)

                def xt_dve():
                    for k in range(1, KD, 2):
                        last = ve.tensor_scalar(xT[:, k, :], ps[6][:, MB * k:MB * k + MB], A2[:, k:k + 1], modc[:, 24 + k:25 + k], ALU.mult, ALU.add)
                    last.then_inc(xt_evac_d, 1)

                def y_row():
                    ve.tensor_tensor(yb, ps[5][:, :], g2bc[:, :], ALU.mult).then_inc(y_taken, 1)

                ve.sem_inc(y_taken, 1)
                dve.wait_ge(xt_ready, 1)
                xt_dve()
                dve.wait_ge(sil_ready, 1)
                ve.tensor_tensor(hx, ps[3][64:P, :], hsil[64:P, :], ALU.mult).then_inc(hx_ready, 1)
                dve.wait_ge(xt_ready, 2)
                xt_dve()
                with dve.Fori(0, nb1) as b:
                    dve.wait_ge(sil_ready, b + 2)
                    dve.wait_ge(ht_ready, b + 1)
                    ve.tensor_tensor(hx, ps[3][64:P, :], hsil[64:P, :], ALU.mult).then_inc(hx_ready, 1)
                    dve.wait_ge(xt_ready, b + 3)
                    xt_dve()
                    dve.wait_ge(y_ready, b + 1)
                    dve.wait_ge(y_out, b * 32 + 32)
                    y_row()
                dve.wait_ge(y_ready, nb)
                dve.wait_ge(y_out, nb * 32)
                y_row()
                for i in range(NT):
                    dve.wait_ge(yg_in[i], l * 32 + 32)
                    for k in range(2):
                        link(ve.scalar_tensor_tensor(xs[:, i, :], yg[:, i, k, :], wsel[:, k, i:i + 1], xs[:, i, :], ALU.mult, ALU.add))
                layer_end(dve, l, share(4))


def program(nc, args):
    trunk(nc, *args)


_INS = ["x", "c", "positions", "ada_w", "ada_b", "norm_mix_w", "norm_ffn_w", "w_in", "b_igate", "b_fgate",
        "q_norm_w", "k_norm_w", "sinks", "conv_w", "conv_b", "mlstm_norm_w", "w_attn_up", "w_mlstm_up",
        "w_out", "router_w", "router_bias", "w_gate", "w_up", "w_down"]


def kernel(**inputs):
    import concourse.bacc as _bacc
    from concourse.bass_utils import run_bass_kernel_spmd as _run

    nc = _bacc.Bacc("TRN2", target_bir_lowering=False, num_devices=1)
    arrays, args = {}, []
    for name in _INS:
        a = np.ascontiguousarray(inputs[name])
        arrays[f"in_{name}_dram"] = a
        args.append(nc.dram_tensor(f"in_{name}_dram", a.shape, mybir.dt.from_np(a.dtype), kind="ExternalInput").ap())
    args.append(nc.dram_tensor("out_0_dram", inputs["x"].shape, F32, kind="ExternalOutput").ap())
    program(nc, args)
    r = _run(nc, [arrays], core_ids=[0])
    return r.results[0]["out_0_dram"]
```

```python
from contextlib import ExitStack

import numpy as np

import concourse.bass as bass
from concourse import mybir

ALU = mybir.AluOpType
ACT = mybir.ActivationFunctionType
F32 = mybir.dt.float32
BF16 = mybir.dt.bfloat16
I32 = mybir.dt.int32
U32 = mybir.dt.uint32
AX = mybir.AxisListType

P = 128
NEG = -1.0e30
THETA = 500000.0
EPS = 1e-6
MB = 64
RING = 6
BUF = 3
HEAD_ADA = 4
G2_ADA = 10
MID_ADA = {1: 4, 2: 5, 3: 6, 4: 7, 5: 8, 6: 9}

def group_order(NT, NH, HM):
    o = [("h1T", k) for k in range(8)]
    for i in range(NT):
        o += [("q", i), ("kv", i)]
    o += [("gates", 0)]
    for m in range(8):
        o += [("mqk", m)]
        if m == 0:
            o += [("gsum", 0)]
        if 1 <= m <= NT:
            o += [("qT", m - 1), ("kT", m - 1)]
    o += [("mv", i) for i in range(NT)]
    o += [("mo", i) for i in range(NT)]
    o += [("rT", 0)] + [("mubc", h) for h in range(HM)] + [("dec", 0)]
    for j in range(8):
        o += [("ga", j), ("ya", j)]
    o += [("gb", 0), ("gb", 1)]
    o += [("hmT", i) for i in range(NT)]
    for j in range(8):
        if j >= 2:
            o += [("gb", j)]
        o += [("yb", j)]
        if j - 1 in MID_ADA:
            o += [("ada", MID_ADA[j - 1])]
    for i in range(NT):
        o += [("wo", 2 * i), ("wo", 2 * i + 1)]
    o += [("ada", G2_ADA)]
    o += [("h2T", k) for k in range(8)]
    o += [("rl", 0), ("lg", 0), ("ada", G2_ADA + 1), ("rank", 0)]
    return {name: n for n, name in enumerate(o)}


def trunk(nc, x, c, positions, ada_w, ada_b, norm_mix_w, norm_ffn_w, w_in, b_igate, b_fgate,
          q_norm_w, k_norm_w, sinks, conv_w, conv_b, mlstm_norm_w, w_attn_up, w_mlstm_up, w_out,
          router_w, router_bias, w_gate, w_up, w_down, out):
    _, S, D = x.shape
    DEPTH = ada_w.shape[0]
    NT = S // P
    KD = D // P
    HD = q_norm_w.shape[1]
    HQ = sinks.shape[1]
    HKV = HQ // 4
    ROPE = HD // 4
    HALF = ROPE // 2
    HM = b_igate.shape[1]
    DM = 128
    E = router_w.shape[1]
    NG = 4
    EG = E // NG
    F = w_gate.shape[3]
    FC = F // P
    assert (S, D, HD, HQ, HM, E, F) == (512, 1024, 64, 8, 4, 16, 512)
    MAXB = (2 * S + E * (MB - 1)) // MB
    ROWS = ((MAXB + 3) * MB + P - 1) // P * P
    AQ, AK, MQK, MV, MI, MF, MO, GA, GB = 0, 512, 768, 1792, 2304, 2308, 2312, 2824, 3848
    assert GB + D == w_in.shape[2]
    GI = group_order(NT, HM, HM)
    KSCALE = DM ** -0.5 / 4.0

    xd = nc.dram_tensor("expert_rows", [ROWS, D], F32).ap()

    with ExitStack() as ctx:
        def sb(name, shape, dt=F32):
            return ctx.enter_context(nc.sbuf_tensor(name, shape, dt))

        ring = sb("weight_ring", [P, RING, 4096])
        xs = sb("x_tokens", [P, NT, D])
        regA = sb("regA", [P, NT * D])
        hT = sb("h_features", [P, KD, S])
        regB = sb("regB", [P, 6 * S])
        regP = sb("regP", [P, 2 * 2 * 512])
        regU = sb("regU", [P, 2 * 516])
        vaug = sb("mlstm_v_and_one", [P, NT, HM, DM + 1])
        merged = sb("merged_features", [P, KD, S])

        xn = regA[:, :].rearrange("p (i d) -> p i d", i=NT)
        qk_rows = regA[:, 0:NT * 768].rearrange("p (i n) -> p i n", i=NT)
        attn_o = regA[:, 0:4 * S].rearrange("p (c t) -> p c t", c=4)
        rstack = regA[:, NT * 896:NT * 896 + S]
        v_rows = regA[:, NT * 768:NT * 768 + NT * P].rearrange("p (i n) -> p i n", i=NT)
        qkT = regB[:, :].rearrange("p (c t) -> p c t", c=6)
        hmT = regB[:, 0:4 * S].rearrange("p (c t) -> p c t", c=4)
        num = regB[:, 4 * S:4 * S + HM * (DM + 1)].rearrange("p (h n) -> p h n", h=HM)
        pT = regP[:, :].rearrange("p (b k n) -> p b k n", b=2, k=2)
        ke = regP[:, 0:256].rearrange("p (b n) -> p b n", b=2)
        ex = regP[:, 256:512].rearrange("p (b n) -> p b n", b=2)
        wS = regP[:, 512:768].rearrange("p (b n) -> p b n", b=2)
        icb = regP[:, 768:768 + 2 * (DM + 1)].rearrange("p (b n) -> p b n", b=2)
        cst = regP[:, 1028:1028 + HM * (DM + 1)].rearrange("p (h n) -> p h n", h=HM)
        sqs = regP[:, 1544:1544 + 128]
        prm = regP[:, 1024:1024 + P]
        crow = regP[0:KD, 1024 + P:1024 + 2 * P]
        rt = regP[:, 0:1024]
        mqkT = ring[:, 4, :].rearrange("p (m t) -> p m t", m=KD)
        prob = ring[:, 5, 0:2048].rearrange("p (b h n) -> p b h n", b=2, h=4)
        argm = ring[:, 5, 0:2048].rearrange("p (h t) -> p h t", h=HM)
        mo_t = ring[:, 5, 2048:4096].rearrange("p (i n) -> p i n", i=NT)
        conv_u = regU[:, :].rearrange("p (b n) -> p b n", b=2)
        tb = regU[:, 0:1024].rearrange("p (b n) -> p b n", b=2)
        gate_parts = regU[:, 519:519 + S]
        mflat = merged[:, :, :].rearrange("p a b -> p (a b)")
        small = mflat[:, 0:D]
        squares = hT[:, 0:2, :].rearrange("p a b -> p (a b)")
        head_squares = mflat[:, 1024:2048]
        xg = [mflat[0:MB, 0:D], mflat[MB:2 * MB, 0:D]]
        xT = mflat[:, 1024:1024 + KD * MB].rearrange("p (k r) -> p k r", k=KD)
        hsil = mflat[:, 1536:2048]
        hx = mflat[0:MB, 2048:2560]
        hxT = mflat[:, 2560:2560 + FC * MB].rearrange("p (k r) -> p k r", k=FC)
        yb = mflat[:, 3072:3584]
        zeros = vaug[:, :, :, :].rearrange("p a b c -> p (a b c)")[:, 0:D]
        rows4 = mflat[0:HM, D:D + 6 * S].rearrange("p (r t) -> p r t", r=6)
        yg = [hT[:, :, :].rearrange("p a b -> p (a b)").rearrange("p (i d) -> p i d", i=NT), xn]
        vflat = vaug[:, :, :, :].rearrange("p a b c -> p (a b c)")
        as8 = lambda ap: ap.rearrange("p (k n) -> p k n", k=KD)
        gate_w = [as8(ring[:, 0, :]), as8(ring[:, 3, :]), hT[:, :, :]]
        up_w = [as8(ring[:, 1, :]), as8(ring[:, 4, :]), as8(regA[:, :])]
        down_w = [[ring[:, s, D * k:D * k + D] for k in range(FC)] for s in (2, 5)]
        down_w.append([regB[:, D * k:D * k + D] for k in range(FC - 1)] + [vflat[:, 0:D]])
        mrow = regU[:, 0:1024].rearrange("p (b n) -> p b n", b=2)
        mid_sum = regP[:, 512:1024]

        ident = sb("ident", [P, P])
        ones = sb("ones", [P, P])
        onesb = sb("ones_bf16", [P, P], BF16)
        triu = sb("strictly_before_bf16", [P, P], BF16)
        mask = sb("window_mask", [P, 256])
        maskT = sb("causal_mask_T", [P, P])
        fold = sb("fold16", [P, E])
        cz = sb("c_padded", [P, KD, 32])
        rwz = sb("router_padded", [P, KD, 32])
        cosr = sb("cos", [P, NT, HALF])
        sinr = sb("sin", [P, NT, HALF])
        rbias = sb("router_bias", [P, E])
        thr = sb("block_thresholds", [P, 7])
        iog = sb("iota_minus", [P, 4])
        ioe = sb("block_iota", [1, 32])
        nhalf = sb("minus_half", [P, 16])
        pc = sb("param_cols", [P, P])
        modc = sb("mod_cols", [P, 48])
        A1 = sb("scale1", [P, KD])
        A2 = sb("scale2", [P, KD])
        wmc = sb("mlstm_norm_half", [P, HM])
        g1bc = sb("g1_rows", [P, D])
        g2bc = sb("g2_rows", [P, 512])
        wqk = sb("qk_norm_rows", [P, 2, HD])
        gbias = sb("gate_bias", [36, 1])
        sinkb = sb("sinks", [P, HQ])
        wgz = sb("gate_columns_padded", [P, KD, 32])
        fold36 = sb("fold36", [P, 36])
        ss = sb("sum_sq", [P, 16])
        rs = sb("rstd", [P, 16])
        ssq = sb("sum_sq_qk", [P, 16])
        rsq = sb("rstd_qk", [P, 16])
        att = sb("att_small", [P, 2, 32])
        g16 = sb("gate_small", [HM, 40])
        colR = sb("gate_cols", [P, NT, 4, HM])
        decb = sb("decay", [P, HM, 4])
        fin = sb("fin_small", [P, 32])
        Mb = sb("assigned_bf16", [P, NT, E], BF16)
        slot_u = sb("slot_index", [P, 2, NT], U32)
        wsel = sb("gate_weights", [P, 2, NT])
        tabs = sb("block_tables", [1, 64], I32)

        ps = [ctx.enter_context(nc.psum_tensor(f"bank{b}", [P, 512], F32)) for b in range(8)]
        pj = ps[0:2]
        att_s = [ps[2], ps[3]]
        att_t = [ps[4], ps[5]]

        cleared = []

        def lsem(name):
            s = ctx.enter_context(nc.semaphore(name))
            cleared.append(s)
            return s

        def gsem(name):
            return ctx.enter_context(nc.semaphore(name))

        const_in, pool_const, dve_const, act_const = (gsem(n) for n in (
            "const_in", "pool_const", "dve_const", "act_const"))
        zeroed, rows_zeroed, c_cols, x_in, meet_a, meet_b = (gsem(n) for n in (
            "zeroed", "rows_zeroed", "c_cols", "x_in", "meet_a", "meet_b"))
        params_in, scattered = gsem("params_in"), gsem("scattered")
        head_in = [gsem(f"head_in{n}") for n in range(HEAD_ADA)]
        head_sum, head_row, head_bc, head_read, param_cols, mod_ready = (gsem(n) for n in (
            "head_sum", "head_row", "head_bc", "head_read", "param_cols", "mod_ready"))
        head_sq, head_ask, head_pow, head_xn, head_step = (gsem(n) for n in (
            "head_sq", "head_ask", "head_pow", "head_xn", "head_step"))
        yg_in = [gsem(f"yg_in{i}") for i in range(NT)]
        w_dn = [gsem(f"w_down{p}") for p in range(BUF)]
        HELD = [len(range(p, E, BUF)) for p in range(BUF)]
        ring_in = [lsem(f"ring_in{s}") for s in range(RING)]
        xg_in, y_out = [lsem("xg_in0"), lsem("xg_in1")], lsem("y_out")
        pj_ready, mid_ready = lsem("pj_ready"), lsem("mid_ready")
        pj_free = [lsem("pj_free0"), lsem("pj_free1")]
        mrow_ready, bc_ready, bc_read = (lsem(n) for n in ("mrow_ready", "bc_ready", "bc_read"))
        dve_step, pow_ask, pow_done = (lsem(n) for n in ("dve_step", "pow_ask", "pow_done"))
        xn_ready, qk_ready, qk_sq = lsem("xn_ready"), lsem("qk_ready"), lsem("qk_sq")
        s_ready, s_read, m_ready, e_ready, p_norm, pt_ready, pt_evac, o_ready, o_evac = (lsem(n) for n in (
            "s_ready", "s_read", "m_ready", "e_ready", "p_norm", "pt_ready", "pt_evac", "o_ready", "o_evac"))
        rows_ready = lsem("rows_ready")
        gates_f, stack_zero = lsem("gates_f"), lsem("stack_zero")
        ma_ready, ma_act, w_ready, mb_ready, ic_ready, c_upd, hm_ready = (lsem(n) for n in (
            "ma_ready", "ma_act", "w_ready", "mb_ready", "ic_ready", "c_upd", "hm_ready"))
        tb_sum, merged_ready, x_upd, ffn_sq = (lsem(n) for n in ("tb_sum", "merged_ready", "x_upd", "ffn_sq"))
        conv_in, conv_z, conv_t = lsem("conv_in"), lsem("conv_z"), lsem("conv_t")
        routed, tables, combined = lsem("routed"), lsem("tables"), lsem("combined")
        xt_ready, xt_evac_a, xt_evac_d, gu_ready, sil_ready, hx_ready, ht_ready, ht_evac, y_ready, y_taken = (
            lsem(n) for n in ("xt_ready", "xt_evac_a", "xt_evac_d", "gu_ready", "sil_ready", "hx_ready",
                              "ht_ready", "ht_evac", "y_ready", "y_taken"))
        w_gu = [lsem(f"w_gate_up{p}") for p in range(BUF)]
        DN = (16, 16, 32)
        out_done, passed = gsem("out_done"), gsem("passed")

        def lay(ap, l):
            return ap[bass.ds(l, 1)]

        def cols8(w, l, c0, n):
            return lay(w, l)[:, :, c0:c0 + n].rearrange("a (k p) n -> p (a k) n", p=P)

        ITEMS = [("ada", j, (3, 4, 5, 0)[j], ("ada", j)) for j in range(HEAD_ADA)]
        ITEMS += [("q", 0, 1, ("q", NT - 1)), ("kv", 0, 2, ("kv", NT - 1)), ("mqk", 0, 3, ("mqk", 3)),
                  ("mqk", 1, 0, ("mqk", 7)), ("mv", 0, 1, ("mv", NT - 1)), ("mo", 0, 2, ("mo", NT - 1)),
                  ("ga", 0, 3, ("ga", 3)), ("ga", 1, 0, ("ga", 7)), ("ya", 0, 1, ("ya", 7)),
                  ("yb", 0, 2, ("yb", 7)), ("gb", 0, 3, ("gb", 3)), ("gb", 1, 0, ("gb", 7)), ("wo", 0, 1, ("wo", 2 * NT - 1)),
                  ("ada", 4, 4, ("ada", 4)), ("ada", 5, 5, ("ada", 5)), ("ada", 6, 4, ("ada", 6)), ("ada", 7, 5, ("ada", 7)),
                  ("ada", 8, 4, ("ada", 8)), ("ada", 9, 5, ("ada", 9)), ("wo", 1, 4, ("wo", 2 * NT - 1)), ("ada", 10, 5, ("ada", 10))]
        LATE = [("ada", 11, 5, ("ada", 11))]
        FREE = {4: ("hmT", NT - 1), 5: ("hmT", NT - 1)}
        N_ITEMS = len(ITEMS)
        ITEMS += LATE
        ITEM = {(name, part): n for n, (name, part, _, _) in enumerate(ITEMS)}
        COLS = {"q": (AQ, 512), "kv": (AK, 256), "mqk": (MQK, 512), "mv": (MV, 512), "mo": (MO, 512), "ga": (GA, 512), "gb": (GB, 512)}
        HEAD = HEAD_ADA

        def mix_item(l, n):
            name, part = ITEMS[n][:2]
            if name == "ada":
                return cols8(ada_w, l, 512 * part, 512), 512, 8
            if name in COLS:
                c0, w = COLS[name]
                return cols8(w_in, l, c0 + 512 * part, w), w, 8
            if name == "wo":
                return lay(w_out, l)[:, 512 * part:512 * part + 512, :].rearrange("a (k p) n -> p (a k) n", p=P), D, 4
            return cols8({"ya": w_attn_up, "yb": w_mlstm_up}[name], l, 0, D), D, 4

        def slot(name, part, k, w):
            return ring[:, ITEMS[ITEM[(name, part)]][2], 0:k * w].rearrange("p (k n) -> p k n", k=k)

        def before(n):
            return [it[2] for it in ITEMS[:n]].count(ITEMS[n][2])

        def of(w, l, e):
            return w.rearrange("l e (k p) f -> (l e) p k f", p=P)[bass.ds(l * E + e, 1)].rearrange("a p k f -> p (a k) f")

        def blocks_through(eng, e):
            return eng.value_load(tabs[0:1, bass.ds(e + 32, 1)], min_val=1, max_val=MAXB)

        def load_item(sp, l, n, sem):
            src, w, k = mix_item(l, n)
            sp.dma_start(slot(ITEMS[n][0], ITEMS[n][1], k, w), src).then_inc(sem, 16)

        def through(eng, name, part):
            eng.wait_ge(pj_ready, GI[ITEMS[ITEM[(name, part)]][3]] + 1)

        def arrived(eng, name, part):
            n = ITEM[(name, part)]
            if n >= HEAD:
                eng.wait_ge(ring_in[ITEMS[n][2]], 16 * [it[2] for it in ITEMS[HEAD:n + 1]].count(ITEMS[n][2]))

        def bc_bank(j):
            return {G2_ADA: ps[7], G2_ADA + 1: ps[5]}.get(j, ps[2 + j % 2])

        def ready(eng, name, i=0):
            g = GI[(name, i)]
            eng.wait_ge(pj_ready, g + 1)
            return pj[g % 2], pj_free[g % 2]

        def wait_reg(eng, sem, value):
            eng.wait_ge(sem, value)
            eng.sem_inc(passed, 1)

        def wait_head(eng, sem, t, each, k):
            if isinstance(t, int):
                eng.wait_ge(sem, t * each + k)
            else:
                wait_reg(eng, sem, t * each + k)

        def layer_end(eng, l, mine):
            eng.sem_inc(meet_a, 1)
            wait_reg(eng, meet_a, l * 5 + 5)
            for s in mine:
                eng.sem_clear(s)
            eng.sem_inc(meet_b, 1)
            wait_reg(eng, meet_b, l * 5 + 5)

        def share(n):
            return cleared[n::5]

        block = ctx.enter_context(nc.Block())

        @block.sync
        def _(sp):
            def params(l):
                def rows(dst, src):
                    sp.dma_start(dst, src).then_inc(params_in, 16)

                rows(prm[0:8, :], lay(norm_mix_w, l).rearrange("a (k p) -> (a k) p", p=P))
                rows(prm[8:16, :], lay(norm_ffn_w, l).rearrange("a (k p) -> (a k) p", p=P))
                rows(prm[16:48, :], lay(conv_w, l).rearrange("a j (m p) -> (a j m) p", p=P))
                rows(prm[48:56, :], lay(conv_b, l).rearrange("a (m p) -> (a m) p", p=P))
                rows(prm[56:60, :], lay(mlstm_norm_w, l).rearrange("a (m p) -> (a m) p", p=P))
                rows(prm[60:108, :], lay(ada_b, l).rearrange("a (m p) -> (a m) p", p=P))
                rows(g1bc[:, :], lay(ada_b, l)[:, 2 * D:3 * D].to_broadcast([P, D]))
                rows(wqk[:, 0, :], lay(q_norm_w, l).to_broadcast([P, HD]))
                rows(wqk[:, 1, :], lay(k_norm_w, l).to_broadcast([P, HD]))
                rows(sinkb[:, :], lay(sinks, l).to_broadcast([P, HQ]))
                with nc.allow_non_contiguous_dma(reason="gate columns and biases"):
                    rows(gbias[0:4, :], lay(b_igate, l).rearrange("a h -> h a"))
                    rows(gbias[32:36, :], lay(b_fgate, l).rearrange("a h -> h a"))
                    rows(wgz[:, :, 0:4], cols8(w_in, l, MI, 4))
                    rows(wgz[:, :, 4:8], cols8(w_in, l, MF, 4))

            sp.dma_start(crow, c.rearrange("a (k p) -> (a k) p", p=P)).then_inc(const_in, 16)
            with nc.allow_non_contiguous_dma(reason="positions by token"):
                sp.dma_start(rt[:, 0:NT].bitcast(I32), positions.rearrange("a (i p) -> p (a i)", p=P)).then_inc(const_in, 16)
            sp.dma_start(rbias[:, :], router_bias.rearrange("(a e) -> a e", a=1).to_broadcast([P, E])).then_inc(const_in, 16)
            load_item(sp, 0, 0, head_in[0])
            sp.wait_ge(zeroed, 2)
            sp.dma_start(rwz[:, :, 0:E], router_w.rearrange("(k p) e -> p k e", p=P)).then_inc(const_in, 16)
            params(0)
            sp.dma_start(xs[:, :, :], x.rearrange("a (i p) d -> p (a i) d", p=P)).then_inc(x_in, 16)
            for n in range(1, HEAD):
                load_item(sp, 0, n, head_in[n])

            with sp.Fori(0, DEPTH) as l:
                nxt = nc.s_assert_within(l + 1, 1, DEPTH - 1, skip_runtime_bounds_check_because="used where l < DEPTH - 1 only")
                sp.dma_start(g2bc[0:64, :], lay(ada_b, l)[:, 5 * D:5 * D + 512].to_broadcast([64, 512])).then_inc(y_out, 16)
                sp.dma_start(g2bc[64:P, :], lay(ada_b, l)[:, 5 * D + 512:6 * D].to_broadcast([64, 512])).then_inc(y_out, 16)
                def load_next(n):
                    at = ITEMS[n][2]
                    if before(n):
                        prev = [m for m in range(n) if ITEMS[m][2] == at][-1]
                        if prev < HEAD:
                            wait_reg(sp, head_sum, l * HEAD_ADA + HEAD_ADA)
                        g = GI.get(ITEMS[prev][3], 0)
                        sp.wait_ge(pj_ready, max(g, GI[FREE[at]] if at in FREE else 0) + 1)
                    load_item(sp, l, n, ring_in[at])

                for n in range(HEAD, N_ITEMS):
                    load_next(n)
                    if ITEMS[n][:2] == ("mqk", 0):
                        with sp.If(l == 0):
                            sp.wait_ge(zeroed, 3)
                            sp.dma_start(xd.rearrange("(n p) d -> p n d", p=P),
                                         zeros.unsqueeze(1).to_broadcast([P, ROWS // P, D])).then_inc(rows_zeroed, 16)

                def load_gate(p, e):
                    sp.dma_start(gate_w[p], of(w_gate, l, e)).then_inc(w_gu[p], 16)

                def load_up(p, e):
                    sp.dma_start(up_w[p], of(w_up, l, e)).then_inc(w_gu[p], 16)

                def load_expert(p, e):
                    wait_reg(sp, gu_ready, blocks_through(sp, e - BUF))
                    load_gate(p, e)
                    load_up(p, e)

                through(sp, "gb", 1)
                load_gate(0, 0)
                through(sp, "yb", 0)
                load_gate(1, 1)
                load_next(N_ITEMS)
                through(sp, "wo", 1)
                load_up(0, 0)
                load_up(1, 1)
                sp.wait_ge(pj_ready, GI[("rl", 0)] + 1)
                load_gate(2, 2)
                sp.wait_ge(xt_ready, 1)
                load_up(2, 2)
                with sp.Fori(1, E // BUF) as i:
                    for p in range(BUF):
                        load_expert(p, i * BUF + p)
                with sp.If(l < DEPTH - 1):
                    params(nxt)
                for e in range(E // BUF * BUF, E):
                    load_expert(e % BUF, e)
                with sp.If(l < DEPTH - 1):
                    for n in range(HEAD):
                        if n == 0:
                            wait_reg(sp, gu_ready, blocks_through(sp, E - 3))
                        if n == 2:
                            wait_reg(sp, y_ready, blocks_through(sp, E - 3))
                        if n == 3:
                            wait_reg(sp, gu_ready, blocks_through(sp, E - 1))
                        load_item(sp, nxt, n, head_in[n])
                with sp.If(l == DEPTH - 1):
                    for i in range(NT):
                        sp.wait_ge(combined, i + 1)
                        sp.dma_start(out[0, P * i:P * i + P, :], xs[:, i, :]).then_inc(out_done, 16)
                layer_end(sp, l, share(0))
            sp.wait_ge(out_done, 16 * NT)

        @block.gpsimd
        def _(pool):
            po = nc.gpsimd
            n_const = [0]

            def pc_link(ins):
                n_const[0] += 1
                ins.then_inc(pool_const, 1)
                pool.wait_ge(pool_const, n_const[0])

            po.memset(rwz[:, :, :], 0.0)
            po.memset(wgz[:, :, :], 0.0).then_inc(zeroed, 1)
            pool.wait_ge(zeroed, 1)
            po.memset(prm[96:P, :], 0.0).then_inc(zeroed, 1)
            pool.wait_ge(zeroed, 2)
            po.memset(cz[:, :, :], 0.0)
            po.memset(zeros, 0.0).then_inc(zeroed, 1)
            po.memset(ones[:, :], 1.0)
            po.memset(onesb[:, :], 1.0)
            po.memset(ident[:, :], 0.0)
            po.memset(mask[:, :], 0.0)
            po.memset(maskT[:, :], 0.0)
            pc_link(po.memset(nhalf[:, :], -0.5))
            po.affine_select(out=ident[:, :], in_=ident[:, :], compare_op=ALU.not_equal, fill=1.0, base=0,
                             pattern=[[-1, P]], channel_multiplier=1)
            po.affine_select(out=mask[:, 0:P], in_=mask[:, 0:P], compare_op=ALU.is_gt, fill=NEG, base=0,
                             pattern=[[1, P]], channel_multiplier=-1)
            po.affine_select(out=mask[:, P:256], in_=mask[:, P:256], compare_op=ALU.is_ge, fill=NEG, base=0,
                             pattern=[[-1, P]], channel_multiplier=1)
            po.affine_select(out=maskT[:, :], in_=maskT[:, :], compare_op=ALU.is_ge, fill=NEG, base=0,
                             pattern=[[1, P]], channel_multiplier=-1)
            po.affine_select(out=triu[:, :], in_=onesb[:, :], compare_op=ALU.is_gt, fill=0.0, base=0,
                             pattern=[[1, P]], channel_multiplier=-1)
            for k in range(1, 8):
                po.memset(thr[:, k - 1:k], float(MB * k))
            for g in range(4):
                po.memset(iog[:, g:g + 1], float(g - 8))
            pc_link(po.iota(ioe[:, :], pattern=[[1, 32]], base=0, channel_multiplier=0, allow_small_or_imprecise_dtypes=True))

            def power(n, dst, src):
                pool.wait_ge(pow_ask, n)
                w = src.shape[1]
                po.tensor_tensor(dst, src, nhalf[:, 0:w], ALU.pow).then_inc(pow_done, 1)

            def head_power(t):
                for i in range(NT):
                    wait_head(pool, head_ask, t, NT, i + 1)
                    po.tensor_tensor(rs[:, i:i + 1], ss[:, i:i + 1], nhalf[:, 0:1], ALU.pow).then_inc(head_pow, 1)

            head_power(0)
            with pool.Fori(0, DEPTH) as l:
                pool.wait_ge(pj_ready, GI[("h1T", KD - 1)] + 1)
                po.memset(rstack[:, :], 0.0).then_inc(stack_zero, 1)
                for i in range(NT):
                    power(1 + i, rsq[:, 0:10], ssq[:, 0:10])
                for i in range(NT):
                    power(5 + i, fin[:, 8:12], fin[:, 4:8])
                for j in range(KD):
                    pool.wait_ge(tb_sum, j + 1)
                    po.tensor_tensor(merged[:, j, :], merged[:, j, :], tb[:, j % 2, :], ALU.add).then_inc(merged_ready, 1)
                def load_down(p, e):
                    if p < 2:
                        po.dma_start(ring[:, (2, 5)[p], :].rearrange("p (k n) -> p k n", k=FC), of(w_down, l, e)).then_inc(w_dn[p], 16)
                    else:
                        po.dma_start(regB[:, :].rearrange("p (k n) -> p k n", n=D), of(w_down, l, e)[:, 0:FC - 1, :]).then_inc(w_dn[p], 16)
                        po.dma_start(down_w[p][FC - 1].unsqueeze(1), of(w_down, l, e)[:, FC - 1:FC, :]).then_inc(w_dn[p], 16)

                through(pool, "yb", 0)
                load_down(0, 0)
                load_down(2, 2)
                for i in range(NT):
                    power(9 + i, rs[:, 4 + i:5 + i], ss[:, 4 + i:5 + i])

                pool.wait_ge(xn_ready, NT)
                pool.wait_ge(rows_zeroed, 16)
                for k in range(2):
                    pool.wait_ge(routed, 2 + k)
                    for i in range(NT):
                        po.indirect_dma_start(out=xd, out_offset=bass.IndirectOffsetOnAxis(ap=slot_u[:, k, i:i + 1], axis=0),
                                              in_=xn[:, i, :], in_offset=None).then_inc(scattered, 16)
                pool.wait_ge(tables, 1)
                nb = po.value_load(tabs[0:1, 47:48], min_val=E, max_val=MAXB)

                def next_down(p, e):
                    wait_reg(pool, y_ready, blocks_through(po, e - BUF))
                    load_down(p, e)

                through(pool, "ada", G2_ADA + 1)
                pool.wait_ge(xt_ready, 1)
                load_down(1, 1)
                with pool.Fori(1, E // BUF) as i:
                    for p in range(BUF):
                        next_down(p, i * BUF + p)
                for e in range(E // BUF * BUF, E):
                    next_down(e % BUF, e)
                wait_reg(pool, y_out, nb * 32 + 32)
                for i in range(NT):
                    for k in range(2):
                        po.indirect_dma_start(out=yg[k][:, i, :], out_offset=None, in_=xd,
                                              in_offset=bass.IndirectOffsetOnAxis(ap=slot_u[:, k, i:i + 1], axis=0)).then_inc(yg_in[i], 16)
                with pool.If(l < DEPTH - 1):
                    head_power(l + 1)
                layer_end(pool, l, share(1))

        @block.scalar
        def _(act):
            ac = nc.scalar
            act.wait_ge(dve_const, 1)
            ac.activation(sinr[:, :, :].rearrange("p i f -> p (i f)"), rt[:, 64:96], ACT.Sin).then_inc(act_const, 1)
            ac.activation(cosr[:, :, :].rearrange("p i f -> p (i f)"), rt[:, 96:128], ACT.Sin).then_inc(act_const, 1)
            act.wait_ge(c_cols, 1)
            ac.activation(cz[:, :, 0], ps[2][:, 0:KD], ACT.Silu).then_inc(act_const, 1)

            def head_norm(t, wait):
                for i in range(NT + 1):
                    if i < NT:
                        wait(i)
                        ac.activation(head_squares, xs[:, i, :], ACT.Square, accum_out=ss[:, i:i + 1]).then_inc(head_sq, 1)
                        wait_head(act, head_sq, t, NT, i + 1)
                    if i:
                        wait_head(act, head_pow, t, NT, i)
                        ac.activation(xn[:, i - 1, :], xs[:, i - 1, :], ACT.Copy, scale=rs[:, i - 1:i]).then_inc(head_xn, 1)

            def head_rows(t):
                for j in range(HEAD_ADA):
                    wait_head(act, head_sum, t, HEAD_ADA, j + 1)
                    if j >= 2:
                        wait_head(act, head_bc, t, HEAD_ADA, j - 1)
                    ac.activation(mrow[:, j % 2, :], pj[j % 2][:, :], ACT.Copy).then_inc(head_row, 1)

            head_norm(0, lambda i: act.wait_ge(x_in, 16))
            head_rows(0)
            with act.Fori(0, DEPTH) as l:
                def ada_row(j):
                    bank, free = ready(act, "ada", j)
                    ac.activation(mrow[:, j % 2, :], bank[:, :], ACT.Copy).then_inc(mrow_ready, 1)
                    act.wait_ge(mrow_ready, j - G2_ADA + 1)
                    act.sem_inc(free, 1)

                wait_reg(act, mod_ready, l + 1)
                for k in range(1, KD, 2):
                    bank, free = ready(act, "h1T", k)
                    ac.activation(hT[:, k, :], bank[:, :], ACT.Identity, scale=A1[:, k:k + 1],
                                  bias=modc[:, k:k + 1]).then_inc(free, 1)
                for i in range(NT):
                    bank, free = ready(act, "q", i)
                    ac.activation(qk_rows[:, i, 0:512], bank[:, :], ACT.Copy)
                    if i >= 1:
                        act.wait_ge(qk_sq, i)
                    ac.activation(small[:, 0:512], bank[:, :], ACT.Square).then_inc(free, 1)
                    bank, free = ready(act, "kv", i)
                    ac.activation(qk_rows[:, i, 512:640], bank[:, 0:128], ACT.Copy)
                    ac.activation(v_rows[:, i, :], bank[:, 128:256], ACT.Copy)
                    ac.activation(small[:, 512:640], bank[:, 0:128], ACT.Square).then_inc(free, 1)
                bank, free = ready(act, "gates")
                wait_reg(act, head_bc, l * HEAD_ADA + HEAD_ADA)
                ac.activation(gate_parts, bank[:, :], ACT.Copy).then_inc(gates_f, 1)
                act.wait_ge(gates_f, 1)
                act.sem_inc(free, 1)

                def gates_act():
                    bank, free = ready(act, "gsum")
                    ac.activation(rows4[:, 0, :], bank[0:4, :], ACT.Identity, bias=gbias[0:4, :]).then_inc(gates_f, 1)
                    act.wait_ge(gates_f, 3)
                    ac.activation(rows4[:, 2, :], rows4[:, 2, :], ACT.Exp, scale=-1.0).then_inc(gates_f, 1)
                    act.wait_ge(gates_f, 4)
                    ac.activation(rows4[:, 2, :], rows4[:, 2, :], ACT.Ln, bias=1.0).then_inc(gates_f, 1)

                def conv_act(m):
                    bank, free = ready(act, "mqk", m)
                    if m >= 2:
                        act.wait_ge(conv_z, m - 1)
                    ac.activation(conv_u[:, m % 2, 3:515], bank[:, :], ACT.Copy).then_inc(conv_in, 1)
                    act.wait_ge(conv_in, m + 1)
                    act.sem_inc(free, 1)

                def conv_tanh(m):
                    act.wait_ge(conv_z, m + 1)
                    if m == 0:
                        act.wait_ge(qk_sq, NT)
                    if m >= 1:
                        act.wait_ge(conv_t, 2 * m)
                    ac.activation(small[:, 0:512], mqkT[:, m, :], ACT.Tanh, scale=0.5).then_inc(conv_t, 1)

                def qkT_evac(i):
                    bank, free = ready(act, "qT", i)
                    ac.activation(qkT[:, 0:4, P * i:P * i + P], bank[:, :].rearrange("p (c t) -> p c t", c=4), ACT.Copy).then_inc(free, 1)
                    bank, free = ready(act, "kT", i)
                    ac.activation(qkT[:, 4:6, P * i:P * i + P], bank[:, 0:256].rearrange("p (c t) -> p c t", c=2), ACT.Copy).then_inc(free, 1)

                def att_exp(u):
                    n, g = u // HKV, u % HKV
                    lo = 0 if n else P
                    act.wait_ge(m_ready, u + 1)
                    a = att[:, u % 2, :]
                    for h in range(4):
                        ac.activation(prob[:, u % 2, h, lo:256], prob[:, u % 2, h, lo:256], ACT.Exp,
                                      bias=a[:, 4 + h:5 + h], accum_out=a[:, 8 + h:9 + h])
                    ac.activation(a[:, 12:16], a[:, 16:20], ACT.Exp).then_inc(e_ready, 1)

                def att_pt(u):
                    n = u // HKV
                    act.wait_ge(pt_ready, u + 1)
                    if u >= 2:
                        act.wait_ge(o_ready, u // 2)
                    ac.activation(pT[:, u % 2, 1, :], att_t[1][:, :], ACT.Copy).then_inc(pt_evac, 1)

                def att_o(u):
                    n = u // HKV
                    act.wait_ge(o_ready, u // 2 + 1)
                    for g in range(HKV):
                        o4 = ps[6][64 * g:64 * g + 64, :].rearrange("p (a b t) -> p b a t", a=2, b=2)
                        for odd in range(2):
                            last = ac.activation(attn_o[64 * odd:64 * odd + 64, 2 * g:2 * g + 2, P * n:P * n + P], o4[:, odd], ACT.Copy)
                    last.then_inc(o_evac, 1)

                for s in range(16):
                    if s < 8:
                        conv_act(s)
                        if s == 0:
                            gates_act()
                    elif s < 12:
                        i = s - 8
                        if i == 0:
                            act.wait_ge(rows_zeroed, 16)
                        bank, free = ready(act, "mv", i)
                        ac.activation(vaug[:, i, :, 0:DM], bank[:, :].rearrange("p (h n) -> p h n", h=HM), ACT.Copy).then_inc(free, 1)
                    else:
                        i = s - 12
                        bank, free = ready(act, "mo", i)
                        ac.activation(mo_t[:, i, :], bank[:, :], ACT.Tanh, scale=0.5).then_inc(free, 1)
                    if 1 <= s <= NT:
                        qkT_evac(s - 1)
                    if 1 <= s <= 8:
                        conv_tanh(s - 1)
                    if 4 <= s < 12:
                        att_exp(s - 4)
                    if 5 <= s < 13:
                        att_pt(s - 5)
                    if 6 <= s < 14 and s % 2:
                        att_o(s - 6)
                    if s == 14:
                        act.wait_ge(rows_ready, 1)
                        for q in (32, 64, 96):
                            ac.activation(rstack[q:q + 4, :], rstack[q:q + 4, :], ACT.Exp)
                        ac.activation(g16[:, 24:28], g16[:, 20:24], ACT.Exp).then_inc(rows_ready, 1)
                bank, free = ready(act, "rT")
                for q in range(4):
                    ins = ac.activation(colR[:, :, q, :], bank[:, :].rearrange("p (i n) -> p i n", i=NT)[:, :, 32 * q:32 * q + HM], ACT.Copy)
                ins.then_inc(free, 1)
                act.wait_ge(free, GI[("rT", 0)] // 2 + 1)

                def m_act_a(u):
                    c_, h = u // HM, u % HM
                    act.wait_ge(ma_ready, u + 1)
                    if u >= 2:
                        act.wait_ge(mb_ready, u - 1)
                    b = 2 + u % 2
                    ac.activation(ke[:, u % 2, :], ps[b][:, 0:P], ACT.Copy, scale=colR[:, c_, 2, h:h + 1])
                    ac.activation(ex[:, u % 2, :], argm[:, h, P * c_:P * c_ + P], ACT.Exp, bias=colR[:, c_, 0, h:h + 1]).then_inc(ma_act, 1)

                def m_act_b(u):
                    c_, h = u // HM, u % HM
                    act.wait_ge(mb_ready, u + 1)
                    if c_ > 0:
                        if u >= HM + 2:
                            act.wait_ge(c_upd, u - 1)
                        ac.activation(icb[:, u % 2, :], ps[4 + u % 2][:, 256:256 + DM + 1], ACT.Copy,
                                      scale=colR[:, c_, 1, h:h + 1]).then_inc(ic_ready, 1)

                act.wait_ge(pj_free[GI[("mubc", HM - 1)] % 2], GI[("mubc", HM - 1)] // 2 + 1)
                act.wait_ge(pj_free[GI[("mubc", HM - 2)] % 2], GI[("mubc", HM - 2)] // 2 + 1)
                for j in range(8):
                    bank, free = ready(act, "ga", j)
                    ac.activation(merged[:, j, :], bank[:, :], ACT.Tanh, scale=0.5).then_inc(free, 1)
                    for u in (2 * j, 2 * j + 1):
                        m_act_a(u)
                        if u >= 1:
                            m_act_b(u - 1)
                m_act_b(15)
                for j in range(8):
                    bank, free = ready(act, "gb", j)
                    if j >= 2:
                        act.wait_ge(merged_ready, j - 1)
                    ac.activation(tb[:, j % 2, :], bank[:, :], ACT.Tanh, scale=0.5).then_inc(free, 1)

                for i in range(NT):
                    act.wait_ge(x_upd, i + 1)
                    if i:
                        act.wait_ge(ffn_sq, i)
                    ac.activation(squares, xs[:, i, :], ACT.Square, accum_out=ss[:, 4 + i:5 + i]).then_inc(ffn_sq, 1)
                ada_row(G2_ADA)
                for k in range(1, KD, 2):
                    bank, free = ready(act, "h2T", k)
                    ac.activation(hT[:, k, :], bank[:, :], ACT.Identity, scale=A2[:, k:k + 1],
                                  bias=modc[:, 24 + k:25 + k]).then_inc(free, 1)
                bank, free = ready(act, "rl")
                act.wait_ge(ffn_sq, NT)
                ac.activation(small[:, 0:512], bank[:, :], ACT.Copy).then_inc(free, 1)
                bank, free = ready(act, "lg")
                ac.activation(rt[:, 0:64], bank[:, 0:64], ACT.Exp, scale=-1.0).then_inc(free, 1)
                ada_row(G2_ADA + 1)

                act.wait_ge(tables, 1)
                nb = ac.value_load(tabs[0:1, 47:48], min_val=E, max_val=MAXB)
                nb1 = ac.value_load(tabs[0:1, 48:49], min_val=E - 1, max_val=MAXB - 1)

                def xt_act():
                    for k in range(0, KD, 2):
                        last = ac.activation(xT[:, k, :], ps[2][:, MB * k:MB * k + MB], ACT.Identity,
                                             scale=A2[:, k:k + 1], bias=modc[:, 24 + k:25 + k])
                    last.then_inc(xt_evac_a, 1)

                def load_rows(p, b):
                    act.dma_start(xg[p], xd[bass.ds(b * MB, MB), :]).then_inc(xg_in[p], 16)

                def silu_():
                    ac.activation(hsil[64:P, :], ps[3][0:64, :], ACT.Silu).then_inc(sil_ready, 1)

                def h_evac():
                    ac.activation(hxT[:, :, :].rearrange("p k r -> p (k r)"), ps[4][:, 0:FC * MB], ACT.Copy).then_inc(ht_evac, 1)

                def store_rows(b):
                    wait_reg(act, y_taken, b + 2)
                    for h in range(2):
                        act.dma_start(xd[bass.ds(b * MB, MB), 512 * h:512 * h + 512], yb[64 * h:64 * h + 64, :]).then_inc(y_out, 16)

                wait_reg(act, scattered, l * (32 * NT) + 32 * NT)
                load_rows(0, 0)
                load_rows(1, 1)
                act.wait_ge(xt_ready, 1)
                xt_act()
                load_rows(0, 2)
                act.wait_ge(gu_ready, 1)
                silu_()
                act.wait_ge(xt_ready, 2)
                xt_act()
                load_rows(1, 3)
                act.wait_ge(ht_ready, 1)
                h_evac()
                with act.Fori(0, nb1) as b:
                    act.wait_ge(gu_ready, b + 2)
                    silu_()
                    act.wait_ge(xt_ready, b + 3)
                    xt_act()
                    with act.If(b % 2 == 0):
                        load_rows(0, b + 4)
                    with act.Else():
                        load_rows(1, b + 4)
                    act.wait_ge(ht_ready, b + 2)
                    h_evac()
                    store_rows(b)
                store_rows(nb1)
                wait_reg(act, xg_in[0], ((nb + 4) // 2) * 16)
                wait_reg(act, xg_in[1], ((nb + 3) // 2) * 16)
                with act.If(l < DEPTH - 1):
                    head_rows(l + 1)
                    head_norm(l + 1, lambda i: act.wait_ge(combined, i + 1))
                layer_end(act, l, share(2))

        @block.tensor
        def _(pe):
            te = nc.tensor
            pe.wait_ge(const_in, 16 * 4)
            pe.wait_ge(pool_const, 2)
            te.transpose(ps[2][:, 0:KD], crow, ident[0:KD, 0:KD]).then_inc(c_cols, 1)
            pe.wait_ge(act_const, 3)
            pe.wait_ge(dve_const, 3)

            def column_sums(bank, rows):
                for q in range(4):
                    ins = te.matmul(bank[:, q:q + 1], rows[:, P * q:P * q + P], ones[:, 0:1], start=True, stop=True)
                return ins

            def head(t):
                wait_head(pe, params_in, t, 14 * 16, 14 * 16)
                te.transpose(ps[4][:, 0:P], prm[:, :], ident[:, :]).then_inc(param_cols, 1)
                for j in range(HEAD_ADA + 1):
                    if j < HEAD_ADA:
                        wait_head(pe, head_in[j], t, 16, 16)
                        if j >= 2:
                            wait_head(pe, head_row, t, HEAD_ADA, j - 1)
                        w = slot("ada", j, 8, 512)
                        for k in range(KD):
                            g = k % 4
                            ins = te.matmul(pj[j % 2][32 * g:32 * g + 32, :], cz[:, k, :], w[:, k, :], start=(k < 4), stop=(k >= 4))
                        ins.then_inc(head_sum, 1)
                    if j >= 1:
                        wait_head(pe, head_row, t, HEAD_ADA, j)
                        if j >= 3:
                            wait_head(pe, head_read, t, HEAD_ADA, j - 2)
                        column_sums(ps[2 + (j - 1) % 2], mrow[:, (j - 1) % 2, :]).then_inc(head_bc, 1)

            head(0)
            with pe.Fori(0, DEPTH) as l:
                def take(name, i=0):
                    g = GI[(name, i)]
                    if g >= 2:
                        pe.wait_ge(pj_free[g % 2], g // 2)
                    return pj[g % 2]

                def bcast(j):
                    pe.wait_ge(mrow_ready, j - G2_ADA + 1)
                    te.matmul(bc_bank(j)[:, :], ones[:, :], mrow[:, j % 2, :], start=True, stop=True).then_inc(bc_ready, 1)

                def ada_group(j):
                    arrived(pe, "ada", j)
                    bank = take("ada", j)
                    w = slot("ada", j, 8, 512)
                    for k in range(KD):
                        g = k % 4
                        ins = te.matmul(bank[32 * g:32 * g + 32, :], cz[:, k, :], w[:, k, :], start=(k < 4), stop=(k >= 4))
                    ins.then_inc(pj_ready, 1)

                wait_reg(pe, head_xn, l * NT + NT)
                for k in range(KD):
                    bank = take("h1T", k)
                    for i in range(NT):
                        ins = te.transpose(bank[:, P * i:P * i + P], xn[:, i, P * k:P * k + P], ident[:, :])
                    ins.then_inc(pj_ready, 1)
                g = GI[("h1T", KD - 1)]
                pe.wait_ge(pj_free[g % 2], g // 2 + 1)
                pe.wait_ge(pj_free[1 - g % 2], (g - 1) // 2 + 1)

                def token_group(name, i, w):
                    arrived(pe, name, 0)
                    bank = take(name, i)
                    wv = slot(name, 0, 8, w)
                    for k in range(KD):
                        ins = te.matmul(bank[:, 0:w], hT[:, k, P * i:P * i + P], wv[:, k, :], start=(k == 0), stop=(k == KD - 1))
                    ins.then_inc(pj_ready, 1)

                def feature_group(name, m, rhs, kn, w):
                    arrived(pe, name, m // (w // P))
                    bank = take(name, m)
                    wv = slot(name, m // (w // P), kn, w)
                    c0 = P * (m % (w // P))
                    for k in range(kn):
                        ins = te.matmul(bank[:, :], wv[:, k, c0:c0 + P], rhs[:, k, :], start=(k == 0), stop=(k == kn - 1))
                    ins.then_inc(pj_ready, 1)

                for i in range(NT):
                    token_group("q", i, 512)
                    token_group("kv", i, 256)
                bank = take("gates")
                for k in range(KD):
                    g = k % 4
                    ins = te.matmul(bank[32 * g:32 * g + 32, :], wgz[:, k, :], hT[:, k, :], start=(k < 4), stop=(k >= 4))
                ins.then_inc(pj_ready, 1)

                def qk_transposes(i):
                    pe.wait_ge(qk_ready, i + 1)
                    for name, c0, n in (("qT", 0, 4), ("kT", 4, 2)):
                        bank = take(name, i)
                        for m in range(n):
                            ins = te.transpose(bank[:, P * m:P * m + P], qk_rows[:, i, P * (c0 + m):P * (c0 + m) + P], ident[:, :])
                        ins.then_inc(pj_ready, 1)

                def att_scores(u):
                    n, g = u // HKV, u % HKV
                    if u == 0:
                        wait_reg(pe, head_read, l * HEAD_ADA + HEAD_ADA)
                    gi = GI[("kT", n)]
                    pe.wait_ge(pj_free[gi % 2], gi // 2 + 1)
                    pe.wait_ge(pj_free[(gi - 1) % 2], (gi - 1) // 2 + 1)
                    if u >= 1:
                        pe.wait_ge(s_read, u)
                    for h in range(4):
                        hq = 4 * g + h
                        r = 64 * (hq % 2)
                        q = qkT[r:r + 64, hq // 2, P * n:P * n + P]
                        bank = att_s[h % 2]
                        o = 256 * (h // 2)
                        if n:
                            ins = te.matmul(bank[:, o:o + 256], q, qkT[r:r + 64, 4 + g, P * (n - 1):P * (n + 1)], start=True, stop=True)
                        else:
                            ins = te.matmul(bank[:, o + P:o + 256], q, qkT[r:r + 64, 4 + g, 0:P], start=True, stop=True)
                    ins.then_inc(s_ready, 1)

                def att_ptrans(u):
                    n = u // HKV
                    pe.wait_ge(p_norm, u + 1)
                    if u >= 1:
                        pe.wait_ge(pt_evac, 2 * u)
                    for kb in range(0 if n else 1, 2):
                        for h in range(4):
                            ins = te.transpose(att_t[kb][:, P * h:P * h + P], prob[:, u % 2, h, P * kb:P * kb + P], ident[:, :])
                    ins.then_inc(pt_ready, 1)

                def att_out(u):
                    n = u // HKV
                    pe.wait_ge(pt_evac, 2 * (u + 1))
                    if u >= 3:
                        pe.wait_ge(o_evac, u // 2)
                    for kb in range(0 if n else 1, 2):
                        for g in range(HKV):
                            ins = te.matmul(ps[6][64 * g:64 * g + 64, :], v_rows[:, n - 1 + kb, 64 * g:64 * g + 64], pT[:, g, kb, :],
                                            start=(kb == 0 or n == 0), stop=(kb == 1))
                    ins.then_inc(o_ready, 1)

                for s in range(16):
                    if s < 8:
                        feature_group("mqk", s, hT, 8, 512)
                        if s == 0:
                            pe.wait_ge(gates_f, 1)
                            te.matmul(take("gsum")[0:36, :], fold36[:, :], gate_parts, start=True, stop=True).then_inc(pj_ready, 1)
                    elif s < 12:
                        token_group("mv", s - 8, 512)
                    else:
                        token_group("mo", s - 12, 512)
                    if 1 <= s <= NT:
                        qk_transposes(s - 1)
                    if 4 <= s < 12:
                        att_scores(s - 4)
                    if 5 <= s < 13:
                        att_ptrans(s - 5)
                    if 6 <= s < 14 and s % 2:
                        att_out(s - 6)
                pe.wait_ge(rows_ready, 2)
                bank = take("rT")
                for i in range(NT):
                    ins = te.transpose(bank[:, P * i:P * i + P], rstack[:, P * i:P * i + P], ident[:, :])
                ins.then_inc(pj_ready, 1)
                for h in range(HM):
                    bank = take("mubc", h)
                    te.matmul(bank[:, :], ident[0:HM, h:h + 1].to_broadcast([HM, P]), rows4[:, 5, :], start=True, stop=True).then_inc(pj_ready, 1)
                bank = take("dec")
                for h in range(HM):
                    ins = te.matmul(bank[:, 4 * h:4 * h + 4], ident[0:HM, h:h + 1].to_broadcast([HM, P]), g16[:, 24:28], start=True, stop=True)
                ins.then_inc(pj_ready, 1)
                pe.wait_ge(pj_free[GI[("mo", NT - 1)] % 2], GI[("mo", NT - 1)] // 2 + 1)
                pe.wait_ge(conv_t, 16)
                pe.wait_ge(pt_evac, 16)
                pe.wait_ge(o_evac, 4)

                def m_a(u):
                    c_, h = u // HM, u % HM
                    b = 2 + u % 2
                    if u >= 2:
                        pe.wait_ge(ma_act, u - 1)
                        pe.wait_ge(w_ready, u - 1)
                    kf = mqkT[:, HM + h, P * c_:P * c_ + P]
                    te.transpose(ps[b][:, 0:P], kf, ident[:, :])
                    te.matmul(ps[b][:, P:2 * P], kf, mqkT[:, h, P * c_:P * c_ + P], start=True, stop=True).then_inc(ma_ready, 1)

                def m_b(u):
                    c_, h = u // HM, u % HM
                    pe.wait_ge(w_ready, u + 1)
                    pe.wait_ge(ma_act, u + 1)
                    if u >= 2:
                        pe.wait_ge(c_upd, u - 1)
                    ins = te.matmul(ps[4 + u % 2][:, 0:DM + 1], wS[:, u % 2, :], vaug[:, c_, h, :], start=True, stop=True)
                    if c_ > 0:
                        pe.wait_ge(c_upd, u - HM + 1)
                        ins = te.matmul(ps[4 + u % 2][:, 256:256 + DM + 1], mqkT[:, h, P * c_:P * c_ + P], cst[:, h, :], start=True, stop=True)
                    if c_ < NT - 1:
                        ins = te.matmul(ps[6 + u % 2][:, 0:DM + 1], ke[:, u % 2, :], vaug[:, c_, h, :], start=True, stop=True)
                    ins.then_inc(mb_ready, 1)

                for j in range(8):
                    feature_group("ga", j, hT, 8, 512)
                    for u in (2 * j, 2 * j + 1):
                        m_a(u)
                        if u >= 1:
                            m_b(u - 1)
                    feature_group("ya", j, attn_o, 4, D)
                m_b(15)
                feature_group("gb", 0, hT, 8, 512)
                feature_group("gb", 1, hT, 8, 512)
                for i in range(NT):
                    pe.wait_ge(hm_ready, i + 1)
                    bank = take("hmT", i)
                    for h in range(HM):
                        ins = te.transpose(bank[:, P * h:P * h + P], mo_t[:, i, P * h:P * h + P], ident[:, :])
                    ins.then_inc(pj_ready, 1)
                for j in range(8):
                    if j >= 2:
                        feature_group("gb", j, hT, 8, 512)
                    if j == 0:
                        for g in (GI[("hmT", NT - 1)], GI[("hmT", NT - 2)]):
                            pe.wait_ge(pj_free[g % 2], g // 2 + 1)
                    feature_group("yb", j, hmT, 4, D)
                    if j - 1 in MID_ADA:
                        c_ = MID_ADA[j - 1]
                        pe.wait_ge(mid_ready, c_ - HEAD_ADA + 1)
                        bank = take("ada", c_)
                        if c_ < 6:
                            ins = te.matmul(bank[:, :], ones[:, :], mid_sum, start=True, stop=True)
                        else:
                            ins = column_sums(bank, mid_sum)
                        ins.then_inc(pj_ready, 1)
                pe.wait_ge(merged_ready, 8)
                for i in range(NT):
                    for h in range(2):
                        if h == 0 and i == 0:
                            arrived(pe, "wo", 0)
                            arrived(pe, "wo", 1)
                        bank = take("wo", 2 * i + h)
                        for k in range(KD):
                            ins = te.matmul(bank[:, :], merged[:, k, P * i:P * i + P],
                                            slot("wo", k // 4, 4, D)[:, k % 4, 512 * h:512 * h + 512], start=(k == 0), stop=(k == KD - 1))
                        ins.then_inc(pj_ready, 1)

                ada_group(G2_ADA)
                pe.wait_ge(xn_ready, NT)
                for k in range(KD):
                    bank = take("h2T", k)
                    for i in range(NT):
                        ins = te.transpose(bank[:, P * i:P * i + P], xn[:, i, P * k:P * k + P], ident[:, :])
                    ins.then_inc(pj_ready, 1)
                g = GI[("h2T", KD - 1)]
                pe.wait_ge(pj_free[g % 2], g // 2 + 1)
                pe.wait_ge(pj_free[1 - g % 2], (g - 1) // 2 + 1)
                bank = take("rl")
                for k in range(KD):
                    g = k % 4
                    ins = te.matmul(bank[32 * g:32 * g + 32, :], rwz[:, k, :], hT[:, k, :], start=(k < 4), stop=(k >= 4))
                ins.then_inc(pj_ready, 1)
                g = GI[("rl", 0)]
                pe.wait_ge(pj_free[g % 2], g // 2 + 1)
                bank = take("lg")
                for i in range(NT):
                    ins = te.matmul(bank[:, E * i:E * i + E], small[:, P * i:P * i + P], fold[:, :], start=True, stop=True)
                ins.then_inc(pj_ready, 1)
                ada_group(G2_ADA + 1)
                bcast(G2_ADA)
                bcast(G2_ADA + 1)
                pe.wait_ge(routed, 1)
                bank = take("rank")
                for i in range(NT):
                    for j in range(i):
                        te.matmul(bank[:, E * i:E * i + E], onesb[:, :], Mb[:, j, :], start=(j == 0), stop=False)
                    te.matmul(bank[:, E * i:E * i + E], triu[:, :], Mb[:, i, :], start=(i == 0), stop=True)
                for j in range(NT):
                    ins = te.matmul(bank[:, E * NT:E * NT + E], onesb[:, :], Mb[:, j, :], start=(j == 0), stop=(j == NT - 1))
                ins.then_inc(pj_ready, 1)

                pe.wait_ge(tables, 1)
                nb = te.value_load(tabs[0:1, 47:48], min_val=E, max_val=MAXB)
                nb1 = te.value_load(tabs[0:1, 48:49], min_val=E - 1, max_val=MAXB - 1)

                def x_transposes(p):
                    for k in range(KD):
                        ins = te.transpose(ps[(2, 6)[k % 2]][:, MB * k:MB * k + MB], xg[p][:, P * k:P * k + P],
                                           ident[MB * p:MB * p + MB, MB * p:MB * p + MB])
                    ins.then_inc(xt_ready, 1)

                def gate_up(p):
                    for k in range(KD):
                        for part in range(2):
                            w = (gate_w, up_w)[part][p]
                            ins = te.matmul(ps[3][64 * part:64 * part + 64, :], xT[:, k, :], w[:, k, :], start=(k == 0), stop=(k == KD - 1))
                    ins.then_inc(gu_ready, 1)

                def h_transposes(b):
                    wait_reg(pe, hx_ready, b + 1)
                    for k in range(FC):
                        ins = te.transpose(ps[4][:, MB * k:MB * k + MB], hx[:, P * k:P * k + P], ident[0:MB, 0:MB])
                    ins.then_inc(ht_ready, 1)

                def down(p):
                    for k in range(FC):
                        for half in range(2):
                            ins = te.matmul(ps[5][64 * half:64 * half + 64, :], hxT[:, k, :], down_w[p][k][:, 512 * half:512 * half + 512],
                                            start=(k == 0), stop=(k == FC - 1))
                    ins.then_inc(y_ready, 1)

                def in_buffer(e, products, sems, each, held):
                    def there(p):
                        wait_reg(pe, sems[p], l * (held[p] * each[p]) + (e // BUF) * each[p] + each[p])
                        products(p)

                    with pe.If(e % BUF == 0):
                        there(0)
                    with pe.Else():
                        with pe.If(e % BUF == 1):
                            there(1)
                        with pe.Else():
                            there(2)

                pe.wait_ge(xg_in[0], 16)
                x_transposes(0)
                pe.wait_ge(xt_evac_a, 1)
                pe.wait_ge(xt_evac_d, 1)
                pe.wait_ge(w_gu[0], 32)
                gate_up(0)
                pe.wait_ge(xg_in[1], 16)
                x_transposes(1)
                h_transposes(0)
                with pe.Fori(0, nb1) as b:
                    e1 = te.value_load(tabs[0:1, bass.ds(b + 1, 1)], min_val=0, max_val=E - 1)
                    e0 = te.value_load(tabs[0:1, bass.ds(b, 1)], min_val=0, max_val=E - 1)
                    pe.wait_ge(xt_evac_a, b + 2)
                    pe.wait_ge(xt_evac_d, b + 2)
                    in_buffer(e1, gate_up, w_gu, (32, 32, 32), (0, 0, 0))
                    with pe.If(b % 2 == 0):
                        wait_reg(pe, xg_in[0], (b // 2) * 16 + 32)
                        x_transposes(0)
                    with pe.Else():
                        wait_reg(pe, xg_in[1], (b // 2) * 16 + 32)
                        x_transposes(1)
                    pe.wait_ge(ht_evac, b + 1)
                    pe.wait_ge(y_taken, b + 1)
                    in_buffer(e0, down, w_dn, DN, HELD)
                    h_transposes(b + 1)
                pe.wait_ge(ht_evac, nb)
                pe.wait_ge(y_taken, nb)
                last = (E - 1) % BUF
                wait_reg(pe, w_dn[last], (l + 1) * (HELD[last] * DN[last]))
                down(last)
                with pe.If(l < DEPTH - 1):
                    wait_reg(pe, xt_evac_a, nb + 1)
                    head(l + 1)
                layer_end(pe, l, share(3))

        @block.vector
        def _(dve):
            ve = nc.vector
            cstep = [0]

            def clink(ins):
                cstep[0] += 1
                ins.then_inc(dve_step, 1)
                dve.wait_ge(dve_step, cstep[0])

            dve.wait_ge(const_in, 16 * 4)
            clink(ve.tensor_copy(rt[:, 4:8], rt[:, 0:4].bitcast(I32)))
            inv = np.power(np.float32(THETA), -(np.arange(0, ROPE, 2, dtype=np.float32) / np.float32(ROPE)), dtype=np.float32)
            for f in range(HALF):
                ins = ve.tensor_scalar(rt[:, 64:96].rearrange("p (i f) -> p i f", f=HALF)[:, :, f], rt[:, 4:8], float(inv[f]), None, ALU.mult)
            clink(ins)
            parts, rest = [], 2.0 * np.pi
            for bits in (8, 8, 8):
                e = np.floor(np.log2(rest)) - (bits - 1)
                parts.append(float(np.floor(rest / 2.0 ** e) * 2.0 ** e))
                rest -= parts[-1]
            parts.append(float(rest))
            BIG = 12582912.0
            clink(ve.tensor_copy(rt[:, 96:128], rt[:, 64:96]))
            for off, shift, last in ((64, 0.0, 0.0), (96, 0.25, float(np.pi / 2))):
                a, k = rt[:, off:off + 32], rt[:, 128:160]
                clink(ve.tensor_scalar(k, a, float(1.0 / (2.0 * np.pi)), shift, ALU.mult, ALU.add))
                clink(ve.tensor_scalar(k, k, BIG, None, ALU.add))
                clink(ve.tensor_scalar(k, k, -BIG, None, ALU.add))
                for part in parts:
                    clink(ve.scalar_tensor_tensor(a, k, -part, a, ALU.mult, ALU.add))
                clink(ve.tensor_scalar(a, a, last, None, ALU.add))
                clink(ve.tensor_scalar(a, a, 3.1415925, -3.1415925, ALU.min, ALU.max))
            ve.sem_inc(dve_const, 1)
            dve.wait_ge(pool_const, 2)
            clink(ve.tensor_tensor(fold[:, :], ident[:, 0:E], ident[:, 32:32 + E], ALU.add))
            clink(ve.tensor_tensor(fold[:, :], fold[:, :], ident[:, 64:64 + E], ALU.add))
            clink(ve.tensor_tensor(fold[:, :], fold[:, :], ident[:, 96:96 + E], ALU.add))
            clink(ve.memset(fold36[:, :], 0.0))
            ve.tensor_copy(fold36[:, 0:4], fold[:, 0:4])
            clink(ve.tensor_copy(fold36[:, 32:36], fold[:, 4:8]))
            ve.memset(g16[:, 0:1], 0.0)
            ve.sem_inc(dve_const, 2)
            dve.wait_ge(act_const, 3)
            ve.sem_clear(dve_step)

            hn = [0]

            def hlink(ins):
                hn[0] += 1
                ins.then_inc(head_step, 1)
                dve.wait_ge(head_step, hn[0])

            def columns(j, bank, read, lnk):
                lnk(ve.tensor_copy(modc[:, 4 * j:4 * j + 4], bank[:, 0:4]))
                ve.sem_inc(read, 1)

            def head_norm(t, i):
                wait_head(dve, head_sq, t, NT, i + 1)
                hlink(ve.tensor_scalar(ss[:, i:i + 1], ss[:, i:i + 1], 1.0 / D, EPS, ALU.mult, ALU.add))
                ve.sem_inc(head_ask, 1)

            def head_mod(t):
                wait_head(dve, param_cols, t, 1, 1)
                hlink(ve.tensor_copy(pc[:, :], ps[4][:, 0:P]))
                for j in range(HEAD_ADA):
                    wait_head(dve, head_bc, t, HEAD_ADA, j + 1)
                    columns(j, ps[2 + j % 2], head_read, hlink)
                hlink(ve.tensor_tensor(modc[:, 0:16], modc[:, 0:16], pc[:, 60:76], ALU.add))
                hlink(ve.scalar_tensor_tensor(A1[:, :], modc[:, 8:16], 1.0, pc[:, 0:8], ALU.add, ALU.mult))
                ve.sem_inc(mod_ready, 1)

            for i in range(NT):
                head_norm(0, i)
            head_mod(0)
            with dve.Fori(0, DEPTH) as l:
                n = [0]
                asks = [0]

                def link(ins):
                    n[0] += 1
                    ins.then_inc(dve_step, 1)
                    dve.wait_ge(dve_step, n[0])

                def ask_power():
                    asks[0] += 1
                    ve.sem_inc(pow_ask, 1)
                    dve.wait_ge(pow_done, asks[0])

                def mod_chunk(j):
                    if j >= G2_ADA:
                        dve.wait_ge(bc_ready, j - G2_ADA + 1)
                        bank, read = bc_bank(j), bc_read
                    else:
                        bank, read = ready(dve, "ada", j)
                    if j in (4, 5):
                        h = j - 4
                        link(ve.tensor_tensor(g1bc[:, 512 * h:512 * h + 512], bank[:, :], g1bc[:, 512 * h:512 * h + 512], ALU.add))
                        ve.sem_inc(read, 1)
                    elif j >= G2_ADA:
                        r = 64 * (j - G2_ADA)
                        dve.wait_ge(y_out, 32)
                        link(ve.tensor_tensor(g2bc[r:r + 64, :], bank[r:r + 64, :], g2bc[r:r + 64, :], ALU.add))
                        ve.sem_inc(read, 1)
                    else:
                        columns(j, bank, read, link)
                    if j == 9:
                        link(ve.tensor_tensor(modc[:, 24:40], modc[:, 24:40], pc[:, 84:100], ALU.add))
                        link(ve.scalar_tensor_tensor(A2[:, :], modc[:, 32:40], 1.0, pc[:, 8:16], ALU.add, ALU.mult))

                ve.memset(conv_u[:, :, 0:3], 0.0)
                ve.tensor_scalar(wmc[:, :], pc[:, 56:60], 0.5, None, ALU.mult)
                link(ve.tensor_scalar(wqk[:, 0, :], wqk[:, 0, :], HD ** -0.5, None, ALU.mult))
                for k in range(0, KD, 2):
                    bank, free = ready(dve, "h1T", k)
                    ve.tensor_scalar(hT[:, k, :], bank[:, :], A1[:, k:k + 1], modc[:, k:k + 1], ALU.mult, ALU.add).then_inc(free, 1)

                nh = HQ + HKV
                for i in range(NT):
                    g = GI[("kv", i)]
                    dve.wait_ge(pj_free[g % 2], g // 2 + 1)
                    dve.wait_ge(pj_free[1 - g % 2], (g - 1) // 2 + 1)
                    qk = qk_rows[:, i, 0:nh * HD].rearrange("p (h n) -> p h n", n=HD)
                    link(ve.tensor_reduce(ssq[:, 0:nh], small[:, 0:nh * HD].rearrange("p (h n) -> p h n", n=HD), AX.X, ALU.add))
                    ve.sem_inc(qk_sq, 1)
                    link(ve.tensor_scalar(ssq[:, 0:nh], ssq[:, 0:nh], 1.0 / HD, EPS, ALU.mult, ALU.add))
                    ask_power()
                    link(ve.tensor_tensor(qk, qk, rsq[:, 0:nh].unsqueeze(2).to_broadcast([P, nh, HD]), ALU.mult))
                    ve.tensor_tensor(qk[:, 0:HQ], qk[:, 0:HQ], wqk[:, 0:1, :].to_broadcast([P, HQ, HD]), ALU.mult)
                    link(ve.tensor_tensor(qk[:, HQ:nh], qk[:, HQ:nh], wqk[:, 1:2, :].to_broadcast([P, HKV, HD]), ALU.mult))
                    t1, t2 = qk[:, :, 0:HALF], qk[:, :, HALF:ROPE]
                    co = cosr[:, i, :].unsqueeze(1).to_broadcast([P, nh, HALF])
                    si = sinr[:, i, :].unsqueeze(1).to_broadcast([P, nh, HALF])
                    r4 = rt[:, 0:4 * nh * HALF].rearrange("p (a h f) -> p a h f", a=4, h=nh)
                    ve.tensor_tensor(r4[:, 0], t1, co, ALU.mult)
                    ve.tensor_tensor(r4[:, 1], t2, si, ALU.mult)
                    ve.tensor_tensor(r4[:, 2], t2, co, ALU.mult)
                    link(ve.tensor_tensor(r4[:, 3], t1, si, ALU.mult))
                    ve.tensor_tensor(t1, r4[:, 0], r4[:, 1], ALU.subtract)
                    link(ve.tensor_tensor(t2, r4[:, 2], r4[:, 3], ALU.add))
                    link(ve.tensor_copy(qk_rows[:, i, 640:768].rearrange("p (a n) -> p a n", a=2), qk_rows[:, i, 576:640].unsqueeze(1).to_broadcast([P, 2, HD])))
                    ve.tensor_copy(qk_rows[:, i, 576:640], qk_rows[:, i, 512:576]).then_inc(qk_ready, 1)

                bank, free = ready(dve, "gsum")
                dve.wait_ge(gates_f, 2)
                link(ve.tensor_scalar(rows4[:, 1, :], bank[32:36, :], gbias[32:36, :], None, ALU.add))
                ve.sem_inc(free, 1)
                link(ve.scalar_tensor_tensor(rows4[:, 2, :], rows4[:, 1, :], -1.0, rows4[:, 1, :], ALU.mult, ALU.max))
                ve.sem_inc(gates_f, 1)

                def conv(m):
                    dve.wait_ge(conv_in, m + 1)
                    u = conv_u[:, m % 2, :]
                    z = mqkT[:, m, :]
                    link(ve.tensor_scalar(z, u[:, 0:S], pc[:, 16 + m:17 + m], pc[:, 48 + m:49 + m], ALU.mult, ALU.add))
                    for t in range(1, 4):
                        link(ve.scalar_tensor_tensor(z, u[:, t:t + S], pc[:, 16 + 8 * t + m:17 + 8 * t + m], z, ALU.mult, ALU.add))
                    ve.sem_inc(conv_z, 1)

                def conv_silu(m):
                    dve.wait_ge(conv_t, 2 * m + 1)
                    ve.scalar_tensor_tensor(mqkT[:, m, :], small[:, 0:S], 1.0, mqkT[:, m, :], ALU.add, ALU.mult).then_inc(conv_t, 1)

                def att_max(u):
                    nb_, g = u // HKV, u % HKV
                    lo = 0 if nb_ else P
                    dve.wait_ge(s_ready, u + 1)
                    if u >= 2:
                        dve.wait_ge(pt_ready, u - 1)
                    a = att[:, u % 2, :]
                    for h in range(4):
                        ins = ve.tensor_tensor_reduce(prob[:, u % 2, h, lo:256], att_s[h % 2][:, 256 * (h // 2) + lo:256 * (h // 2) + 256],
                                                      mask[:, lo:256], 1.0, sinkb[:, 4 * g + h:4 * g + h + 1], ALU.add, ALU.max, a[:, h:h + 1])
                    link(ins)
                    ve.sem_inc(s_read, 1)
                    ve.tensor_scalar(a[:, 4:8], a[:, 0:4], -1.0, None, ALU.mult)
                    link(ve.tensor_tensor(a[:, 16:20], sinkb[:, 4 * g:4 * g + 4], a[:, 0:4], ALU.subtract))
                    ve.sem_inc(m_ready, 1)

                def att_norm(u):
                    nb_ = u // HKV
                    lo = 0 if nb_ else P
                    dve.wait_ge(e_ready, u + 1)
                    a = att[:, u % 2, :]
                    link(ve.tensor_tensor(a[:, 8:12], a[:, 8:12], a[:, 12:16], ALU.add))
                    link(ve.reciprocal(a[:, 8:12], a[:, 8:12]))
                    for h in range(4):
                        ins = ve.tensor_scalar(prob[:, u % 2, h, lo:256], prob[:, u % 2, h, lo:256], a[:, 8 + h:9 + h], None, ALU.mult)
                    ins.then_inc(p_norm, 1)

                def att_pt(u):
                    nb_ = u // HKV
                    if nb_:
                        dve.wait_ge(pt_ready, u + 1)
                        if u >= 2:
                            dve.wait_ge(o_ready, u // 2)
                        ve.tensor_copy(pT[:, u % 2, 0, :], att_t[0][:, :]).then_inc(pt_evac, 1)
                    else:
                        ve.sem_inc(pt_evac, 1)

                def gate_rows():
                    lf, b_, mu, nmu = rows4[:, 1, :], rows4[:, 3, :], rows4[:, 4, :], rows4[:, 5, :]
                    dve.wait_ge(gates_f, 5)
                    dve.wait_ge(stack_zero, 1)
                    link(ve.scalar_tensor_tensor(lf, rows4[:, 1, :], 0.0, rows4[:, 2, :], ALU.min, ALU.subtract))
                    ch = [slice(P * i, P * i + P) for i in range(NT)]
                    for t in ch:
                        ins = ve.tensor_tensor_scan(b_[:, t], ones[0:HM, :], lf[:, t], 0.0, ALU.mult, ALU.add)
                    link(ins)
                    a_ = rstack[0:4, :]
                    link(ve.tensor_tensor(a_, rows4[:, 0, :], b_, ALU.subtract))
                    for t in ch:
                        ins = ve.tensor_tensor_scan(mu[:, t], a_[:, t], a_[:, t], NEG, ALU.max, ALU.max)
                    link(ins)
                    last = lambda r: r.rearrange("p (i t) -> p i t", t=P)[:, :, P - 1]
                    bl = g16[:, 8:12]
                    ve.tensor_copy(bl, last(b_))
                    link(ve.tensor_copy(g16[:, 12:16], last(mu)))
                    link(ve.tensor_tensor_scan(g16[:, 1:5], g16[:, 12:16], bl, 0.0, ALU.max, ALU.add))
                    mprev, mnew = g16[:, 0:4], g16[:, 1:5]
                    mp = mprev.unsqueeze(2).to_broadcast([HM, 4, P])
                    v3 = lambda r: r.rearrange("p (i t) -> p i t", t=P)
                    link(ve.tensor_tensor(v3(mu), v3(mu), mp, ALU.max))
                    ve.tensor_scalar(nmu, mu, -1.0, None, ALU.mult)
                    link(ve.tensor_tensor(v3(rstack[32:36, :]), v3(mu), mp, ALU.subtract))
                    link(ve.tensor_scalar(rstack[32:36, :], rstack[32:36, :], -1.0, None, ALU.mult))
                    link(ve.tensor_tensor(g16[:, 16:20], bl, mnew, ALU.subtract))
                    link(ve.tensor_tensor(v3(rstack[64:68, :]), v3(a_), g16[:, 16:20].unsqueeze(2).to_broadcast([HM, 4, P]), ALU.add))
                    link(ve.tensor_tensor(rstack[96:100, :], b_, mu, ALU.add))
                    link(ve.tensor_scalar(rstack[96:100, :], rstack[96:100, :], -1.0, None, ALU.mult))
                    link(ve.tensor_tensor(g16[:, 20:24], g16[:, 16:20], mprev, ALU.add))
                    ve.sem_inc(rows_ready, 1)

                for s in range(16):
                    if s < 8:
                        conv(s)
                    if 1 <= s <= 8:
                        conv_silu(s - 1)
                    if 4 <= s < 12:
                        att_max(s - 4)
                        att_norm(s - 4)
                    if 5 <= s < 13:
                        att_pt(s - 5)
                    if s == 12:
                        gate_rows()
                    if s == 7:
                        dve.wait_ge(rows_zeroed, 16)
                        ve.memset(vaug[:, :, :, DM:DM + 1], 1.0)
                for h in range(HM):
                    bank, free = ready(dve, "mubc", h)
                    link(ve.tensor_tensor(argm[:, h, :].rearrange("p (i t) -> p i t", t=P), bank[:, :].rearrange("p (i t) -> p i t", t=P),
                                          maskT[:, :].unsqueeze(1).to_broadcast([P, NT, P]), ALU.add))
                    ve.sem_inc(free, 1)
                bank, free = ready(dve, "dec")
                link(ve.tensor_copy(decb[:, :, :].rearrange("p h c -> p (h c)"), bank[:, 0:16]))
                ve.sem_inc(free, 1)

                def m_w(u):
                    dve.wait_ge(ma_ready, u + 1)
                    dve.wait_ge(ma_act, u + 1)
                    if u >= 2:
                        dve.wait_ge(mb_ready, u - 1)
                    ve.scalar_tensor_tensor(wS[:, u % 2, :], ps[2 + u % 2][:, P:2 * P], KSCALE, ex[:, u % 2, :], ALU.mult, ALU.mult).then_inc(w_ready, 1)

                def m_state(u):
                    c_, h = u // HM, u % HM
                    dve.wait_ge(mb_ready, u + 1)
                    if c_ == 0:
                        ins = ve.tensor_copy(num[:, h, :], ps[4 + u % 2][:, 0:DM + 1])
                    else:
                        dve.wait_ge(ic_ready, u - HM + 1)
                        ins = ve.tensor_tensor(num[:, h, :], ps[4 + u % 2][:, 0:DM + 1], icb[:, u % 2, :], ALU.add)
                    link(ins)
                    kv = ps[6 + u % 2][:, 0:DM + 1]
                    if c_ == 0:
                        link(ve.tensor_scalar(cst[:, h, :], kv, KSCALE, None, ALU.mult))
                    elif c_ < NT - 1:
                        link(ve.tensor_scalar(cst[:, h, :], cst[:, h, :], decb[:, h, c_:c_ + 1], None, ALU.mult))
                        link(ve.scalar_tensor_tensor(cst[:, h, :], kv, KSCALE, cst[:, h, :], ALU.mult, ALU.add))
                    ve.sem_inc(c_upd, 1)

                def m_finish(c_):
                    den = num[:, :, DM]
                    link(ve.scalar_tensor_tensor(fin[:, 0:4], den, -1.0, den, ALU.mult, ALU.max))
                    link(ve.tensor_tensor(fin[:, 0:4], fin[:, 0:4], colR[:, c_, 3, :], ALU.max))
                    link(ve.reciprocal(fin[:, 0:4], fin[:, 0:4]))
                    hv = num[:, :, 0:DM]
                    link(ve.tensor_tensor(hv, hv, fin[:, 0:4].unsqueeze(2).to_broadcast([P, HM, DM]), ALU.mult))
                    for h in range(HM):
                        ins = ve.tensor_tensor_reduce(sqs, num[:, h, 0:DM], num[:, h, 0:DM], 1.0, 0.0, ALU.mult, ALU.add, fin[:, 4 + h:5 + h])
                        link(ins)
                    link(ve.tensor_scalar(fin[:, 4:8], fin[:, 4:8], 1.0 / DM, EPS, ALU.mult, ALU.add))
                    ask_power()
                    mo = mo_t[:, c_, :].rearrange("p (h n) -> p h n", h=HM)
                    link(ve.tensor_scalar(mo, mo, 1.0, None, ALU.add))
                    link(ve.tensor_tensor(mo, mo, hv, ALU.mult))
                    ve.tensor_tensor(mo, mo, fin[:, 8:12].unsqueeze(2).to_broadcast([P, HM, DM]), ALU.mult).then_inc(hm_ready, 1)

                ve.memset(fin[:, :], 0.0)
                def sum_mid(j):
                    arrived(dve, "ada", j)
                    w = slot("ada", j, 8, 512)
                    link(ve.tensor_scalar(mid_sum, w[:, 0, :], cz[:, 0, 0:1], None, ALU.mult))
                    for k in range(1, KD):
                        link(ve.scalar_tensor_tensor(mid_sum, w[:, k, :], cz[:, k, 0:1], mid_sum, ALU.mult, ALU.add))
                    ve.sem_inc(mid_ready, 1)

                for j in range(8):
                    for u in (2 * j, 2 * j + 1):
                        m_w(u)
                        if u >= 1:
                            m_state(u - 1)
                            if u % HM == 0:
                                m_finish(u // HM - 1)
                    bank, free = ready(dve, "ya", j)
                    g = GI[("ga", j)]
                    dve.wait_ge(pj_free[g % 2], g // 2 + 1)
                    ve.scalar_tensor_tensor(merged[:, j, :], merged[:, j, :], 1.0, bank[:, :], ALU.add, ALU.mult).then_inc(free, 1)
                m_state(15)
                m_finish(NT - 1)
                for i in range(NT):
                    bank, free = ready(dve, "hmT", i)
                    ve.tensor_tensor(hmT[:, :, P * i:P * i + P], bank[:, :].rearrange("p (h t) -> p h t", h=HM),
                                     wmc[:, :].unsqueeze(2).to_broadcast([P, HM, P]), ALU.mult).then_inc(free, 1)
                for j in range(8):
                    bank, free = ready(dve, "yb", j)
                    g = GI[("gb", j)]
                    dve.wait_ge(pj_free[g % 2], g // 2 + 1)
                    link(ve.scalar_tensor_tensor(tb[:, j % 2, :], tb[:, j % 2, :], 1.0, bank[:, :], ALU.add, ALU.mult))
                    ve.sem_inc(free, 1)
                    ve.sem_inc(tb_sum, 1)
                    if j - 1 in MID_ADA:
                        mod_chunk(MID_ADA[j - 1])
                    if j in MID_ADA:
                        sum_mid(MID_ADA[j])
                for i in range(NT):
                    for h in range(2):
                        bank, free = ready(dve, "wo", 2 * i + h)
                        link(ve.scalar_tensor_tensor(regP[:, 0:512], bank[:, :], 0.5, g1bc[:, 512 * h:512 * h + 512], ALU.mult, ALU.mult))
                        ve.sem_inc(free, 1)
                        link(ve.tensor_tensor(xs[:, i, 512 * h:512 * h + 512], xs[:, i, 512 * h:512 * h + 512], regP[:, 0:512], ALU.add))
                    ve.sem_inc(x_upd, 1)
                    dve.wait_ge(ffn_sq, i + 1)
                    link(ve.tensor_scalar(ss[:, 4 + i:5 + i], ss[:, 4 + i:5 + i], 1.0 / D, EPS, ALU.mult, ALU.add))
                    ask_power()
                    ve.tensor_scalar(xn[:, i, :], xs[:, i, :], rs[:, 4 + i:5 + i], None, ALU.mult).then_inc(xn_ready, 1)
                for k in range(0, KD, 2):
                    bank, free = ready(dve, "h2T", k)
                    ve.tensor_scalar(hT[:, k, :], bank[:, :], A2[:, k:k + 1], modc[:, 24 + k:25 + k], ALU.mult, ALU.add).then_inc(free, 1)

                g = GI[("lg", 0)]
                dve.wait_ge(pj_free[g % 2], g // 2 + 1)
                r = lambda a, w: rt[:, a:a + w]
                s_, sel = r(0, 64), r(64, 64)
                link(ve.tensor_scalar(s_, s_, 1.0, None, ALU.add))
                link(ve.reciprocal(s_, s_))
                link(ve.tensor_tensor(sel.rearrange("p (i e) -> p i e", e=E), s_.rearrange("p (i e) -> p i e", e=E),
                                      rbias[:, :].unsqueeze(1).to_broadcast([P, NT, E]), ALU.add))
                v4 = sel.rearrange("p (g j) -> p g j", j=EG)
                hi1, hi2, lo1, lo2 = (r(128 + 16 * q, 16) for q in range(4))
                ve.tensor_tensor(hi1, v4[:, :, 0], v4[:, :, 1], ALU.max)
                ve.tensor_tensor(lo1, v4[:, :, 0], v4[:, :, 1], ALU.min)
                ve.tensor_tensor(hi2, v4[:, :, 2], v4[:, :, 3], ALU.max)
                link(ve.tensor_tensor(lo2, v4[:, :, 2], v4[:, :, 3], ALU.min))
                m1, mn, ml = r(192, 16), r(208, 16), r(224, 16)
                ve.tensor_tensor(m1, hi1, hi2, ALU.max)
                ve.tensor_tensor(mn, hi1, hi2, ALU.min)
                link(ve.tensor_tensor(ml, lo1, lo2, ALU.max))
                link(ve.tensor_tensor(mn, mn, ml, ALU.max))
                gs = r(240, 16)
                link(ve.tensor_tensor(gs, m1, mn, ALU.add))

                def first_max(one, val, tmp, red):
                    v = val.rearrange("p (i g) -> p i g", g=4)
                    o = one.rearrange("p (i g) -> p i g", g=4)
                    t = tmp.rearrange("p (i g) -> p i g", g=4)
                    io = iog[:, :].unsqueeze(1).to_broadcast([P, NT, 4])
                    link(ve.tensor_reduce(red, v, AX.X, ALU.max))
                    link(ve.tensor_tensor(t, v, red.unsqueeze(2).to_broadcast([P, NT, 4]), ALU.is_equal))
                    link(ve.tensor_tensor(t, t, io, ALU.mult))
                    link(ve.tensor_reduce(red, t, AX.X, ALU.min))
                    link(ve.tensor_tensor(o, io, red.unsqueeze(2).to_broadcast([P, NT, 4]), ALU.is_equal))

                og, tmp, red, ing, o1, o2 = r(256, 16), r(272, 16), r(288, 4), r(292, 16), r(308, 16), r(324, 16)
                first_max(og, gs, tmp, red)
                big = r(340, 64)
                link(ve.tensor_tensor(big.rearrange("p (g j) -> p g j", j=EG), v4, og.unsqueeze(2).to_broadcast([P, NT * NG, EG]), ALU.mult))
                link(ve.tensor_reduce(ing.rearrange("p (i j) -> p i j", j=EG), big.rearrange("p (i g j) -> p i j g", g=NG, j=EG), AX.X, ALU.add))
                first_max(o1, ing, tmp, red)
                link(ve.scalar_tensor_tensor(ing, o1, NEG, ing, ALU.mult, ALU.add))
                first_max(o2, ing, tmp, red)
                E1, E2 = r(404, 64), r(468, 64)
                for Ek, ok in ((E1, o1), (E2, o2)):
                    for i in range(NT):
                        ins = ve.tensor_tensor(Ek[:, E * i:E * i + E].rearrange("p (g j) -> p g j", j=EG),
                                               og[:, 4 * i:4 * i + 4].unsqueeze(2).to_broadcast([P, NG, EG]),
                                               ok[:, 4 * i:4 * i + 4].unsqueeze(1).to_broadcast([P, NG, EG]), ALU.mult)
                link(ins)
                link(ve.tensor_tensor(Mb[:, :, :].rearrange("p i e -> p (i e)"), E1, E2, ALU.add))
                ve.sem_inc(routed, 1)
                for k, Ek in enumerate((E1, E2)):
                    link(ve.tensor_tensor(big, s_, Ek, ALU.mult))
                    link(ve.tensor_reduce(wsel[:, k, :], big.rearrange("p (i e) -> p i e", e=E), AX.X, ALU.add))
                link(ve.tensor_tensor(red, wsel[:, 0, :], wsel[:, 1, :], ALU.add))
                link(ve.reciprocal(red, red))
                link(ve.tensor_tensor(wsel[:, :, :], wsel[:, :, :], red.unsqueeze(1).to_broadcast([P, 2, NT]), ALU.mult))
                bank, free = ready(dve, "rank")
                cmp, nbk, cum, base = r(532, 112), r(644, 16), r(660, 16), r(676, 16)
                cnt = r(692, 80)
                link(ve.tensor_copy(cnt, bank[:, 0:80]))
                link(ve.tensor_tensor(cmp.rearrange("p (e k) -> p e k", k=7), cnt[:, 64:80].unsqueeze(2).to_broadcast([P, E, 7]),
                                      thr[:, :].unsqueeze(1).to_broadcast([P, E, 7]), ALU.is_gt))
                link(ve.tensor_reduce(nbk, cmp.rearrange("p (e k) -> p e k", k=7), AX.X, ALU.add))
                link(ve.tensor_scalar(nbk, nbk, 1.0, None, ALU.add))
                link(ve.tensor_tensor_scan(cum, ones[:, 0:E], nbk, 0.0, ALU.mult, ALU.add))
                link(ve.tensor_tensor(base, cum, nbk, ALU.subtract))
                link(ve.tensor_scalar(base, base, float(MB), None, ALU.mult))
                link(ve.tensor_tensor(cnt[:, 0:64].rearrange("p (i e) -> p i e", e=E), cnt[:, 0:64].rearrange("p (i e) -> p i e", e=E),
                                      base.unsqueeze(1).to_broadcast([P, NT, E]), ALU.add))
                for k, Ek in enumerate((E1, E2)):
                    link(ve.tensor_tensor(big, cnt[:, 0:64], Ek, ALU.mult))
                    link(ve.tensor_reduce(red, big.rearrange("p (i e) -> p i e", e=E), AX.X, ALU.add))
                    link(ve.tensor_copy(slot_u[:, k, :], red))
                    ve.sem_inc(routed, 1)
                tb32 = rt[0:1, 0:512]
                link(ve.tensor_tensor(tb32.rearrange("p (b e) -> p b e", e=E), cum[0:1, :].unsqueeze(1).to_broadcast([1, 32, E]),
                                      ioe[:, :].unsqueeze(2).to_broadcast([1, 32, E]), ALU.is_le))
                link(ve.tensor_reduce(rt[0:1, 512:544], tb32.rearrange("p (b e) -> p b e", e=E), AX.X, ALU.add))
                ve.tensor_copy(tabs[0:1, 0:32], rt[0:1, 512:544])
                ve.tensor_copy(tabs[0:1, 32:48], cum[0:1, :])
                link(ve.tensor_scalar(tabs[0:1, 48:49], cum[0:1, E - 1:E], 1.0, None, ALU.subtract))
                ve.sem_inc(tables, 1)

                nb = ve.value_load(tabs[0:1, 47:48], min_val=E, max_val=MAXB)
                nb1 = ve.value_load(tabs[0:1, 48:49], min_val=E - 1, max_val=MAXB - 1)

                def xt_dve():
                    for k in range(1, KD, 2):
                        last = ve.tensor_scalar(xT[:, k, :], ps[6][:, MB * k:MB * k + MB], A2[:, k:k + 1], modc[:, 24 + k:25 + k], ALU.mult, ALU.add)
                    last.then_inc(xt_evac_d, 1)

                def y_row():
                    ve.tensor_tensor(yb, ps[5][:, :], g2bc[:, :], ALU.mult).then_inc(y_taken, 1)

                mod_chunk(G2_ADA)
                mod_chunk(G2_ADA + 1)
                ve.sem_inc(y_taken, 1)
                dve.wait_ge(xt_ready, 1)
                xt_dve()
                dve.wait_ge(sil_ready, 1)
                ve.tensor_tensor(hx, ps[3][64:P, :], hsil[64:P, :], ALU.mult).then_inc(hx_ready, 1)
                dve.wait_ge(xt_ready, 2)
                xt_dve()
                with dve.Fori(0, nb1) as b:
                    dve.wait_ge(sil_ready, b + 2)
                    dve.wait_ge(ht_ready, b + 1)
                    ve.tensor_tensor(hx, ps[3][64:P, :], hsil[64:P, :], ALU.mult).then_inc(hx_ready, 1)
                    dve.wait_ge(xt_ready, b + 3)
                    xt_dve()
                    dve.wait_ge(y_ready, b + 1)
                    dve.wait_ge(y_out, b * 32 + 32)
                    y_row()
                dve.wait_ge(y_ready, nb)
                dve.wait_ge(y_out, nb * 32)
                y_row()
                def combine(i):
                    dve.wait_ge(yg_in[i], l * 32 + 32)
                    for k in range(2):
                        hlink(ve.scalar_tensor_tensor(xs[:, i, :], yg[k][:, i, :], wsel[:, k, i:i + 1], xs[:, i, :], ALU.mult, ALU.add))
                    ve.sem_inc(combined, 1)

                ve.sem_clear(head_step)
                with dve.If(l < DEPTH - 1):
                    hn[0] = 0
                    head_mod(l + 1)
                    for i in range(NT):
                        combine(i)
                        if i:
                            head_norm(l + 1, i - 1)
                    head_norm(l + 1, NT - 1)
                with dve.If(l == DEPTH - 1):
                    hn[0] = 0
                    for i in range(NT):
                        combine(i)
                layer_end(dve, l, share(4))


def program(nc, args):
    trunk(nc, *args)


_INS = ["x", "c", "positions", "ada_w", "ada_b", "norm_mix_w", "norm_ffn_w", "w_in", "b_igate", "b_fgate",
        "q_norm_w", "k_norm_w", "sinks", "conv_w", "conv_b", "mlstm_norm_w", "w_attn_up", "w_mlstm_up",
        "w_out", "router_w", "router_bias", "w_gate", "w_up", "w_down"]


def kernel(**inputs):
    import concourse.bacc as _bacc
    from concourse.bass_utils import run_bass_kernel_spmd as _run

    nc = _bacc.Bacc("TRN2", target_bir_lowering=False, num_devices=1)
    arrays, args = {}, []
    for name in _INS:
        a = np.ascontiguousarray(inputs[name])
        arrays[f"in_{name}_dram"] = a
        args.append(nc.dram_tensor(f"in_{name}_dram", a.shape, mybir.dt.from_np(a.dtype), kind="ExternalInput").ap())
    args.append(nc.dram_tensor("out_0_dram", inputs["x"].shape, F32, kind="ExternalOutput").ap())
    program(nc, args)
    r = _run(nc, [arrays], core_ids=[0])
    return r.results[0]["out_0_dram"]
```
